# Optimizing a Trainium2 kernel written in Bass

```python
import math
import jax, jax.numpy as jnp
from jax import lax
import numpy as np

D_MODEL = 1024
BATCH = 1
SEQ = 512
DEPTH = 1

N_MEM = 256
GDN_HEADS = 8
GDN_DK = 128
GDN_DV = 128
GDN_KW = GDN_HEADS * GDN_DK
GDN_VW = GDN_HEADS * GDN_DV
SHORT_CONV = 4
CHUNK = 64
CONV_CH = D_MODEL
CONV_WIDTH = 31
XATTN_HEADS = 4
XATTN_HD = D_MODEL // XATTN_HEADS
D_FF = 2816
QKV_W = 2 * GDN_KW + GDN_VW
IN_SIZES = (QKV_W, GDN_VW, GDN_HEADS, GDN_HEADS, 2 * CONV_CH, 2 * D_MODEL)
IN_WIDTH = QKV_W + GDN_VW + 2 * GDN_HEADS + 2 * CONV_CH + 2 * D_MODEL
DN_ALPHA = (2 * DEPTH) ** 0.25
DN_BETA = (8 * DEPTH) ** -0.25
LN_EPS = 1e-5
RMS_EPS = 1e-6


def layer_norm(x, g, b):
    xf = x.astype(jnp.float32)
    mu = jnp.mean(xf, axis=-1, keepdims=True)
    var = jnp.mean(jnp.square(xf - mu), axis=-1, keepdims=True)
    y = (xf - mu) * lax.rsqrt(var + LN_EPS)
    return (y * g.astype(jnp.float32) + b.astype(jnp.float32)).astype(x.dtype)

def rms_norm(x, g):
    xf = x.astype(jnp.float32)
    y = xf * lax.rsqrt(jnp.mean(jnp.square(xf), axis=-1, keepdims=True) + RMS_EPS)
    return (y * g.astype(jnp.float32)).astype(x.dtype)

def l2_normalize(x):
    return x * lax.rsqrt(jnp.sum(jnp.square(x), axis=-1, keepdims=True) + RMS_EPS)

def causal_depthwise_conv(x, w):
    k = w.shape[0]
    return lax.conv_general_dilated(
        x, w[:, None, :].astype(x.dtype), window_strides=(1,), padding=[(k - 1, 0)],
        dimension_numbers=("NWC", "WIO", "NWC"), feature_group_count=x.shape[-1])

def swiglu_ffn(x, w_gate, w_up, w_down):
    return (jax.nn.silu(x @ w_gate) * (x @ w_up)) @ w_down

def chunk_gated_delta_rule(q, k, v, g, beta):
    b, l, h, dk = q.shape
    dv = v.shape[-1]
    n = l // CHUNK
    q = l2_normalize(q) * (dk ** -0.5)
    k = l2_normalize(k)

    def chunks(t):
        return t.reshape(b, n, CHUNK, h, -1).transpose(0, 3, 1, 2, 4)

    qc, kc, vc = chunks(q), chunks(k), chunks(v)
    gc = jnp.cumsum(g.reshape(b, n, CHUNK, h).transpose(0, 3, 1, 2), axis=-1)
    bc = beta.reshape(b, n, CHUNK, h).transpose(0, 3, 1, 2)
    kb = kc * bc[..., None]
    vb = vc * bc[..., None]

    tri = jnp.tril(jnp.ones((CHUNK, CHUNK), dtype=bool))
    strict = jnp.tril(jnp.ones((CHUNK, CHUNK), dtype=bool), -1)
    diff = gc[..., :, None] - gc[..., None, :]
    decay = jnp.where(tri, jnp.exp(jnp.where(tri, diff, 0.0)), 0.0)

    m = jnp.where(strict, jnp.einsum("bhncd,bhnmd->bhncm", kb, kc) * decay, 0.0)
    t_sys = jnp.eye(CHUNK, dtype=q.dtype) + m
    u = lax.linalg.triangular_solve(t_sys, vb, left_side=True, lower=True, unit_diagonal=True)
    w = lax.linalg.triangular_solve(t_sys, kb * jnp.exp(gc)[..., None], left_side=True,
                                    lower=True, unit_diagonal=True)
    a_qk = jnp.einsum("bhncd,bhnmd->bhncm", qc, kc) * decay

    def step(state, xs):
        q_i, k_i, u_i, w_i, a_i, g_i = xs
        v_new = u_i - jnp.einsum("bhcd,bhde->bhce", w_i, state)
        o_i = (jnp.einsum("bhcd,bhde->bhce", q_i * jnp.exp(g_i)[..., None], state)
               + jnp.einsum("bhcm,bhme->bhce", a_i, v_new))
        g_last = g_i[..., -1]
        k_dec = k_i * jnp.exp(g_last[..., None] - g_i)[..., None]
        state = state * jnp.exp(g_last)[..., None, None] + jnp.einsum("bhcd,bhce->bhde", k_dec, v_new)
        return state, o_i

    xs = tuple(jnp.moveaxis(t, 2, 0) for t in (qc, kc, u, w, a_qk, gc))
    s0 = jnp.zeros((b, h, dk, dv), dtype=q.dtype)
    _, o = lax.scan(step, s0, xs)
    return o.transpose(1, 0, 3, 2, 4).reshape(b, l, h, dv)

def parallel_mixers(h, w_in, gdn_conv_qkv, gdn_a_log, gdn_dt_bias, gdn_norm_g, w_gdn_out,
                    conv_dw_w, conv_dw_b, conv_ln_g, conv_ln_b, w_conv_out, b_conv_out, w_mix_out):
    b, l, _ = h.shape
    proj = h @ w_in
    offs = np.cumsum(IN_SIZES)[:-1].tolist()
    qkv, z, a, bt, glu, gates = jnp.split(proj, offs, axis=-1)

    qkv = jax.nn.silu(causal_depthwise_conv(qkv, gdn_conv_qkv))
    q, k, v = jnp.split(qkv, [GDN_KW, 2 * GDN_KW], axis=-1)
    q = q.reshape(b, l, GDN_HEADS, GDN_DK)
    k = k.reshape(b, l, GDN_HEADS, GDN_DK)
    v = v.reshape(b, l, GDN_HEADS, GDN_DV)
    af = a.astype(jnp.float32)
    g = -jnp.exp(gdn_a_log.astype(jnp.float32)) * jax.nn.softplus(af + gdn_dt_bias.astype(jnp.float32))
    beta = jax.nn.sigmoid(bt.astype(jnp.float32))
    o = chunk_gated_delta_rule(q.astype(jnp.float32), k.astype(jnp.float32),
                               v.astype(jnp.float32), g, beta).astype(h.dtype)
    o = rms_norm(o, gdn_norm_g) * jax.nn.silu(z.reshape(b, l, GDN_HEADS, GDN_DV))
    y_a = o.reshape(b, l, GDN_VW) @ w_gdn_out

    c_lin, c_gate = jnp.split(glu, 2, axis=-1)
    c = c_lin * jax.nn.sigmoid(c_gate)
    c = causal_depthwise_conv(c, conv_dw_w) + conv_dw_b
    c = jax.nn.silu(layer_norm(c, conv_ln_g, conv_ln_b))
    y_c = c @ w_conv_out + b_conv_out

    g_a, g_c = jnp.split(gates, 2, axis=-1)
    y = jax.nn.sigmoid(g_a) * y_a + jax.nn.sigmoid(g_c) * y_c
    return y @ w_mix_out

def memory_cross_attention(x, mem, w_xq, w_xkv, w_xo):
    b, l, _ = x.shape
    q = (x @ w_xq).reshape(b, l, XATTN_HEADS, XATTN_HD)
    k, v = jnp.split(mem @ w_xkv, 2, axis=-1)
    k = k.reshape(b, -1, XATTN_HEADS, XATTN_HD)
    v = v.reshape(b, -1, XATTN_HEADS, XATTN_HD)
    s = jnp.einsum("blhd,bmhd->bhlm", q, k).astype(jnp.float32) * (XATTN_HD ** -0.5)
    p = jax.nn.softmax(s, axis=-1).astype(v.dtype)
    o = jnp.einsum("bhlm,bmhd->blhd", p, v).reshape(b, l, D_MODEL)
    return o @ w_xo

def first_inputs(seed: int = 0) -> dict:
    key = jax.random.key(seed)
    keys = jax.random.split(key, 48)
    counter = [0]

    def nk():
        kk = keys[counter[0]]
        counter[0] += 1
        return kk

    def nrm(shape, scale):
        return jax.random.normal(nk(), shape, jnp.float32) * scale

    def gain(shape):
        return 1.0 + nrm(shape, 0.02)

    L = DEPTH
    dt = jnp.exp(jax.random.uniform(nk(), (L, GDN_HEADS), jnp.float32,
                                    minval=math.log(1e-3), maxval=math.log(0.1)))
    return {
        "x": nrm((BATCH, SEQ, D_MODEL), 1.0),
        "mem": nrm((BATCH, N_MEM, D_MODEL), 1.0),
        "ffn1_wg": nrm((L, D_MODEL, D_FF), D_MODEL ** -0.5),
        "ffn1_wu": nrm((L, D_MODEL, D_FF), D_MODEL ** -0.5),
        "ffn1_wd": nrm((L, D_FF, D_MODEL), DN_BETA * D_FF ** -0.5),
        "ln1_g": gain((L, D_MODEL)),
        "ln1_b": nrm((L, D_MODEL), 0.02),
        "w_in": nrm((L, D_MODEL, IN_WIDTH), D_MODEL ** -0.5),
        "gdn_conv_qkv": nrm((L, SHORT_CONV, QKV_W), SHORT_CONV ** -0.5),
        "gdn_a_log": jnp.log(jax.random.uniform(nk(), (L, GDN_HEADS), jnp.float32, minval=1.0, maxval=16.0)),
        "gdn_dt_bias": dt + jnp.log(-jnp.expm1(-dt)),
        "gdn_norm_g": gain((L, GDN_DV)),
        "w_gdn_out": nrm((L, GDN_VW, D_MODEL), GDN_VW ** -0.5),
        "conv_dw_w": nrm((L, CONV_WIDTH, CONV_CH), CONV_WIDTH ** -0.5),
        "conv_dw_b": nrm((L, CONV_CH), 0.02),
        "conv_ln_g": gain((L, CONV_CH)),
        "conv_ln_b": nrm((L, CONV_CH), 0.02),
        "w_conv_out": nrm((L, CONV_CH, D_MODEL), CONV_CH ** -0.5),
        "b_conv_out": nrm((L, D_MODEL), 0.02),
        "w_mix_out": nrm((L, D_MODEL, D_MODEL), DN_BETA * D_MODEL ** -0.5),
        "ln2_g": gain((L, D_MODEL)),
        "ln2_b": nrm((L, D_MODEL), 0.02),
        "w_xq": nrm((L, D_MODEL, D_MODEL), D_MODEL ** -0.5),
        "w_xkv": nrm((L, D_MODEL, 2 * D_MODEL), D_MODEL ** -0.5),
        "w_xo": nrm((L, D_MODEL, D_MODEL), DN_BETA * D_MODEL ** -0.5),
        "ln3_g": gain((L, D_MODEL)),
        "ln3_b": nrm((L, D_MODEL), 0.02),
        "ffn2_wg": nrm((L, D_MODEL, D_FF), D_MODEL ** -0.5),
        "ffn2_wu": nrm((L, D_MODEL, D_FF), D_MODEL ** -0.5),
        "ffn2_wd": nrm((L, D_FF, D_MODEL), DN_BETA * D_FF ** -0.5),
        "ln4_g": gain((L, D_MODEL)),
        "ln4_b": nrm((L, D_MODEL), 0.02),
    }

def first_block(x, mem, ffn1_wg, ffn1_wu, ffn1_wd, ln1_g, ln1_b,
              w_in, gdn_conv_qkv, gdn_a_log, gdn_dt_bias, gdn_norm_g, w_gdn_out,
              conv_dw_w, conv_dw_b, conv_ln_g, conv_ln_b, w_conv_out, b_conv_out, w_mix_out,
              ln2_g, ln2_b, w_xq, w_xkv, w_xo, ln3_g, ln3_b,
              ffn2_wg, ffn2_wu, ffn2_wd, ln4_g, ln4_b):
    for i in range(DEPTH):
        x = layer_norm(DN_ALPHA * x + 0.5 * swiglu_ffn(x, ffn1_wg[i], ffn1_wu[i], ffn1_wd[i]),
                       ln1_g[i], ln1_b[i])
        y = parallel_mixers(x, w_in[i], gdn_conv_qkv[i], gdn_a_log[i], gdn_dt_bias[i], gdn_norm_g[i],
                            w_gdn_out[i], conv_dw_w[i], conv_dw_b[i], conv_ln_g[i], conv_ln_b[i],
                            w_conv_out[i], b_conv_out[i], w_mix_out[i])
        x = layer_norm(DN_ALPHA * x + y, ln2_g[i], ln2_b[i])
        x = layer_norm(DN_ALPHA * x + memory_cross_attention(x, mem, w_xq[i], w_xkv[i], w_xo[i]),
                       ln3_g[i], ln3_b[i])
        x = layer_norm(DN_ALPHA * x + 0.5 * swiglu_ffn(x, ffn2_wg[i], ffn2_wu[i], ffn2_wd[i]),
                       ln4_g[i], ln4_b[i])
    return x


_first_inputs = first_inputs


def first_inputs(seed=0):
    import zlib

    import numpy as np

    out = dict(_first_inputs(seed))
    spreads = {}
    factors = {'ln1_b': 2.693,
     'gdn_a_log': 3.435,
     'gdn_norm_g': 8.0,
     'conv_dw_b': 8.0,
     'conv_ln_g': 8.0,
     'conv_ln_b': 8.0,
     'b_conv_out': 8.0,
     'ln2_g': 2.931,
     'ln2_b': 2.722,
     'ln3_g': 2.77,
     'ln3_b': 2.765,
     'ln4_g': 2.77,
     'ln4_b': 2.898}
    for name, (base, spread) in spreads.items():
        noise = np.random.default_rng([zlib.crc32(name.encode()), seed]).standard_normal(out[name].shape)
        drawn = base * np.exp(spread * noise) if base else spread * noise
        out[name] = __import__('jax').numpy.asarray(drawn.astype(out[name].dtype))
    for name, factor in factors.items():
        out[name] = (out[name] * factor).astype(out[name].dtype)
    return out


_narrow_inputs = first_inputs


def first_inputs(seed=0):

    out = dict(_narrow_inputs(seed))
    wider = {'gdn_norm_g': 5.04,
     'conv_ln_g': 4.12,
     'conv_ln_b': 4.15,
     'ln2_g': 3.03,
     'ln2_b': 3.03,
     'ln4_g': 3.1,
     'ln4_b': 3.12}
    for name, times in wider.items():
        mean = out[name].mean()
        out[name] = (mean + times * (out[name] - mean)).astype(out[name].dtype)
    return out


HEAD_DIM = 64
RET_HEADS = 8
NSA_HEADS = 8
NSA_KV_HEADS = 2
NSA_GROUP = NSA_HEADS // NSA_KV_HEADS
D_RET = RET_HEADS * HEAD_DIM
D_NSA = NSA_HEADS * HEAD_DIM
D_MIX = D_RET + D_NSA
D_KV = NSA_KV_HEADS * HEAD_DIM
N_BRANCH = 3
RET_CHUNK = 128
ROPE_THETA = 10000.0
CMP_BLOCK = 32
CMP_STRIDE = 16
CMP_HIDDEN = 256
SLC_BLOCK = 64
SLC_TOPK = 16
SLC_QBLOCK = 64
WIN_SIZE = 512
WIN_QBLOCK = 128
EPS = 1e-6
NEG = -1e30
FORCE_BONUS = 1e4

IN_WIDTHS = (D_RET, D_RET, D_RET, D_RET,
             D_NSA, D_NSA,
             D_KV, D_KV, D_KV, D_KV, D_KV, D_KV,
             N_BRANCH * NSA_HEADS)
D_IN = sum(IN_WIDTHS)
SPLIT_POINTS = [int(s) for s in np.cumsum(IN_WIDTHS)[:-1]]


def rms_norm_2(x, w):
    xf = x.astype(jnp.float32)
    y = xf * lax.rsqrt(jnp.mean(xf * xf, axis=-1, keepdims=True) + EPS)
    return (y * w.astype(jnp.float32)).astype(x.dtype)

def rope(x):
    T = x.shape[2]
    half = HEAD_DIM // 2
    inv = ROPE_THETA ** (-jnp.arange(half, dtype=jnp.float32) / half)
    ang = jnp.arange(T, dtype=jnp.float32)[:, None] * inv[None, :]
    cos, sin = jnp.cos(ang), jnp.sin(ang)
    x1, x2 = x[..., :half], x[..., half:]
    return jnp.concatenate([x1 * cos - x2 * sin, x1 * sin + x2 * cos], axis=-1)

def retention(q, k, v):
    B, H, T, d = q.shape
    C = RET_CHUNK
    N = T // C
    f32 = jnp.float32
    log_g = jnp.log1p(-jnp.exp2(-5.0 - jnp.arange(H, dtype=f32)))
    qc = rope(q.astype(f32)).reshape(B, H, N, C, d)
    kc = (rope(k.astype(f32)) * d ** -0.5).reshape(B, H, N, C, d)
    vc = v.astype(f32).reshape(B, H, N, C, d)
    pos = jnp.arange(C, dtype=f32)
    diff = pos[:, None] - pos[None, :]
    decay = jnp.where(diff >= 0, jnp.exp(log_g[:, None, None] * jnp.maximum(diff, 0.0)), 0.0)
    s = jnp.einsum('bhncd,bhnsd->bhncs', qc, kc) * decay[None, :, None]
    o_inner = jnp.einsum('bhncs,bhnse->bhnce', s, vc)
    zeta = jnp.exp(log_g[:, None] * (C - 1.0 - pos))
    kv = jnp.einsum('bhnsd,bhnse->nbhde', kc, vc * zeta[None, :, None, :, None])
    g_chunk = jnp.exp(log_g * C)[None, :, None, None]

    def step(R, kv_i):
        return R * g_chunk + kv_i, R

    _, R_prev = lax.scan(step, jnp.zeros((B, H, d, d), f32), kv)
    xi = jnp.exp(log_g[:, None] * (pos + 1.0))
    o_cross = jnp.einsum('bhncd,nbhde->bhnce', qc, R_prev) * xi[None, :, None, :, None]
    return (o_inner + o_cross).reshape(B, H, T, d)

def compress(kv, pos_emb, w1, w2):
    B, G, T, d = kv.shape
    n_cmp = (T - CMP_BLOCK) // CMP_STRIDE + 1
    idx = np.arange(n_cmp)[:, None] * CMP_STRIDE + np.arange(CMP_BLOCK)[None, :]
    blocks = kv[:, :, idx] + pos_emb
    flat = blocks.reshape(B, G, n_cmp, CMP_BLOCK * d)
    return jax.nn.silu(flat @ w1) @ w2

def compressed_branch(q, kc_raw, vc_raw, k_norm, pos_k, w1_k, w2_k, pos_v, w1_v, w2_v):
    B, G, R, T, d = q.shape
    kc = rms_norm_2(compress(kc_raw, pos_k, w1_k, w2_k), k_norm)
    vc = compress(vc_raw, pos_v, w1_v, w2_v)
    n_cmp = kc.shape[2]
    block_end = np.arange(n_cmp) * CMP_STRIDE + CMP_BLOCK - 1
    valid = jnp.asarray(block_end[None, :] <= np.arange(T)[:, None])
    s = jnp.einsum('bgrtd,bgnd->bgrtn', q, kc).astype(jnp.float32) * d ** -0.5
    p = jax.nn.softmax(jnp.where(valid, s, NEG), axis=-1)
    p = jnp.where(valid, p, 0.0)
    o = jnp.einsum('bgrtn,bgnd->bgrtd', p.astype(vc.dtype), vc)
    return o, p

def overlap_matrix(T):
    n_cmp = (T - CMP_BLOCK) // CMP_STRIDE + 1
    pos = np.arange(n_cmp)[:, None] * CMP_STRIDE + np.arange(CMP_BLOCK)[None, :]
    blk = pos // SLC_BLOCK
    return (blk[:, :, None] == np.arange(T // SLC_BLOCK)[None, None, :]).mean(axis=1).astype(np.float32)

def selected_branch(q, ks, vs, p_cmp):
    B, G, R, T, d = q.shape
    n_slc = T // SLC_BLOCK
    top = min(SLC_TOPK, n_slc)
    M = jnp.asarray(overlap_matrix(T))
    imp = jnp.einsum('bgtn,ns->bgts', p_cmp.sum(axis=2), M)
    t = jnp.arange(T)
    blk = jnp.arange(n_slc)
    valid = blk[None, :] * SLC_BLOCK <= t[:, None]
    force = (blk[None, :] == (t // SLC_BLOCK)[:, None]) | (blk[None, :] == 0)
    score = jnp.where(valid, jnp.where(force, imp + FORCE_BONUS, imp), NEG)
    _, idx = lax.top_k(score, top)
    ks_blk = ks.reshape(B, G, n_slc, SLC_BLOCK, d)
    vs_blk = vs.reshape(B, G, n_slc, SLC_BLOCK, d)
    nb = T // SLC_QBLOCK
    q_b = q.reshape(B, G, R, nb, SLC_QBLOCK, d).transpose(3, 0, 1, 2, 4, 5)
    idx_b = idx.reshape(B, G, nb, SLC_QBLOCK, top).transpose(2, 0, 1, 3, 4)
    t_b = t.reshape(nb, SLC_QBLOCK)
    gather = jax.vmap(jax.vmap(lambda arr, ib: arr[ib]))

    def block(args):
        qb, ib, tb = args
        flat = ib.reshape(B, G, SLC_QBLOCK * top)
        kg = gather(ks_blk, flat).reshape(B, G, SLC_QBLOCK, top, SLC_BLOCK, d)
        vg = gather(vs_blk, flat).reshape(B, G, SLC_QBLOCK, top, SLC_BLOCK, d)
        s = jnp.einsum('bgrqd,bgqkld->bgrqkl', qb, kg).astype(jnp.float32) * d ** -0.5
        key_pos = ib[..., None] * SLC_BLOCK + jnp.arange(SLC_BLOCK)
        mask = key_pos <= tb[None, None, :, None, None]
        s = jnp.where(mask[:, :, None], s, NEG).reshape(B, G, R, SLC_QBLOCK, top * SLC_BLOCK)
        p = jax.nn.softmax(s, axis=-1).reshape(B, G, R, SLC_QBLOCK, top, SLC_BLOCK)
        return jnp.einsum('bgrqkl,bgqkld->bgrqd', p.astype(vg.dtype), vg)

    o = lax.map(block, (q_b, idx_b, t_b))
    return o.transpose(1, 2, 3, 0, 4, 5).reshape(B, G, R, T, d)

def window_branch(q, kw, vw):
    B, G, R, T, d = q.shape
    nb = T // WIN_QBLOCK
    span = WIN_QBLOCK + WIN_SIZE
    idx = np.arange(nb)[:, None] * WIN_QBLOCK + np.arange(span)[None, :]
    pad = ((0, 0), (0, 0), (WIN_SIZE, 0), (0, 0))
    kp = jnp.pad(kw, pad)[:, :, idx]
    vp = jnp.pad(vw, pad)[:, :, idx]
    qb = q.reshape(B, G, R, nb, WIN_QBLOCK, d)
    tq = np.arange(nb)[:, None] * WIN_QBLOCK + np.arange(WIN_QBLOCK)[None, :]
    s_pos = idx - WIN_SIZE
    delta = tq[:, :, None] - s_pos[:, None, :]
    mask = jnp.asarray((delta >= 0) & (delta < WIN_SIZE) & (s_pos[:, None, :] >= 0))
    s = jnp.einsum('bgrnqd,bgnsd->bgrnqs', qb, kp).astype(jnp.float32) * d ** -0.5
    p = jax.nn.softmax(jnp.where(mask, s, NEG), axis=-1)
    o = jnp.einsum('bgrnqs,bgnsd->bgrnqd', p.astype(vp.dtype), vp)
    return o.reshape(B, G, R, T, d)

def hybrid_layer(x, norm_w, w_in, ret_norm_w, q_norm_w, k_norm_cmp, k_norm_slc, k_norm_win,
                 cmp_pos_k, cmp_w1_k, cmp_w2_k, cmp_pos_v, cmp_w1_v, cmp_w2_v, b_gate, w_out):
    B, T, _ = x.shape
    h = rms_norm_2(x, norm_w)
    proj = h @ w_in
    rq, rk, rv, rg, nq, ng, ck, cv, sk, sv, wk, wv, gl = jnp.split(proj, SPLIT_POINTS, axis=-1)

    def heads(t, n):
        return t.reshape(B, T, n, HEAD_DIM).transpose(0, 2, 1, 3)

    o_ret = retention(heads(rq, RET_HEADS), heads(rk, RET_HEADS), heads(rv, RET_HEADS))
    o_ret = rms_norm_2(o_ret.transpose(0, 2, 1, 3), ret_norm_w).astype(x.dtype)
    y_ret = o_ret.reshape(B, T, D_RET) * jax.nn.silu(rg)

    q = rms_norm_2(heads(nq, NSA_HEADS), q_norm_w).reshape(B, NSA_KV_HEADS, NSA_GROUP, T, HEAD_DIM)
    kc_raw, vc_raw = heads(ck, NSA_KV_HEADS), heads(cv, NSA_KV_HEADS)
    ks, vs = rms_norm_2(heads(sk, NSA_KV_HEADS), k_norm_slc), heads(sv, NSA_KV_HEADS)
    kw, vw = rms_norm_2(heads(wk, NSA_KV_HEADS), k_norm_win), heads(wv, NSA_KV_HEADS)
    o_cmp, p_cmp = compressed_branch(q, kc_raw, vc_raw, k_norm_cmp,
                                     cmp_pos_k, cmp_w1_k, cmp_w2_k, cmp_pos_v, cmp_w1_v, cmp_w2_v)
    o_slc = selected_branch(q, ks, vs, p_cmp)
    o_win = window_branch(q, kw, vw)
    gates = jax.nn.sigmoid((gl + b_gate).astype(jnp.float32))
    gates = gates.reshape(B, T, N_BRANCH, NSA_HEADS).transpose(2, 0, 3, 1)[..., None]
    shp = (B, NSA_HEADS, T, HEAD_DIM)
    o_nsa = (gates[0] * o_cmp.reshape(shp) + gates[1] * o_slc.reshape(shp)
             + gates[2] * o_win.reshape(shp)).astype(x.dtype)
    y_nsa = o_nsa.transpose(0, 2, 1, 3).reshape(B, T, D_NSA) * jax.nn.silu(ng)

    y = jnp.concatenate([y_ret, y_nsa], axis=-1) @ w_out
    return x + y

def second_inputs(seed: int = 0) -> dict:
    key = jax.random.key(seed)
    ks = jax.random.split(key, 17)

    def nrm(k, shape, scale):
        return jax.random.normal(k, shape, jnp.float32) * scale

    L = DEPTH
    return {
        "x": nrm(ks[0], (BATCH, SEQ, D_MODEL), 1.0),
        "norm_w": 1.0 + nrm(ks[1], (L, D_MODEL), 0.01),
        "w_in": nrm(ks[2], (L, D_MODEL, D_IN), D_MODEL ** -0.5),
        "ret_norm_w": 1.0 + nrm(ks[3], (L, RET_HEADS, HEAD_DIM), 0.01),
        "q_norm_w": 1.0 + nrm(ks[4], (L, HEAD_DIM), 0.01),
        "k_norm_cmp": 1.0 + nrm(ks[5], (L, HEAD_DIM), 0.01),
        "k_norm_slc": 1.0 + nrm(ks[6], (L, HEAD_DIM), 0.01),
        "k_norm_win": 1.0 + nrm(ks[7], (L, HEAD_DIM), 0.01),
        "cmp_pos_k": nrm(ks[8], (L, CMP_BLOCK, HEAD_DIM), 0.02),
        "cmp_w1_k": nrm(ks[9], (L, CMP_BLOCK * HEAD_DIM, CMP_HIDDEN), (CMP_BLOCK * HEAD_DIM) ** -0.5),
        "cmp_w2_k": nrm(ks[10], (L, CMP_HIDDEN, HEAD_DIM), CMP_HIDDEN ** -0.5),
        "cmp_pos_v": nrm(ks[11], (L, CMP_BLOCK, HEAD_DIM), 0.02),
        "cmp_w1_v": nrm(ks[12], (L, CMP_BLOCK * HEAD_DIM, CMP_HIDDEN), (CMP_BLOCK * HEAD_DIM) ** -0.5),
        "cmp_w2_v": nrm(ks[13], (L, CMP_HIDDEN, HEAD_DIM), CMP_HIDDEN ** -0.5),
        "b_gate": nrm(ks[14], (L, N_BRANCH * NSA_HEADS), 0.01),
        "w_out": nrm(ks[15], (L, D_MIX, D_MODEL), D_MIX ** -0.5),
    }

def second_block(x, norm_w, w_in, ret_norm_w, q_norm_w, k_norm_cmp, k_norm_slc, k_norm_win,
              cmp_pos_k, cmp_w1_k, cmp_w2_k, cmp_pos_v, cmp_w1_v, cmp_w2_v, b_gate, w_out):
    for layer in range(DEPTH):
        x = hybrid_layer(x, norm_w[layer], w_in[layer], ret_norm_w[layer], q_norm_w[layer],
                         k_norm_cmp[layer], k_norm_slc[layer], k_norm_win[layer],
                         cmp_pos_k[layer], cmp_w1_k[layer], cmp_w2_k[layer],
                         cmp_pos_v[layer], cmp_w1_v[layer], cmp_w2_v[layer],
                         b_gate[layer], w_out[layer])
    return x


_first_inputs_2 = second_inputs


def second_inputs(seed=0):
    import zlib

    import numpy as np

    out = dict(_first_inputs_2(seed))
    spreads = {}
    factors = {'norm_w': 6.466,
     'ret_norm_w': 8.0,
     'q_norm_w': 8.0,
     'k_norm_cmp': 8.0,
     'k_norm_slc': 8.0,
     'k_norm_win': 8.0,
     'cmp_pos_k': 8.0,
     'cmp_pos_v': 8.0,
     'b_gate': 8.0}
    for name, (base, spread) in spreads.items():
        noise = np.random.default_rng([zlib.crc32(name.encode()), seed]).standard_normal(out[name].shape)
        drawn = base * np.exp(spread * noise) if base else spread * noise
        out[name] = __import__('jax').numpy.asarray(drawn.astype(out[name].dtype))
    for name, factor in factors.items():
        out[name] = (out[name] * factor).astype(out[name].dtype)
    return out


_narrow_inputs_2 = second_inputs


def second_inputs(seed=0):

    out = dict(_narrow_inputs_2(seed))
    wider = {'ret_norm_w': 8.85, 'k_norm_cmp': 4.57, 'cmp_pos_v': 8.78, 'b_gate': 7.79}
    for name, times in wider.items():
        mean = out[name].mean()
        out[name] = (mean + times * (out[name] - mean)).astype(out[name].dtype)
    return out


GRID_W = 64

NA_HEADS = 8
NA_HEAD_DIM = 64
NA_WIDTH = NA_HEADS * NA_HEAD_DIM
NA_WIN_ROWS_MAX = 8
NA_WIN_COLS = 16

MLA_HEADS = 8
MLA_Q_LORA = 256
MLA_KV_LORA = 128
MLA_NOPE_DIM = 64
MLA_ROPE_DIM = 32
MLA_QK_DIM = MLA_NOPE_DIM + MLA_ROPE_DIM
MLA_V_DIM = 64
MLA_WIDTH = MLA_HEADS * MLA_V_DIM
MLA_Q_BLOCK = 128

IN_SIZES_3 = (NA_WIDTH, NA_WIDTH, NA_WIDTH, MLA_Q_LORA, MLA_KV_LORA, MLA_ROPE_DIM, D_MODEL, D_MODEL)
IN_TOTAL = 3 * NA_WIDTH + MLA_Q_LORA + MLA_KV_LORA + MLA_ROPE_DIM + 2 * D_MODEL

FFN_HIDDEN = -(-8 * D_MODEL // (3 * 256)) * 256

DN_ALPHA_3 = (2.0 * DEPTH) ** 0.25
DN_BETA_3 = (8.0 * DEPTH) ** -0.25


def layer_norm_3(x, g, b):
    xf = x.astype(jnp.float32)
    mu = jnp.mean(xf, axis=-1, keepdims=True)
    var = jnp.mean(jnp.square(xf - mu), axis=-1, keepdims=True)
    y = (xf - mu) * lax.rsqrt(var + LN_EPS) * g.astype(jnp.float32) + b.astype(jnp.float32)
    return y.astype(x.dtype)

def rms_norm_3(x, g):
    xf = x.astype(jnp.float32)
    y = xf * lax.rsqrt(jnp.mean(jnp.square(xf), axis=-1, keepdims=True) + RMS_EPS) * g.astype(jnp.float32)
    return y.astype(x.dtype)

def axial_rope_tables(seq_len):
    t = jnp.arange(seq_len)
    rows = (t // GRID_W).astype(jnp.float32)
    cols = (t % GRID_W).astype(jnp.float32)
    half = MLA_ROPE_DIM // 2
    inv_freq = ROPE_THETA ** (-jnp.arange(0, half, 2, dtype=jnp.float32) / half)
    ang_r = rows[:, None, None] * inv_freq
    ang_c = cols[:, None, None] * inv_freq
    return jnp.cos(ang_r), jnp.sin(ang_r), jnp.cos(ang_c), jnp.sin(ang_c)

def rotate_pairs(x, cos, sin):
    x1, x2 = jnp.split(x, 2, axis=-1)
    return jnp.concatenate([x1 * cos - x2 * sin, x2 * cos + x1 * sin], axis=-1)

def apply_axial_rope(x, tables):
    cos_r, sin_r, cos_c, sin_c = tables
    xf = x.astype(jnp.float32)
    xr, xc = jnp.split(xf, 2, axis=-1)
    out = jnp.concatenate([rotate_pairs(xr, cos_r, sin_r), rotate_pairs(xc, cos_c, sin_c)], axis=-1)
    return out.astype(x.dtype)

def neighbourhood_attention_2d(q, k, v, rpb):
    B, S, H, dh = q.shape
    rows = S // GRID_W
    kr = min(NA_WIN_ROWS_MAX, rows)
    kc = NA_WIN_COLS
    qg = q.reshape(B, rows, GRID_W, H, dh).transpose(1, 0, 2, 3, 4)
    kg = k.reshape(B, rows, GRID_W, H, dh)
    vg = v.reshape(B, rows, GRID_W, H, dh)
    col = jnp.arange(GRID_W)
    col_start = jnp.clip(col - kc // 2, 0, GRID_W - kc)
    col_idx = col_start[:, None] + jnp.arange(kc)[None, :]
    col_bias_idx = col_idx - col[:, None] + (NA_WIN_COLS - 1)
    rpb_cols = rpb.astype(jnp.float32)[:, :, col_bias_idx]
    scale = dh ** -0.5

    def one_row(args):
        r, q_row = args
        r_start = jnp.clip(r - kr // 2, 0, rows - kr)
        k_band = lax.dynamic_slice_in_dim(kg, r_start, kr, axis=1)
        v_band = lax.dynamic_slice_in_dim(vg, r_start, kr, axis=1)
        k_nb = k_band[:, :, col_idx]
        v_nb = v_band[:, :, col_idx]
        row_bias_idx = r_start + jnp.arange(kr) - r + (NA_WIN_ROWS_MAX - 1)
        bias = rpb_cols[:, row_bias_idx].transpose(0, 2, 1, 3)
        s = jnp.einsum('bqhd,brqchd->bhqrc', q_row, k_nb).astype(jnp.float32) * scale + bias[None]
        p = jax.nn.softmax(s.reshape(B, H, GRID_W, kr * kc), axis=-1).reshape(B, H, GRID_W, kr, kc)
        return jnp.einsum('bhqrc,brqchd->bqhd', p.astype(v.dtype), v_nb)

    out = lax.map(one_row, (jnp.arange(rows), qg))
    return out.transpose(1, 0, 2, 3, 4).reshape(B, S, H * dh)

def latent_attention(q_lat, kv_lat, k_rope, q_norm_g, w_uq, kv_norm_g, w_ukv, tables):
    B, S, _ = q_lat.shape
    H = MLA_HEADS
    q = (rms_norm_3(q_lat, q_norm_g) @ w_uq).reshape(B, S, H, MLA_QK_DIM)
    q_nope, q_pe = jnp.split(q, [MLA_NOPE_DIM], axis=-1)
    q = jnp.concatenate([q_nope, apply_axial_rope(q_pe, tables)], axis=-1)
    kv = (rms_norm_3(kv_lat, kv_norm_g) @ w_ukv).reshape(B, S, H, MLA_NOPE_DIM + MLA_V_DIM)
    k_nope, v = jnp.split(kv, [MLA_NOPE_DIM], axis=-1)
    k_pe = apply_axial_rope(k_rope[:, :, None, :], tables)
    k = jnp.concatenate([k_nope, jnp.broadcast_to(k_pe, (B, S, H, MLA_ROPE_DIM))], axis=-1)
    scale = MLA_QK_DIM ** -0.5
    n_blk = S // MLA_Q_BLOCK
    qb = q.reshape(B, n_blk, MLA_Q_BLOCK, H, MLA_QK_DIM).transpose(1, 0, 2, 3, 4)

    def one_block(q_blk):
        s = jnp.einsum('bqhd,bkhd->bhqk', q_blk, k).astype(jnp.float32) * scale
        p = jax.nn.softmax(s, axis=-1)
        return jnp.einsum('bhqk,bkhd->bqhd', p.astype(v.dtype), v)

    o = lax.map(one_block, qb)
    return o.transpose(1, 0, 2, 3, 4).reshape(B, S, H * MLA_V_DIM)

def hybrid_mixer(x, w_in, b_gate, na_rpb, mla_q_norm, mla_w_uq, mla_kv_norm, mla_w_ukv,
                 w_branch_na, w_branch_mla, w_out, tables):
    B, S, _ = x.shape
    h = x @ w_in
    offs = [int(o) for o in np.cumsum(IN_SIZES_3)[:-1]]
    q_na, k_na, v_na, q_lat, kv_lat, k_rope, g_a, g_b = jnp.split(h, offs, axis=-1)
    shp = (B, S, NA_HEADS, NA_HEAD_DIM)
    y_a = neighbourhood_attention_2d(q_na.reshape(shp), k_na.reshape(shp), v_na.reshape(shp), na_rpb) @ w_branch_na
    y_b = latent_attention(q_lat, kv_lat, k_rope, mla_q_norm, mla_w_uq, mla_kv_norm, mla_w_ukv, tables) @ w_branch_mla
    b_a, b_b = jnp.split(b_gate, 2, axis=-1)
    merged = jax.nn.sigmoid(g_a + b_a) * y_a + jax.nn.sigmoid(g_b + b_b) * y_b
    return merged @ w_out

def swiglu(x, w_ffn_in, w_ffn_out):
    gate, up = jnp.split(x @ w_ffn_in, 2, axis=-1)
    return (jax.nn.silu(gate) * up) @ w_ffn_out

def third_inputs(seed: int = 0) -> dict:
    key = jax.random.key(seed)
    ks = jax.random.split(key, 18)
    nrm = jax.random.normal
    f32 = jnp.float32
    L = DEPTH
    return {
        "x": nrm(ks[0], (BATCH, SEQ, D_MODEL), f32),
        "w_in": nrm(ks[1], (L, D_MODEL, IN_TOTAL), f32) * D_MODEL ** -0.5,
        "b_gate": nrm(ks[2], (L, 2 * D_MODEL), f32) * 0.01,
        "na_rpb": nrm(ks[3], (L, NA_HEADS, 2 * NA_WIN_ROWS_MAX - 1, 2 * NA_WIN_COLS - 1), f32) * 0.02,
        "mla_q_norm": 1.0 + 0.01 * nrm(ks[4], (L, MLA_Q_LORA), f32),
        "mla_w_uq": nrm(ks[5], (L, MLA_Q_LORA, MLA_HEADS * MLA_QK_DIM), f32) * MLA_Q_LORA ** -0.5,
        "mla_kv_norm": 1.0 + 0.01 * nrm(ks[6], (L, MLA_KV_LORA), f32),
        "mla_w_ukv": nrm(ks[7], (L, MLA_KV_LORA, MLA_HEADS * (MLA_NOPE_DIM + MLA_V_DIM)), f32) * MLA_KV_LORA ** -0.5,
        "w_branch_na": nrm(ks[8], (L, NA_WIDTH, D_MODEL), f32) * (NA_WIDTH ** -0.5 * DN_BETA_3),
        "w_branch_mla": nrm(ks[9], (L, MLA_WIDTH, D_MODEL), f32) * (MLA_WIDTH ** -0.5 * DN_BETA_3),
        "w_out": nrm(ks[10], (L, D_MODEL, D_MODEL), f32) * (D_MODEL ** -0.5 * DN_BETA_3),
        "ln1_g": 1.0 + 0.01 * nrm(ks[11], (L, D_MODEL), f32),
        "ln1_b": 0.01 * nrm(ks[12], (L, D_MODEL), f32),
        "w_ffn_in": nrm(ks[13], (L, D_MODEL, 2 * FFN_HIDDEN), f32) * D_MODEL ** -0.5,
        "w_ffn_out": nrm(ks[14], (L, FFN_HIDDEN, D_MODEL), f32) * (FFN_HIDDEN ** -0.5 * DN_BETA_3),
        "ln2_g": 1.0 + 0.01 * nrm(ks[15], (L, D_MODEL), f32),
        "ln2_b": 0.01 * nrm(ks[16], (L, D_MODEL), f32),
    }

def third_block(x, w_in, b_gate, na_rpb, mla_q_norm, mla_w_uq, mla_kv_norm, mla_w_ukv,
              w_branch_na, w_branch_mla, w_out, ln1_g, ln1_b, w_ffn_in, w_ffn_out, ln2_g, ln2_b):
    tables = axial_rope_tables(x.shape[1])
    for l in range(DEPTH):
        m = hybrid_mixer(x, w_in[l], b_gate[l], na_rpb[l], mla_q_norm[l], mla_w_uq[l],
                         mla_kv_norm[l], mla_w_ukv[l], w_branch_na[l], w_branch_mla[l], w_out[l], tables)
        x = layer_norm_3(DN_ALPHA_3 * x + m, ln1_g[l], ln1_b[l])
        x = layer_norm_3(DN_ALPHA_3 * x + swiglu(x, w_ffn_in[l], w_ffn_out[l]), ln2_g[l], ln2_b[l])
    return x


_first_inputs_3 = third_inputs


def third_inputs(seed=0):
    import zlib

    import numpy as np

    out = dict(_first_inputs_3(seed))
    spreads = {}
    factors = {'b_gate': 8.0,
     'na_rpb': 64.0,
     'mla_q_norm': 8.0,
     'mla_w_uq': 3.532,
     'mla_kv_norm': 8.0,
     'mla_w_ukv': 3.167,
     'w_branch_mla': 3.114,
     'ln1_g': 22.793,
     'ln1_b': 23.132,
     'ln2_g': 32.718,
     'ln2_b': 32.708,
     'w_branch_na': 8.0}
    for name, (base, spread) in spreads.items():
        noise = np.random.default_rng([zlib.crc32(name.encode()), seed]).standard_normal(out[name].shape)
        drawn = base * np.exp(spread * noise) if base else spread * noise
        out[name] = __import__('jax').numpy.asarray(drawn.astype(out[name].dtype))
    for name, factor in factors.items():
        out[name] = (out[name] * factor).astype(out[name].dtype)
    return out


_narrow_inputs_3 = third_inputs


def third_inputs(seed=0):

    out = dict(_narrow_inputs_3(seed))
    wider = {'ln1_g': 4.5, 'ln1_b': 4.49, 'ln2_g': 6.44, 'ln2_b': 6.43}
    for name, times in wider.items():
        mean = out[name].mean()
        out[name] = (mean + times * (out[name] - mean)).astype(out[name].dtype)
    return out


def setup_inputs(seed=0):
    out = dict(first_inputs(seed))
    for name, value in second_inputs(seed + 1).items():
        if name != "x":
            out[name + "_2"] = value
    for name, value in third_inputs(seed + 2).items():
        if name != "x":
            out[name + "_3"] = value
    return out


def reference(
    x, mem, ffn1_wg, ffn1_wu, ffn1_wd, ln1_g, ln1_b, w_in, gdn_conv_qkv, gdn_a_log, gdn_dt_bias,
    gdn_norm_g, w_gdn_out, conv_dw_w, conv_dw_b, conv_ln_g, conv_ln_b, w_conv_out, b_conv_out,
    w_mix_out, ln2_g, ln2_b, w_xq, w_xkv, w_xo, ln3_g, ln3_b, ffn2_wg, ffn2_wu, ffn2_wd, ln4_g,
    ln4_b, norm_w_2, w_in_2, ret_norm_w_2, q_norm_w_2, k_norm_cmp_2, k_norm_slc_2, k_norm_win_2,
    cmp_pos_k_2, cmp_w1_k_2, cmp_w2_k_2, cmp_pos_v_2, cmp_w1_v_2, cmp_w2_v_2, b_gate_2, w_out_2,
    w_in_3, b_gate_3, na_rpb_3, mla_q_norm_3, mla_w_uq_3, mla_kv_norm_3, mla_w_ukv_3,
    w_branch_na_3, w_branch_mla_3, w_out_3, ln1_g_3, ln1_b_3, w_ffn_in_3, w_ffn_out_3, ln2_g_3,
    ln2_b_3,
):
    x = first_block(
        x, mem, ffn1_wg, ffn1_wu, ffn1_wd, ln1_g, ln1_b, w_in, gdn_conv_qkv, gdn_a_log,
        gdn_dt_bias, gdn_norm_g, w_gdn_out, conv_dw_w, conv_dw_b, conv_ln_g, conv_ln_b,
        w_conv_out, b_conv_out, w_mix_out, ln2_g, ln2_b, w_xq, w_xkv, w_xo, ln3_g, ln3_b,
        ffn2_wg, ffn2_wu, ffn2_wd, ln4_g, ln4_b,
    )
    x = second_block(
        x, norm_w_2, w_in_2, ret_norm_w_2, q_norm_w_2, k_norm_cmp_2, k_norm_slc_2, k_norm_win_2,
        cmp_pos_k_2, cmp_w1_k_2, cmp_w2_k_2, cmp_pos_v_2, cmp_w1_v_2, cmp_w2_v_2, b_gate_2,
        w_out_2,
    )
    return third_block(
        x, w_in_3, b_gate_3, na_rpb_3, mla_q_norm_3, mla_w_uq_3, mla_kv_norm_3, mla_w_ukv_3,
        w_branch_na_3, w_branch_mla_3, w_out_3, ln1_g_3, ln1_b_3, w_ffn_in_3, w_ffn_out_3,
        ln2_g_3, ln2_b_3,
    )


_drawn_inputs = setup_inputs


def setup_inputs(seed=0):
    import zlib

    import numpy as np

    out = dict(_drawn_inputs(seed))
    spreads = {}
    factors = {'b_gate_3': 8.0}
    for name, (base, spread) in spreads.items():
        noise = np.random.default_rng([zlib.crc32(name.encode()), seed]).standard_normal(out[name].shape)
        drawn = base * np.exp(spread * noise) if base else spread * noise
        out[name] = __import__('jax').numpy.asarray(drawn.astype(out[name].dtype))
    for name, factor in factors.items():
        out[name] = (out[name] * factor).astype(out[name].dtype)
    return out
```

```python
from contextlib import ExitStack

import numpy as np

import concourse.bass as bass
from concourse import mybir

F32 = mybir.dt.float32
F32R = mybir.dt.float32r
ACT = mybir.ActivationFunctionType
ALU = mybir.AluOpType
AX = mybir.AxisListType

P = 128
T = 512
D = 1024
KC = D // P
NT = T // P
DFF = 2816
FC = DFF // P
N_MEM = 256
ALPHA = 2.0 ** 0.25
LN_EPS = 1e-5
RMS_EPS = 1e-6
NEG = -1e30

GDN_HEADS = 8
GDN_DK = 128
CHUNK = 64
SHORT_CONV = 4
CONV_WIDTH = 31
XATTN_HEADS = 4

HEADS = 8
HD = 64
CMP_BLOCK = 32
CMP_STRIDE = 16
N_CMP = (T - CMP_BLOCK) // CMP_STRIDE + 1
CMP_HIDDEN = 256
GRID_W = 64
NA_ROWS = T // GRID_W
NA_WIN_ROWS = 8
NA_WIN_COLS = 16
MLA_QK = 96

STREAM = [
    ("ffn1_in", 22), ("ffn1_out", 11),
    ("glu", 8), ("qkv", 12), ("z", 4), ("gates", 8), ("conv_out", 4), ("gdn_out", 4), ("mix_out", 4),
    ("xk", 4), ("xv", 4), ("xq", 4), ("xo", 4),
    ("ffn2_in", 22), ("ffn2_out", 11),
    ("rqk_2", 4), ("rv_2", 2), ("mid_2", 8), ("v_2", 1), ("out_2", 4),
    ("qk_3", 4), ("v_3", 2), ("rest_3", 10), ("branches_3", 4), ("out_3", 4),
    ("ffn3_in", 22), ("ffn3_out", 11),
]
FIRST_TILE, TILES = {}, {}
N_TILES = 0
for _name, _n in STREAM:
    FIRST_TILE[_name], TILES[_name] = N_TILES, _n
    N_TILES += _n

VECTORS = [
    ("ln1_g", 8), ("ln1_b", 8), ("ln2_g", 8), ("ln2_b", 8), ("ln3_g", 8), ("ln3_b", 8), ("ln4_g", 8), ("ln4_b", 8),
    ("gdn_conv", 4 * 24), ("gdn_norm", 1), ("conv_w", 31 * 8), ("conv_b", 8), ("conv_ln_g", 8), ("conv_ln_b", 8),
    ("b_conv_out", 8),
    ("norm_2", 8), ("ret_norm", 4), ("q_norm_2", 1), ("k_cmp", 1), ("k_slc", 1), ("k_win", 1),
    ("pos_k", 32), ("pos_v", 32),
    ("b_gate_3", 16), ("mla_q", 2), ("mla_kv", 1), ("ln1_g_3", 8), ("ln1_b_3", 8), ("ln2_g_3", 8), ("ln2_b_3", 8),
    ("a_log", 8), ("dt_bias", 8), ("b_gate_2", 24), ("eps", 4),
]
VEC, N_VEC = {}, 0
for _name, _n in VECTORS:
    VEC[_name] = N_VEC
    N_VEC += _n

MATRICES = ["ident", "mean", "ones", "mean128", "mean64", "chunk_tri", "chunk_strict", "chunk_ones",
            "level1", "level2", "level4", "level8", "level16", "level32", "rope64", "rope32", "mean256"]
MAT = {n: i for i, n in enumerate(MATRICES)}

STOP_AFTER = None
DBG = (0, 8)


class Signal:

    def __init__(self, sem):
        self.sem, self.base, self.pending, self.times = sem, 0, 0, 1

    def at(self, n):
        return n + self.base

    def n(self, by=1, times=1):
        self.pending += by * times
        return by


class Kernel:
    def __init__(self, nc, ctx, dram):
        self.nc, self.dram = nc, dram
        self.signals = {}
        self.ctx = ctx
        at = (nc.sbuf_base + 63) // 64 * 64

        def place(name, shape, dt, offset):
            return nc.alloc_sbuf_tensor_at(name, shape, dt, offset=offset)

        tile = 16 * P * 4
        self.raw = place("weights_raw", [P, 2, 16, P], F32, at)
        self.whi = place("weights_hi", [P, 2, 16, P], F32R, at + 2 * tile)
        self.wlo = place("weights_lo", [P, 2, 16, P], F32R, at + 4 * tile)
        at += 6 * tile
        self.xhi = place("x_hi", [P, KC, T], F32R, at)
        self.xlo = place("x_lo", [P, KC, T], F32R, at + KC * T * 4)
        self.pair = place("pair_scratch", [P, 2 * KC, T], F32, at)
        at += 2 * KC * T * 4
        self.A = place("arena", [P, 56, T], F32, at)
        self.hhi = place("h_hi", [P, FC, T], F32R, at + 8 * T * 4)
        self.hlo = place("h_lo", [P, FC, T], F32R, at + (8 + FC) * T * 4)
        at += 56 * T * 4
        self.mats = place("mats", [P, len(MATRICES), P], F32, at)
        at += len(MATRICES) * P * 4
        self.vecs = place("vecs", [P, N_VEC], F32, at)
        at += (N_VEC * 4 + 31) // 32 * 32
        self.small = place("small", [P, 1184], F32, at)
        at += 1184 * 4
        assert at <= nc.sbuf_usable_end
        self.ps = nc.alloc_psum_tensor("psum", [P, 8, 512], F32)

    def s(self, name):
        if name not in self.signals:
            self.signals[name] = Signal(self.nc.alloc_semaphore(name))
        return self.signals[name]

    def eps(self, value):
        return self.vec("eps", {LN_EPS: 0, RMS_EPS: 1, 1.0: 2, 64 * RMS_EPS: 3}[value])

    def mat(self, name):
        return self.mats[:, MAT[name], :]

    def vec(self, name, c=0, n=1):
        return self.vecs[:, VEC[name] + c:VEC[name] + c + n]

    def end_block(self, name):
        for s in self.signals.values():
            s.base += s.pending
            s.pending = 0
        if name == STOP_AFTER:
            raise StopIteration(name)


def span(names):
    names = [names] if isinstance(names, str) else names
    return FIRST_TILE[names[0]], sum(TILES[n] for n in names)


def tile_loop(eng, names, body, unroll=False):
    first, n = span(names)
    pairs = (n - 2) // 2
    done = 0
    if pairs >= 2 and not unroll:
        with eng.Fori(0, pairs) as i:
            for j in range(2):
                g = first + j
                body(2 * i + j, 2 * i + g, i + (g // 2 + 1), g % 2, pairs)
        done = 2 * pairs
    for t in range(done, n):
        g = first + t
        body(t, g, g // 2 + 1, g % 2, 1)



def stream_load(K, sp, name):
    raw_loaded, lo_ready = [K.s("raw_loaded_0"), K.s("raw_loaded_1")], K.s("lo_ready")

    def body(t, g, uses, slot, times):
        if isinstance(g, int) and g + 2 >= N_TILES:
            return
        sp.wait_ge(lo_ready.sem, g + 1)
        sp.dma_start(K.raw[:, slot, :, :], K.dram["stream"][bass.ds(g + 2, 1) if not isinstance(g, int)
                                                           else slice(g + 2, g + 3)].rearrange(
            "a p k n -> (a p) k n")).then_inc(raw_loaded[slot].sem, 16)
    tile_loop(sp, name, body)


def split_hi(K, act, g, uses, slot, times):
    if isinstance(g, int) and g >= N_TILES:
        return
    act.wait_ge(K.s(f"raw_loaded_{slot}").sem, uses * 16)
    if not isinstance(g, int) or g >= 2:
        act.wait_ge(K.s("tile_done").sem, g - 1)
    K.nc.scalar.activation(K.whi[:, slot, :, :], K.raw[:, slot, :, :], ACT.Copy).then_inc(K.s("hi_ready").sem, 1)


def stream_split_lo(K, pool, name):
    def body(t, g, uses, slot, times):
        if isinstance(g, int) and g + 1 >= N_TILES:
            return
        pool.wait_ge(K.s("hi_ready").sem, g + 2)
        K.nc.gpsimd.tensor_tensor(K.wlo[:, 1 - slot, :, :], K.raw[:, 1 - slot, :, :],
                                  K.whi[:, 1 - slot, :, :].bitcast(F32),
                                  ALU.subtract).then_inc(K.s("lo_ready").sem, 1)
    tile_loop(pool, name, body)


def stream_act(K, act, name, evac=None, unroll=False):
    def body(t, g, uses, slot, times):
        split_hi(K, act, g + 1, uses + slot, 1 - slot, times)
        if evac:
            evac(t, g, slot, times)
    tile_loop(act, name, body, unroll)


def stream_dve(K, dve, name, evac, unroll=False):
    tile_loop(dve, name, lambda t, g, uses, slot, times: evac(t, g, slot, times), unroll)


def three_products(K, out, whi, wlo, xhi, xlo, start, stop):
    K.nc.tensor.matmul(out, whi, xhi, start=start, stop=False)
    K.nc.tensor.matmul(out, whi, xlo, start=False, stop=False)
    return K.nc.tensor.matmul(out, wlo, xhi, start=False, stop=stop)


def stream_pe(K, pe, name, n=T, t0=0):
    xhi, xlo = K.xhi, K.xlo
    free = [K.s("bank_free_0"), K.s("bank_free_1")]
    done = [K.s("first_done"), K.s("tile_done")]

    def body(t, g, uses, slot, times):
        pe.wait_ge(K.s("lo_ready").sem, g + 1)
        for j in range(2):
            pe.wait_ge(free[j].sem, free[j].at(t + (t0 - 1)))
            for k in range(KC):
                last = three_products(K, K.ps[:, 2 * slot + j, :n], K.whi[:, slot, 8 * j + k, :],
                                      K.wlo[:, slot, 8 * j + k, :], xhi[:, k, :n], xlo[:, k, :n],
                                      k == 0, k == KC - 1)
            last.then_inc(done[j].sem, 1)
    tile_loop(pe, name, body)


def wait_bank(K, eng, g, j):
    eng.wait_ge(K.s(("first_done", "tile_done")[j]).sem, g + 1)



def phase_start(K):
    nc, dram = K.nc, K.dram
    with nc.Block() as block:
        @block.sync
        def _(sp):
            for i in range(2):
                sp.dma_start(K.raw[:, i, :, :], dram["stream"][i]).then_inc(K.s(f"raw_loaded_{i}").sem, 16)
            sp.dma_start(K.A[:, 0:8, :], dram["x_t"]).then_inc(K.s("x_in").sem, 16)
            sp.dma_start(K.vecs[:, :], dram["vecs"]).then_inc(K.s("loaded").sem, K.s("loaded").n(16))
            sp.dma_start(K.mats[:, :, :], dram["mats"]).then_inc(K.s("loaded").sem, K.s("loaded").n(16))
            sp.dma_start(K.small[:, 0:320], dram["small"]).then_inc(K.s("loaded").sem, K.s("loaded").n(16))
            sp.wait_ge(K.s("loaded").sem, 48)

        @block.scalar
        def _(act):
            split_hi(K, act, 0, 1, 0, 1)
            nc.scalar.nop().then_inc(K.s("bank_free_0").sem, K.s("bank_free_0").n(2))

        @block.gpsimd
        def _(pool):
            pool.wait_ge(K.s("hi_ready").sem, 1)
            nc.gpsimd.tensor_tensor(K.wlo[:, 0, :, :], K.raw[:, 0, :, :], K.whi[:, 0, :, :].bitcast(F32),
                                    ALU.subtract).then_inc(K.s("lo_ready").sem, 1)

        @block.vector
        def _(dve):
            nc.vector.nop().then_inc(K.s("bank_free_1").sem, K.s("bank_free_1").n(2))
            dve.wait_ge(K.s("x_in").sem, 16)
            split_chunks(K, dve, 0)
    K.end_block("start")


def split_chunks(K, dve, unit, n=KC, width=T):
    s = K.s("x_hi_done")
    units = unit if isinstance(unit, list) else [unit + c for c in range(n)]
    for c in range(n):
        K.nc.vector.tensor_copy(K.xhi[:, c, :width], K.A[:, units[c], :width]).then_inc(s.sem, s.n())
    for c in range(n):
        dve.wait_ge(s.sem, s.at(c + 1))
        K.nc.vector.tensor_tensor(K.xlo[:, c, :width], K.A[:, units[c], :width],
                                  K.xhi[:, c, :width].bitcast(F32), ALU.subtract).then_inc(
            K.s("x_split").sem, K.s("x_split").n())


def phase_ffn_in(K, name, weight=0.5):
    nc = K.nc
    silu, h_ready, hhi_ready = K.s("silu_ready"), K.s("h_ready"), K.s("h_hi_ready")
    sg, h = K.A[:, 52:54, :], K.A[:, 54:56, :]
    with nc.Block() as block:
        @block.sync
        def _(sp):
            stream_load(K, sp, name)

        @block.gpsimd
        def _(pool):
            stream_split_lo(K, pool, name)

        @block.tensor
        def _(pe):
            stream_pe(K, pe, name)

        @block.scalar
        def _(act):
            def evac(t, g, slot, times):
                wait_bank(K, act, g, 0)
                nc.scalar.activation(sg[:, slot, :], K.ps[:, 2 * slot, :], ACT.Silu).then_inc(silu.sem, silu.n(1, times))
            stream_act(K, act, name, evac)

        @block.vector
        def _(dve):
            def evac(t, g, slot, times):
                wait_bank(K, dve, g, 1)
                dve.wait_ge(silu.sem, silu.at(t + 1))
                nc.vector.scalar_tensor_tensor(h[:, slot, :], sg[:, slot, :], weight, K.ps[:, 2 * slot + 1, :],
                                               ALU.mult, ALU.mult).then_inc(h_ready.sem, h_ready.n(1, times))
                dve.wait_ge(h_ready.sem, h_ready.at(t + 1))
                nc.vector.nop().then_inc(K.s("bank_free_0").sem, K.s("bank_free_0").n(1, times))
                nc.vector.nop().then_inc(K.s("bank_free_1").sem, K.s("bank_free_1").n(1, times))
                at = bass.ds(t, 1) if not isinstance(t, int) else slice(t, t + 1)
                nc.vector.tensor_copy(K.hhi[:, at, :], h[:, slot:slot + 1, :]).then_inc(hhi_ready.sem, hhi_ready.n(1, times))
                dve.wait_ge(hhi_ready.sem, hhi_ready.at(t + 1))
                nc.vector.tensor_tensor(K.hlo[:, at, :], h[:, slot:slot + 1, :], K.hhi[:, at, :].bitcast(F32),
                                        ALU.subtract)
            stream_dve(K, dve, name, evac)
    K.end_block(name)


def phase_ffn_out(K, name):
    nc = K.nc
    with nc.Block() as block:
        @block.sync
        def _(sp):
            stream_load(K, sp, name)

        @block.gpsimd
        def _(pool):
            stream_split_lo(K, pool, name)

        @block.scalar
        def _(act):
            stream_act(K, act, name)

        @block.tensor
        def _(pe):
            def body(t, g, uses, slot, times):
                pe.wait_ge(K.s("lo_ready").sem, g + 1)
                for j in range(2):
                    f = bass.ds(2 * t + j, 1) if not isinstance(t, int) else slice(2 * t + j, 2 * t + j + 1)
                    for m in range(KC):
                        last = three_products(K, K.ps[:, m:m + 1, :], K.whi[:, slot, 8 * j + m, :],
                                              K.wlo[:, slot, 8 * j + m, :], K.hhi[:, f, :], K.hlo[:, f, :],
                                              isinstance(t, int) and t == 0 and j == 0,
                                              isinstance(t, int) and t == TILES[name] - 1 and j == 1)
                    last.then_inc(K.s(("first_done", "tile_done")[j]).sem, 1)
            n, first = TILES[name], FIRST_TILE[name]
            body(0, first, 0, first % 2, 1)
            loops = (n - 3) // 2
            with pe.Fori(0, loops) as i:
                for j in range(2):
                    body(2 * i + (1 + j), 2 * i + (first + 1 + j), 0, (first + 1 + j) % 2, loops)
            for t in range(1 + 2 * loops, n):
                body(t, first + t, 0, (first + t) % 2, 1)

        @block.vector
        def _(dve):
            wait_bank(K, dve, FIRST_TILE[name] + TILES[name] - 1, 1)
            for m in range(KC):
                nc.vector.scalar_tensor_tensor(K.A[:, m, :], K.A[:, m, :], ALPHA, K.ps[:, m, :], ALU.mult, ALU.add)
    K.end_block(name)


def phase_layer_norm(K, name, src, g, b, func=ACT.Identity, split=True, out=None):
    nc = K.nc
    s = K.s
    sq = K.pair
    with nc.Block() as block:
        @block.tensor
        def _(pe):
            for c in range(KC):
                last = nc.tensor.matmul(K.ps[:, 4, :], K.mat("mean"), K.A[:, src + c, :], start=c == 0, stop=c == KC - 1)
            last.then_inc(s("mean_ready").sem, s("mean_ready").n())
            for c in range(KC):
                pe.wait_ge(s("squared").sem, s("squared").at(c + 1))
                last = nc.tensor.matmul(K.ps[:, 5, :], K.mat("mean"), sq[:, c, :], start=c == 0, stop=c == KC - 1)
            last.then_inc(s("var_ready").sem, s("var_ready").n())

        @block.scalar
        def _(act):
            for c in range(KC):
                act.wait_ge(s("centred").sem, s("centred").at(c + 1))
                nc.scalar.activation(sq[:, c, :], K.A[:, src + c, :], ACT.Square).then_inc(s("squared").sem, s("squared").n())
            act.wait_ge(s("var_ready").sem, s("var_ready").at(1))
            nc.scalar.activation(sq[:, 9, :], K.ps[:, 5, :], ACT.Abs_reciprocal_sqrt,
                                 bias=K.eps(LN_EPS)).then_inc(s("rstd_ready").sem, s("rstd_ready").n())
            for c in range(KC):
                act.wait_ge(s("scaled").sem, s("scaled").at(c + 1))
                nc.scalar.activation(K.A[:, src + c, :], K.A[:, src + c, :], func, bias=K.vec(b, c),
                                     scale=K.vec(g, c)).then_inc(s("normed").sem, s("normed").n())

        @block.vector
        def _(dve):
            dve.wait_ge(s("mean_ready").sem, s("mean_ready").at(1))
            for c in range(KC):
                nc.vector.tensor_tensor(K.A[:, src + c, :], K.A[:, src + c, :], K.ps[:, 4, :],
                                        ALU.subtract).then_inc(s("centred").sem, s("centred").n())
            dve.wait_ge(s("rstd_ready").sem, s("rstd_ready").at(1))
            for c in range(KC):
                nc.vector.tensor_tensor(K.A[:, src + c, :], K.A[:, src + c, :], sq[:, 9, :],
                                        ALU.mult).then_inc(s("scaled").sem, s("scaled").n())
            if split:
                dve.wait_ge(s("normed").sem, s("normed").at(KC))
                split_chunks(K, dve, src)
    K.end_block(name)


def phase_stream(K, label, names, pe=None, act=None, dve=None, load=None, act_first=None, pe_last=None,
                 presplit=None, unroll=True, end=True):
    nc = K.nc
    with nc.Block() as block:
        @block.sync
        def _(sp):
            if load:
                load(sp)
            stream_load(K, sp, names)

        @block.gpsimd
        def _(pool):
            stream_split_lo(K, pool, names)

        @block.tensor
        def _(pe_):
            if presplit is not None:
                pe_.wait_ge(K.s("x_split").sem, K.s("x_split").at(KC))
            if pe:
                pe(pe_)
            else:
                stream_pe(K, pe_, names)
            if pe_last:
                pe_last(pe_)

        @block.scalar
        def _(act_):
            if act_first:
                act_first(act_)
            stream_act(K, act_, names, act and (lambda t, g, slot, times: act(act_, t, g, slot)), unroll)

        @block.vector
        def _(dve_):
            if presplit is not None:
                split_chunks(K, dve_, presplit)
            if dve:
                stream_dve(K, dve_, names, lambda t, g, slot, times: dve(dve_, t, g, slot), unroll)
    K.end_block(label)


def free_bank(K, j):
    s = K.s(f"bank_free_{j}")
    return s.sem, s.n()


def phase_glu(K):
    nc, s = K.nc, K.s
    sg = K.A[:, 48:50, :]

    def load(sp):
        sp.dma_start(K.dram["keep_x"], K.A[:, 0:8, :]).then_inc(s("spilled").sem, s("spilled").n(16))

    def act(act, t, g, slot):
        wait_bank(K, act, g, 1)
        if t >= 2:
            act.wait_ge(s("glu_ready").sem, s("glu_ready").at(t - 1))
        nc.scalar.activation(sg[:, slot, :], K.ps[:, 2 * slot + 1, :], ACT.Sigmoid).then_inc(s("sigmoid").sem, s("sigmoid").n())

    def dve(dve, t, g, slot):
        wait_bank(K, dve, g, 0)
        dve.wait_ge(s("sigmoid").sem, s("sigmoid").at(t + 1))
        nc.vector.tensor_tensor(K.A[:, 8 + t, :], K.ps[:, 2 * slot, :], sg[:, slot, :],
                                ALU.mult).then_inc(s("glu_ready").sem, s("glu_ready").n())
        dve.wait_ge(s("glu_ready").sem, s("glu_ready").at(t + 1))
        nc.vector.nop().then_inc(*free_bank(K, 0))
        nc.vector.nop().then_inc(*free_bank(K, 1))

    def pe_last(pe):
        for i in range(NT):
            for k in range(KC):
                last = nc.tensor.matmul(K.ps[:, 6, 16 * i:16 * i + 16], K.A[:, k, P * i:P * i + P],
                                        K.small[:, 16 * k:16 * k + 16], start=k == 0, stop=k == KC - 1)
        last.then_inc(s("ab_ready").sem, s("ab_ready").n())
        pe.wait_ge(s("spilled").sem, s("spilled").at(16))
    phase_stream(K, "glu", "glu", act=act, dve=dve, load=load, pe_last=pe_last)


AB, G, BETA, GC, BG, KD, EGL, T1 = 320, 384, 416, 448, 480, 512, 544, 608


def phase_projections(K):
    nc, s = K.nc, K.s
    tmp = K.A[:, 48:56, :]
    names = ["qkv", "z", "gates"]

    def act(act, t, g, slot):
        for j in range(2):
            c = 2 * t + j
            if t < 12:
                act.wait_ge(s("short_done").sem, s("short_done").at(4 * (c + 1)))
                nc.scalar.activation(K.A[:, 24 + c, :], tmp[:, 2 * slot + j, :], ACT.Silu).then_inc(
                    s("qkv_ready").sem, s("qkv_ready").n())
            else:
                u = c - 24
                wait_bank(K, act, g, j)
                if u >= 4:
                    act.wait_ge(s(f"spilled_{u % 4}").sem, s(f"spilled_{u % 4}").at(16 * (u // 4)))
                nc.scalar.activation(tmp[:, 4 + u % 4, :], K.ps[:, 2 * slot + j, :],
                                     ACT.Silu if t < 16 else ACT.Sigmoid).then_inc(
                    s("gate_ready").sem, s("gate_ready").n())
                act.wait_ge(s("gate_ready").sem, s("gate_ready").at(u + 1))
                act.dma_start(K.dram["keep_gates"][u], tmp[:, 4 + u % 4, :]).then_inc(
                    s(f"spilled_{u % 4}").sem, s(f"spilled_{u % 4}").n(16))
        if t == 23:
            for r in range(4):
                act.wait_ge(s(f"spilled_{r}").sem, s(f"spilled_{r}").at(16 * 6))

    def long_conv():
        acc, src = 16, 8
        done = s("long_done")
        n = 0
        for tap in range(CONV_WIDTH - 1, -1, -1):
            back = CONV_WIDTH - 1 - tap
            for c in range(KC):
                w = K.vec("conv_w", 8 * tap + c)
                if back == 0:
                    nc.vector.tensor_scalar(K.A[:, acc + c, :], K.A[:, src + c, :], w, K.vec("conv_b", c),
                                            ALU.mult, ALU.add).then_inc(done.sem, done.n())
                else:
                    nc.vector.wait_ge(done.sem, done.at(n - KC + 1))
                    nc.vector.scalar_tensor_tensor(K.A[:, acc + c, back:], K.A[:, src + c, :T - back], w,
                                                   K.A[:, acc + c, back:], ALU.mult, ALU.add).then_inc(done.sem, done.n())
                n += 1
                yield

    conv = long_conv()

    def dve(dve, t, g, slot):
        if t < 12:
            short = s("short_done")
            for j in range(2):
                c = 2 * t + j
                bank, acc = K.ps[:, 2 * slot + j, :], tmp[:, 2 * slot + j, :]
                wait_bank(K, dve, g, j)
                if t >= 2:
                    dve.wait_ge(s("qkv_ready").sem, s("qkv_ready").at(c - 3))
                for tap in range(SHORT_CONV - 1, -1, -1):
                    back = SHORT_CONV - 1 - tap
                    w = K.vec("gdn_conv", 4 * c + tap)
                    if back == 0:
                        nc.vector.tensor_scalar(acc, bank, w, None, ALU.mult).then_inc(short.sem, short.n())
                    else:
                        dve.wait_ge(short.sem, short.at(4 * c + back))
                        nc.vector.scalar_tensor_tensor(acc[:, back:], bank[:, :T - back], w, acc[:, back:],
                                                       ALU.mult, ALU.add).then_inc(short.sem, short.n())
                dve.wait_ge(short.sem, short.at(4 * c + 4))
                nc.vector.nop().then_inc(*free_bank(K, j))
        else:
            for j in range(2):
                dve.wait_ge(s("gate_ready").sem, s("gate_ready").at(2 * t + j - 23))
                nc.vector.nop().then_inc(*free_bank(K, j))
        for _ in range(8 if t < 12 else 13):
            next(conv, None)
    phase_stream(K, "projections", names, act=act, dve=dve)


def phase_conv_out(K):
    nc, s = K.nc, K.s

    def load(sp):
        sp.dma_start(K.A[:, 0:8, :], K.dram["keep_gates"][16:24].rearrange("c p n -> p c n")).then_inc(
            s("reloaded").sem, s("reloaded").n(16))

    def dve(dve, t, g, slot):
        if t == 0:
            dve.wait_ge(s("reloaded").sem, s("reloaded").at(16))
        for j in range(2):
            c = 2 * t + j
            wait_bank(K, dve, g, j)
            nc.vector.scalar_tensor_tensor(K.A[:, 8 + c, :], K.ps[:, 2 * slot + j, :], K.vec("b_conv_out", c),
                                           K.A[:, c, :], ALU.add, ALU.mult).then_inc(*free_bank(K, j))
    phase_stream(K, "conv_out", "conv_out", dve=dve, load=load)
    with nc.Block() as block:
        @block.sync
        def _(sp):
            sp.dma_start(K.dram["keep_yc"], K.A[:, 8:16, :]).then_inc(s("spilled").sem, s("spilled").n(16))
            sp.wait_ge(s("spilled").sem, s("spilled").at(16))
    K.end_block("yc_spill")


def phase_gdn_gates(K):
    nc, s = K.nc, K.s

    def f(at, n=32):
        return K.small[:, at:at + n]

    def th(at):
        return K.small[:, at:at + 32].rearrange("p (i h) -> p i h", h=GDN_HEADS)

    a_in = K.ps[:, 6, 0:64].rearrange("p (i c) -> p i c", c=16)
    with nc.Block() as block:
        @block.vector
        def _(dve):
            step = s("gates_dve")

            def link(ins, n):
                ins.then_inc(step.sem, step.n())
                dve.wait_ge(step.sem, step.at(n))
            row = K.vec("dt_bias", 0, 8).unsqueeze(1).broadcast_to([P, NT, 8])
            link(nc.vector.tensor_tensor(th(T1), a_in[:, :, 0:8], row, ALU.add), 1)
            link(nc.vector.tensor_scalar(f(T1 + 32), f(T1), -1.0, None, ALU.mult), 2)
            link(nc.vector.tensor_tensor(f(T1 + 32), f(T1), f(T1 + 32), ALU.min), 3)
            dve.wait_ge(s("gates_act").sem, s("gates_act").at(2))
            link(nc.vector.scalar_tensor_tensor(f(T1), f(T1), 0.0, f(T1 + 64), ALU.max, ALU.add), 4)
            row = f(T1 + 96, 8).unsqueeze(1).broadcast_to([P, NT, 8])
            dve.wait_ge(s("gates_act").sem, s("gates_act").at(3))
            link(nc.vector.tensor_tensor(th(G), th(T1), row, ALU.mult), 5)
            link(nc.vector.tensor_scalar(f(G), f(G), -1.0, None, ALU.mult), 6)
            dve.wait_ge(s("gates_pe").sem, s("gates_pe").at(1))
            link(nc.vector.tensor_copy(f(GC), K.ps[:, 5, 0:32]), 7)
            link(nc.vector.tensor_tensor(f(KD), K.ps[:, 5, 32:64], f(GC), ALU.subtract), 8)
            dve.wait_ge(s("gates_act").sem, s("gates_act").at(5))
            link(nc.vector.tensor_tensor(f(BG), f(BG), f(BETA), ALU.mult), 9)

        @block.scalar
        def _(act):
            done, dve_done = s("gates_act"), s("gates_dve")
            act.wait_ge(dve_done.sem, dve_done.at(3))
            nc.scalar.activation(f(T1 + 32), f(T1 + 32), ACT.Exp).then_inc(done.sem, done.n())
            act.wait_ge(done.sem, done.at(1))
            nc.scalar.activation(f(T1 + 64), f(T1 + 32), ACT.Ln, bias=K.eps(1.0)).then_inc(done.sem, done.n())
            nc.scalar.activation(f(T1 + 96, 8), K.vec("a_log", 0, 8), ACT.Exp).then_inc(done.sem, done.n())
            nc.scalar.activation(th(BETA), a_in[:, :, 8:16], ACT.Sigmoid).then_inc(done.sem, done.n())
            act.wait_ge(dve_done.sem, dve_done.at(7))
            nc.scalar.activation(f(BG), f(GC), ACT.Exp).then_inc(done.sem, done.n())
            act.wait_ge(dve_done.sem, dve_done.at(8))
            nc.scalar.activation(f(KD), f(KD), ACT.Exp).then_inc(done.sem, done.n())

        @block.tensor
        def _(pe):
            pe.wait_ge(s("gates_dve").sem, s("gates_dve").at(6))
            nc.tensor.matmul(K.ps[:, 5, 0:32], K.mat("chunk_tri"), f(G), start=True, stop=True)
            nc.tensor.matmul(K.ps[:, 5, 32:64], K.mat("chunk_ones"), f(G), start=True, stop=True).then_inc(
                s("gates_pe").sem, s("gates_pe").n())
    K.end_block("gdn_gates")


def phase_head_norm(K, label, items, scratch, eps=RMS_EPS, after=None):
    nc, s = K.nc, K.s
    n = len(items)
    sq, rstd = K.A[:, scratch:scratch + 2, :], K.A[:, scratch + 2:scratch + 4, :]
    with nc.Block() as block:
        @block.scalar
        def _(act):
            def square(i):
                if i >= 2:
                    act.wait_ge(s("norm_sum").sem, s("norm_sum").at(i - 1))
                nc.scalar.activation(sq[:, i % 2, :], K.A[:, items[i][0], :], ACT.Square).then_inc(
                    s("norm_sq").sem, s("norm_sq").n())
            square(0)
            for i in range(n):
                if i + 1 < n:
                    square(i + 1)
                act.wait_ge(s("norm_sum").sem, s("norm_sum").at(i + 1))
                if i >= 2:
                    act.wait_ge(s("norm_out").sem, s("norm_out").at(i - 1))
                nc.scalar.activation(rstd[:, i % 2, :], K.ps[:, i % 4, :], ACT.Abs_reciprocal_sqrt,
                                     bias=K.eps(eps(i) if callable(eps) else eps)).then_inc(s("norm_rstd").sem, s("norm_rstd").n())

        @block.tensor
        def _(pe):
            for i in range(n):
                pe.wait_ge(s("norm_sq").sem, s("norm_sq").at(i + 1))
                if i >= 4:
                    pe.wait_ge(s("norm_rstd").sem, s("norm_rstd").at(i - 3))
                nc.tensor.matmul(K.ps[:, i % 4, :], K.mat(items[i][1]), sq[:, i % 2, :], start=True,
                                 stop=True).then_inc(s("norm_sum").sem, s("norm_sum").n())

        @block.sync
        def _(sp):
            if after:
                after(sp)

        @block.vector
        def _(dve):
            for i, (c, _, gain, *times) in enumerate(items):
                dve.wait_ge(s("norm_rstd").sem, s("norm_rstd").at(i + 1))
                nc.vector.scalar_tensor_tensor(K.A[:, c, :], K.A[:, c, :], gain, rstd[:, i % 2, :], ALU.mult,
                                               ALU.mult).then_inc(s("norm_out").sem, s("norm_out").n())
                if times:
                    if i == 0 and after:
                        dve.wait_ge(s("reloaded").sem, s("reloaded").at(16))
                    dve.wait_ge(s("norm_out").sem, s("norm_out").at(i + 1))
                    nc.vector.tensor_tensor(K.A[:, c, :], K.A[:, c, :], K.A[:, times[0], :], ALU.mult)
    K.end_block(label)


def tiles_of(ap):
    return ap.rearrange("p (i n) -> p i n", n=P)


def over_tiles(ap):
    return ap.unsqueeze(1).broadcast_to([P, NT, P])


def per_token(K, at, h):
    return K.small[:, at:at + 32].rearrange("p (i h) -> p i h", h=8)[:, :, h:h + 1].broadcast_to([P, NT, P])


UU, AT, MT, TT, QQ, KK, VV = 0, 8, 16, 48, 24, 32, 40


def phase_gdn_matrices(K):
    nc, s = K.nc, K.s
    A, W = K.A, K.pair

    def w(kind, h):
        return W[:, 2 * kind + h % 2, :]
    TRI, DIAG, DEC, EXPG, MD = range(5)
    with nc.Block() as block:
        @block.vector
        def _(dve):
            step = s("mat_dve")
            state = [0]

            def link(ins):
                ins.then_inc(step.sem, step.n())
                state[0] += 1

            def settle():
                dve.wait_ge(step.sem, step.at(state[0]))

            def first(h):
                if h >= 2:
                    dve.wait_ge(s("mat_pe").sem, s("mat_pe").at(2 * (h - 1)))
                link(nc.vector.tensor_tensor(tiles_of(w(TRI, h)), over_tiles(K.mat("chunk_tri")), per_token(K, G, h), ALU.mult))
                link(nc.vector.tensor_tensor(tiles_of(w(DIAG, h)), over_tiles(K.mat("ident")), per_token(K, BETA, h), ALU.mult))
                settle()
                nc.vector.nop().then_inc(s("mat_in").sem, s("mat_in").n())
            first(0)
            for h in range(GDN_HEADS):
                b = 4 * (h % 2)
                if h + 1 < GDN_HEADS:
                    first(h + 1)
                dve.wait_ge(s("mat_pe").sem, s("mat_pe").at(2 * h + 1))
                link(nc.vector.tensor_tensor(tiles_of(w(DEC, h)), tiles_of(K.ps[:, b, :]), per_token(K, GC, h), ALU.subtract))
                settle()
                link(nc.vector.tensor_scalar(w(DEC, h), w(DEC, h), 0.0, None, ALU.min))
                settle()
                nc.vector.nop().then_inc(s("mat_dec").sem, s("mat_dec").n())
                dve.wait_ge(s("mat_pe").sem, s("mat_pe").at(2 * h + 2))
                dve.wait_ge(s("mat_exp").sem, s("mat_exp").at(2 * h + 2))
                link(nc.vector.tensor_tensor(tiles_of(w(DEC, h)), tiles_of(w(DEC, h)), over_tiles(K.mat("chunk_tri")), ALU.mult))
                link(nc.vector.tensor_tensor(A[:, QQ + h, :], A[:, QQ + h, :], w(EXPG, h), ALU.mult))
                settle()
                link(nc.vector.tensor_tensor(A[:, AT + h, :], w(DEC, h), K.ps[:, b + 3, :], ALU.mult))
                link(nc.vector.tensor_tensor(w(MD, h), w(DEC, h), K.ps[:, b + 1, :], ALU.mult))
                settle()
                link(nc.vector.tensor_tensor(A[:, MT + h, :], w(MD, h), K.ps[:, b + 2, :], ALU.mult))
                settle()
                link(nc.vector.tensor_tensor(tiles_of(w(MD, h)), tiles_of(A[:, MT + h, :]), over_tiles(K.mat("level1")), ALU.mult))
                settle()
                link(nc.vector.tensor_tensor(tiles_of(A[:, UU + h, :]), over_tiles(K.mat("ident")), tiles_of(w(MD, h)), ALU.subtract))
                settle()
                nc.vector.nop().then_inc(s("mat_u").sem, s("mat_u").n())

        @block.scalar
        def _(act):
            for h in range(GDN_HEADS):
                b = 4 * (h % 2)
                act.wait_ge(s("mat_dec").sem, s("mat_dec").at(h + 1))
                nc.scalar.activation(w(DEC, h), w(DEC, h), ACT.Exp).then_inc(s("mat_exp").sem, s("mat_exp").n())
                nc.scalar.activation(w(EXPG, h), K.ps[:, b, :], ACT.Exp).then_inc(s("mat_exp").sem, s("mat_exp").n())
                nc.scalar.activation(K.small[:, EGL + 8 * h:EGL + 8 * h + 8],
                                     K.ps[:, b, :].rearrange("p (n c) -> p n c", c=CHUNK)[:, :, CHUNK - 1],
                                     ACT.Exp).then_inc(s("mat_egl").sem, s("mat_egl").n())
                act.wait_ge(s("mat_t").sem, s("mat_t").at(h + 1))
                nc.scalar.activation(A[:, TT + h, :], K.ps[:, b, :], ACT.Copy).then_inc(s("mat_tc").sem, s("mat_tc").n())

        @block.tensor
        def _(pe):
            def products(h):
                b = 4 * (h % 2)
                if h >= 2:
                    pe.wait_ge(s("mat_tc").sem, s("mat_tc").at(h - 1))
                    pe.wait_ge(s("mat_u").sem, s("mat_u").at(h - 1))
                pe.wait_ge(s("mat_in").sem, s("mat_in").at(h + 1))
                nc.tensor.matmul(K.ps[:, b, :], K.mat("ones"), w(TRI, h), start=True, stop=True).then_inc(
                    s("mat_pe").sem, s("mat_pe").n())
                nc.tensor.matmul(K.ps[:, b + 1, :], K.mat("ones"), w(DIAG, h), start=True, stop=True)
                for i in range(NT):
                    t = slice(P * i, P * i + P)
                    nc.tensor.matmul(K.ps[:, b + 2, t], A[:, KK + h, t], A[:, KK + h, t], start=True, stop=True)
                    last = nc.tensor.matmul(K.ps[:, b + 3, t], A[:, KK + h, t], A[:, QQ + h, t], start=True, stop=True)
                last.then_inc(s("mat_pe").sem, s("mat_pe").n())
            products(0)
            for h in range(GDN_HEADS):
                b = 4 * (h % 2)
                if h + 1 < GDN_HEADS:
                    products(h + 1)
                pe.wait_ge(s("mat_u").sem, s("mat_u").at(h + 1))
                pe.wait_ge(s("mat_egl").sem, s("mat_egl").at(h + 1))
                for i in range(NT):
                    t = slice(P * i, P * i + P)
                    last = nc.tensor.transpose(K.ps[:, b, t], A[:, UU + h, t], K.mat("ident"))
                last.then_inc(s("mat_t").sem, s("mat_t").n())
    K.end_block("gdn_matrices")


def phase_gdn_inverse(K):
    nc, s = K.nc, K.s
    A, W = K.A, K.pair
    items = [(level, h) for level in (2, 4, 8, 16, 32) for h in range(GDN_HEADS)]
    n = len(items)
    with nc.Block() as block:
        @block.gpsimd
        def _(pool):
            for x, (level, h) in enumerate(items):
                if x >= 3:
                    pool.wait_ge(s("inv_lt").sem, s("inv_lt").at(x - 2))
                nc.gpsimd.tensor_tensor(tiles_of(W[:, x % 3, :]), tiles_of(A[:, MT + h, :]),
                                        over_tiles(K.mat(f"level{level}")), ALU.mult).then_inc(s("inv_mask").sem, s("inv_mask").n())

        @block.vector
        def _(dve):
            for x, (level, h) in enumerate(items):
                dve.wait_ge(s("inv_tlt").sem, s("inv_tlt").at(x + 1))
                if level < 32:
                    nc.vector.tensor_tensor(A[:, TT + h, :], A[:, TT + h, :], K.ps[:, 2 + x % 2, :], ALU.subtract)
                nc.vector.tensor_tensor(A[:, UU + h, :], A[:, UU + h, :], K.ps[:, 4 + x % 2, :],
                                        ALU.subtract).then_inc(s("inv_done").sem, s("inv_done").n())

        @block.scalar
        def _(act):
            for x in range(n):
                act.wait_ge(s("inv_lt").sem, s("inv_lt").at(x + 1))
                if x >= 2:
                    act.wait_ge(s("inv_tlt").sem, s("inv_tlt").at(x - 1))
                nc.scalar.activation(W[:, 3 + x % 2, :], K.ps[:, x % 2, :], ACT.Copy).then_inc(s("inv_copy").sem, s("inv_copy").n())

        @block.tensor
        def _(pe):
            def lt(x):
                level, h = items[x]
                pe.wait_ge(s("inv_mask").sem, s("inv_mask").at(x + 1))
                if x >= 8:
                    pe.wait_ge(s("inv_done").sem, s("inv_done").at(x - 7))
                if x >= 2:
                    pe.wait_ge(s("inv_copy").sem, s("inv_copy").at(x - 1))
                for i in range(NT):
                    t = slice(P * i, P * i + P)
                    last = nc.tensor.matmul(K.ps[:, x % 2, t], W[:, x % 3, t], A[:, TT + h, t], start=True, stop=True)
                last.then_inc(s("inv_lt").sem, s("inv_lt").n())
            lt(0)
            for x, (level, h) in enumerate(items):
                if x + 1 < n:
                    lt(x + 1)
                pe.wait_ge(s("inv_copy").sem, s("inv_copy").at(x + 1))
                if x >= 2:
                    pe.wait_ge(s("inv_done").sem, s("inv_done").at(x - 1))
                for i in range(NT):
                    t = slice(P * i, P * i + P)
                    if level < 32:
                        nc.tensor.matmul(K.ps[:, 2 + x % 2, t], A[:, UU + h, t], W[:, 3 + x % 2, t], start=True, stop=True)
                    last = nc.tensor.matmul(K.ps[:, 4 + x % 2, t], W[:, 3 + x % 2, t], A[:, UU + h, t], start=True, stop=True)
                last.then_inc(s("inv_tlt").sem, s("inv_tlt").n())
    K.end_block("gdn_inverse")


def phase_gdn_tokens(K):
    nc, s = K.nc, K.s
    A, W = K.A, K.pair
    with nc.Block() as block:
        @block.tensor
        def _(pe):
            def turn(h):
                b = 3 * (h % 2)
                if h >= 2:
                    pe.wait_ge(s("tok_scaled").sem, s("tok_scaled").at(h - 1))
                for i in range(NT):
                    t = slice(P * i, P * i + P)
                    nc.tensor.transpose(K.ps[:, b, t], A[:, VV + h, t], K.mat("ident"))
                    last = nc.tensor.transpose(K.ps[:, b + 1, t], A[:, KK + h, t], K.mat("ident"))
                last.then_inc(s("tok_turned").sem, s("tok_turned").n())
            turn(0)
            for h in range(GDN_HEADS):
                if h + 1 < GDN_HEADS:
                    turn(h + 1)
                pe.wait_ge(s("tok_scaled").sem, s("tok_scaled").at(h + 1))
                if h >= 2:
                    pe.wait_ge(s("tok_w").sem, s("tok_w").at(h - 1))
                for i in range(NT):
                    t = slice(P * i, P * i + P)
                    last = nc.tensor.matmul(K.ps[:, 3 * (h % 2) + 2, t], W[:, h % 2, t], A[:, UU + h, t], start=True, stop=True)
                last.then_inc(s("tok_wt").sem, s("tok_wt").n())

        @block.vector
        def _(dve):
            for h in range(GDN_HEADS):
                b = 3 * (h % 2)
                dve.wait_ge(s("tok_turned").sem, s("tok_turned").at(h + 1))
                if h >= 2:
                    dve.wait_ge(s("tok_wt").sem, s("tok_wt").at(h - 1))
                nc.vector.tensor_tensor(tiles_of(A[:, VV + h, :]), tiles_of(K.ps[:, b, :]), per_token(K, BETA, h), ALU.mult)
                nc.vector.tensor_tensor(tiles_of(W[:, h % 2, :]), tiles_of(K.ps[:, b + 1, :]), per_token(K, BG, h), ALU.mult)
                nc.vector.tensor_tensor(tiles_of(A[:, MT + h, :]), tiles_of(K.ps[:, b + 1, :]), per_token(K, KD, h),
                                        ALU.mult).then_inc(s("tok_scaled").sem, s("tok_scaled").n())

        @block.scalar
        def _(act):
            for h in range(GDN_HEADS):
                act.wait_ge(s("tok_wt").sem, s("tok_wt").at(h + 1))
                nc.scalar.activation(A[:, KK + h, :], K.ps[:, 3 * (h % 2) + 2, :], ACT.Copy, scale=-1.0).then_inc(
                    s("tok_w").sem, s("tok_w").n())
    K.end_block("gdn_tokens")


def phase_gdn_scan(K):
    nc, s = K.nc, K.s
    A, W = K.A, K.pair
    state = A[:, TT:TT + 2, :].rearrange("p u (h n) -> p (u h) n", n=P)
    items = [(n, grp) for n in range(T // CHUNK) for grp in range(2)]
    with nc.Block() as block:
        @block.vector
        def _(dve):
            nc.vector.memset(A[:, TT:TT + 2, :], 0.0).then_inc(s("scan_zero").sem, s("scan_zero").n())
            dve.wait_ge(s("scan_zero").sem, s("scan_zero").at(1))
            for x, (n, grp) in enumerate(items):
                dve.wait_ge(s("scan_kv").sem, s("scan_kv").at(x + 1))
                for hh in range(4):
                    h = 4 * grp + hh
                    last = nc.vector.scalar_tensor_tensor(
                        state[:, h, :], state[:, h, :], K.small[:, EGL + 8 * h + n:EGL + 8 * h + n + 1],
                        K.ps[:, 4 + grp, P * hh:P * hh + P], ALU.mult, ALU.add)
                last.then_inc(s("scan_state").sem, s("scan_state").n())

        @block.scalar
        def _(act):
            for x, (n, grp) in enumerate(items):
                rows = slice(CHUNK * (n % 2), CHUNK * (n % 2) + CHUNK)
                act.wait_ge(s("scan_v").sem, s("scan_v").at(x + 1))
                nc.scalar.activation(W[rows, grp, :], K.ps[rows, grp, :], ACT.Copy).then_inc(s("scan_vc").sem, s("scan_vc").n())
                act.wait_ge(s("scan_kv").sem, s("scan_kv").at(x + 1))
                nc.scalar.activation(A[:, QQ + 4 * grp:QQ + 4 * grp + 4, CHUNK * n:CHUNK * n + CHUNK],
                                     K.ps[:, 2 + grp, 0:4 * CHUNK].rearrange("p (h c) -> p h c", c=CHUNK),
                                     ACT.Copy).then_inc(s("scan_o").sem, s("scan_o").n())

        @block.tensor
        def _(pe):
            pe.wait_ge(s("scan_zero").sem, s("scan_zero").at(1))

            def new_v(x):
                n, grp = items[x]
                i, rows, cols = n // 2, slice(CHUNK * (n % 2), CHUNK * (n % 2) + CHUNK), slice(CHUNK * n, CHUNK * n + CHUNK)
                if x >= 2:
                    pe.wait_ge(s("scan_state").sem, s("scan_state").at(x - 1))
                    pe.wait_ge(s("scan_vc").sem, s("scan_vc").at(x - 1))
                for hh in range(4):
                    h = 4 * grp + hh
                    out = K.ps[rows, grp, P * hh:P * hh + P]
                    nc.tensor.matmul(out, A[:, UU + h, cols], A[:, VV + h, P * i:P * i + P], start=True, stop=False)
                    last = nc.tensor.matmul(out, A[:, KK + h, cols], state[:, h, :], start=False, stop=True)
                last.then_inc(s("scan_v").sem, s("scan_v").n())
            new_v(0)
            for x, (n, grp) in enumerate(items):
                i, rows, cols = n // 2, slice(CHUNK * (n % 2), CHUNK * (n % 2) + CHUNK), slice(CHUNK * n, CHUNK * n + CHUNK)
                if x == 0:
                    new_v(1)
                pe.wait_ge(s("scan_vc").sem, s("scan_vc").at(x + 1))
                if x >= 2:
                    pe.wait_ge(s("scan_o").sem, s("scan_o").at(x - 1))
                for hh in range(4):
                    h = 4 * grp + hh
                    out = K.ps[:, 2 + grp, CHUNK * hh:CHUNK * hh + CHUNK]
                    nc.tensor.matmul(out, state[:, h, :], A[:, QQ + h, cols], start=True, stop=False)
                    nc.tensor.matmul(out, W[rows, grp, P * hh:P * hh + P], A[rows, AT + h, cols], start=False, stop=True)
                    last = nc.tensor.matmul(K.ps[:, 4 + grp, P * hh:P * hh + P], A[rows, MT + h, P * i:P * i + P],
                                            W[rows, grp, P * hh:P * hh + P], start=True, stop=True)
                last.then_inc(s("scan_kv").sem, s("scan_kv").n())
                if x >= 1 and x + 1 < len(items):
                    new_v(x + 1)
    K.end_block("gdn_scan")


def phase_gdn_out(K):
    nc, s = K.nc, K.s

    def load(sp):
        sp.dma_start(K.A[:, 8:16, :], K.dram["keep_gates"][8:16].rearrange("c p n -> p c n")).then_inc(
            s("reloaded").sem, s("reloaded").n(16))
        sp.dma_start(K.A[:, 16:24, :], K.dram["keep_yc"]).then_inc(s("reloaded").sem, s("reloaded").n(16))

    def dve(dve, t, g, slot):
        if t == 0:
            dve.wait_ge(s("reloaded").sem, s("reloaded").at(32))
        for j in range(2):
            c = 2 * t + j
            wait_bank(K, dve, g, j)
            nc.vector.tensor_tensor(K.A[:, 8 + c, :], K.A[:, 8 + c, :], K.ps[:, 2 * slot + j, :],
                                    ALU.mult).then_inc(*free_bank(K, j))
            dve.wait_ge(s(f"bank_free_{j}").sem, s(f"bank_free_{j}").at(t + 1))
            nc.vector.tensor_tensor(K.A[:, 8 + c, :], K.A[:, 8 + c, :], K.A[:, 16 + c, :], ALU.add).then_inc(
                s("y_ready").sem, s("y_ready").n())
    phase_stream(K, "gdn_out", "gdn_out", dve=dve, load=load, presplit=24)


def phase_residual(K, label, presplit, reload=True, alpha=ALPHA):
    nc, s = K.nc, K.s

    def load(sp):
        if reload:
            sp.dma_start(K.A[:, 0:8, :], K.dram["keep_x"]).then_inc(s("reloaded").sem, s("reloaded").n(16))

    def dve(dve, t, g, slot):
        if t == 0 and reload:
            dve.wait_ge(s("reloaded").sem, s("reloaded").at(16))
        for j in range(2):
            c = 2 * t + j
            wait_bank(K, dve, g, j)
            nc.vector.scalar_tensor_tensor(K.A[:, c, :], K.A[:, c, :], alpha, K.ps[:, 2 * slot + j, :], ALU.mult,
                                           ALU.add).then_inc(*free_bank(K, j))
    phase_stream(K, label, label, dve=dve, load=load, presplit=presplit)


def block1_mixers(K):
    phase_glu(K)
    phase_projections(K)
    phase_layer_norm(K, "conv_ln", 16, "conv_ln_g", "conv_ln_b", ACT.Silu)
    phase_conv_out(K)
    phase_gdn_gates(K)
    phase_head_norm(K, "gdn_l2", [(QQ + h, "ones", GDN_DK ** -0.5) for h in range(8)] + [(KK + h, "ones", 1.0) for h in range(8)], 0)
    phase_gdn_matrices(K)
    phase_gdn_inverse(K)
    phase_gdn_tokens(K)
    phase_gdn_scan(K)

    def reload_z(sp):
        sp.dma_start(K.A[:, 0:8, :], K.dram["keep_gates"][0:8].rearrange("c p n -> p c n")).then_inc(
            K.s("reloaded").sem, K.s("reloaded").n(16))
    phase_head_norm(K, "gdn_norm", [(QQ + h, "mean128", K.vec("gdn_norm"), h) for h in range(8)], 40, after=reload_z)
    phase_gdn_out(K)
    phase_residual(K, "mix_out", 8)
    phase_layer_norm(K, "ln2", 0, "ln2_g", "ln2_b", split=False)


def stream_pe_tokens(K, pe, names, n_tok=NT, t0=0):
    free = [K.s("bank_free_0"), K.s("bank_free_1")]
    done = [K.s("first_done"), K.s("tile_done")]

    def body(t, g, uses, slot, times):
        pe.wait_ge(K.s("lo_ready").sem, g + 1)
        whi = K.whi[:, slot, :, :].rearrange("p (j k) n -> p k j n", k=KC)
        wlo = K.wlo[:, slot, :, :].rearrange("p (j k) n -> p k j n", k=KC)
        for j in range(2):
            pe.wait_ge(free[j].sem, free[j].at(t + (t0 - 1)))
            for b in range(n_tok // 2):
                tok = slice(P * (n_tok // 2 * j + b), P * (n_tok // 2 * j + b) + P)
                out = K.ps[:, 2 * slot + j, 256 * b:256 * b + 256].rearrange("p (j n) -> p j n", n=P)
                for k in range(KC):
                    hi, lo = K.xhi[:, k, tok], K.xlo[:, k, tok]
                    K.nc.tensor.matmul(out, hi, whi[:, k], start=k == 0, stop=False)
                    K.nc.tensor.matmul(out, hi, wlo[:, k], start=False, stop=False)
                    last = K.nc.tensor.matmul(out, lo, whi[:, k], start=False, stop=k == KC - 1)
            last.then_inc(done[j].sem, 1)
    tile_loop(pe, names, body)


NMAX, SUMS, RSUM = 704, 708, 712


def phase_attention(K, label, heads, p_unit, pt_unit, load=None):
    nc, s = K.nc, K.s
    A = K.A
    groups = [(h, b) for h in range(len(heads)) for b in range(len(heads[h]["branches"]))]
    items = [(y, i) for y in range(len(groups)) for i in range(NT)]
    n = len(items)

    def br(y):
        h, b = groups[y]
        return heads[h]["branches"][b]

    def prob(x):
        return p_unit[0][:, p_unit[1] + x % 4, :]

    def turned(y, mt):
        return pt_unit[0][:, pt_unit[1] + 4 * (y % 2) + mt, :]

    def blocks(y, i):
        w = br(y)["width"](i)
        return [(m, min(P, w - P * m)) for m in range((w + P - 1) // P)]

    def out_bank(h, o):
        return 5 + (len(heads[h]["out"]) * h + o) % 3

    def col(at, x):
        return K.small[:, at + x % 4:at + x % 4 + 1]

    with nc.Block() as block:
        @block.sync
        def _(sp):
            if load:
                load(sp)

        @block.tensor
        def _(pe):
            def scores(x):
                y, i = items[x]
                w = br(y)["width"](i)
                if x >= 3:
                    pe.wait_ge(s("att_exp").sem, s("att_exp").at(x - 2))
                parts = br(y)["scores"](i)
                for p, (q, k) in enumerate(parts):
                    last = nc.tensor.matmul(K.ps[:, x % 3, :w], q, k[:, :w], start=p == 0, stop=p == len(parts) - 1)
                last.then_inc(s("att_scores").sem, s("att_scores").n())

            def turn(x):
                y, i = items[x]
                pe.wait_ge(s("att_prob").sem, s("att_prob").at(x + 1))
                if x >= 2:
                    pe.wait_ge(s("att_copied").sem, s("att_copied").at(x - 1))
                for m, w in blocks(y, i):
                    last = nc.tensor.transpose(K.ps[:w, 3 + x % 2, P * m:P * m + P], prob(x)[:, P * m:P * m + w], K.mat("ident"))
                last.then_inc(s("att_turned").sem, s("att_turned").n())

            def product(y):
                h, b = groups[y]
                head = heads[h]
                pe.wait_ge(s("att_copied").sem, s("att_copied").at(4 * y + 4))
                before = h - 1 if len(head["out"]) == 2 else h - 3
                if b == 0 and before >= 0:
                    pe.wait_ge(s("att_out").sem, s("att_out").at(before + 1))
                bl = blocks(y, NT - 1)
                for o, (rows, _) in enumerate(head["out"]):
                    for m, w in bl:
                        first = P * m if br(y)["causal"] else 0
                        last = nc.tensor.matmul(K.ps[rows, out_bank(h, o), first:], br(y)["v"](m, o), turned(y, m)[:w, first:],
                                                start=b == 0 and m == 0,
                                                stop=b == len(head["branches"]) - 1 and m == bl[-1][0])
                last.then_inc(s("att_pv").sem, s("att_pv").n())

            scores(0)
            scores(1)
            for x, (y, i) in enumerate(items):
                if x + 2 < n:
                    scores(x + 2)
                turn(x)
                if i == 0 and y >= 1:
                    product(y - 1)
            product(len(groups) - 1)

        @block.vector
        def _(dve):
            def before(x):
                y, i = items[x]
                w = br(y)["width"](i)
                dve.wait_ge(s("att_scores").sem, s("att_scores").at(x + 1))
                if br(y)["bias"]:
                    cols, bias = br(y)["bias"](i)
                    out = K.ps[:, x % 3, cols]
                    if len(bias.shape) == 3:
                        out = out.rearrange("p (r c) -> p r c", c=bias.shape[2])
                    nc.vector.tensor_tensor(out, out, bias, ALU.add).then_inc(s("att_bias").sem, s("att_bias").n())
                    dve.wait_ge(s("att_bias").sem, s("att_bias").base + s("att_bias").pending)
                nc.vector.tensor_reduce(col(NMAX, x), K.ps[:, x % 3, :w], AX.X, ALU.max, negate=True).then_inc(
                    s("att_max").sem, s("att_max").n())

            def after(x):
                y, i = items[x]
                w = br(y)["width"](i)
                step = s("att_dve")
                dve.wait_ge(s("att_exp").sem, s("att_exp").at(x + 1))
                nc.vector.reciprocal(col(RSUM, x), col(SUMS, x)).then_inc(step.sem, step.n())
                dve.wait_ge(step.sem, step.base + step.pending)
                if br(y)["gate"]:
                    nc.vector.tensor_tensor(col(RSUM, x), col(RSUM, x), br(y)["gate"](i), ALU.mult).then_inc(step.sem, step.n())
                    dve.wait_ge(step.sem, step.base + step.pending)
                if br(y)["mask"]:
                    last = nc.vector.scalar_tensor_tensor(prob(x)[:, :w], prob(x)[:, :w], col(RSUM, x), br(y)["mask"](i),
                                                          ALU.mult, ALU.mult)
                else:
                    last = nc.vector.tensor_scalar(prob(x)[:, :w], prob(x)[:, :w], col(RSUM, x), None, ALU.mult)
                last.then_inc(s("att_prob").sem, s("att_prob").n())

            def evacuate(y):
                h, b = groups[y]
                if b < len(heads[h]["branches"]) - 1:
                    return
                dve.wait_ge(s("att_pv").sem, s("att_pv").at(y + 1))
                for o, (rows, unit) in enumerate(heads[h]["out"]):
                    if "times" in heads[h]:
                        last = nc.vector.tensor_tensor(A[rows, unit, :], K.ps[rows, out_bank(h, o), :],
                                                       heads[h]["times"], ALU.mult)
                        continue
                    last = nc.vector.tensor_copy(A[rows, unit, :], K.ps[rows, out_bank(h, o), :])
                last.then_inc(s("att_out").sem, s("att_out").n())

            if load:
                dve.wait_ge(s("reloaded").sem, s("reloaded").at(16))
            before(0)
            before(1)
            for x, (y, i) in enumerate(items):
                after(x)
                if x + 2 < n:
                    before(x + 2)
                if i == 1 and y >= 1:
                    evacuate(y - 1)
            evacuate(len(groups) - 1)

        @block.scalar
        def _(act):
            def exponential(x):
                y, i = items[x]
                w = br(y)["width"](i)
                act.wait_ge(s("att_max").sem, s("att_max").at(x + 1))
                if x >= 4:
                    act.wait_ge(s("att_turned").sem, s("att_turned").at(x - 3))
                nc.scalar.activation(prob(x)[:, :w], K.ps[:, x % 3, :w], ACT.Exp, bias=col(NMAX, x),
                                     accum_out=col(SUMS, x)).then_inc(s("att_exp").sem, s("att_exp").n())

            def copy(x):
                y, i = items[x]
                bl = blocks(y, i)
                act.wait_ge(s("att_turned").sem, s("att_turned").at(x + 1))
                if i == 0 and y >= 2:
                    act.wait_ge(s("att_pv").sem, s("att_pv").at(y - 1))
                w = bl[-1][1]
                at = pt_unit[1] + 4 * (y % 2)
                nc.scalar.activation(pt_unit[0][:w, at:at + len(bl), P * i:P * i + P],
                                     K.ps[:w, 3 + x % 2, :P * len(bl)].rearrange("p (m c) -> p m c", c=P),
                                     ACT.Copy).then_inc(s("att_copied").sem, s("att_copied").n())
            exponential(0)
            exponential(1)
            for x in range(n):
                copy(x)
                if x + 2 < n:
                    exponential(x + 2)
    K.end_block(label)


def copy_evac(K, unit_of, scale=1.0, func=ACT.Copy, bias=None):
    def act(act, t, g, slot):
        for j in range(2):
            c = 2 * t + j
            unit, f, sc, b = unit_of(c)
            wait_bank(K, act, g, j)
            kw = {"bias": b} if b is not None else {}
            K.nc.scalar.activation(unit, K.ps[:, 2 * slot + j, :unit.shape[-1]], f, scale=sc, **kw).then_inc(*free_bank(K, j))
    return act


def block1_memory(K):
    nc, s = K.nc, K.s
    A = K.A
    with nc.Block() as block:
        @block.sync
        def _(sp):
            sp.dma_start(A[:, 8:16, 0:N_MEM], K.dram["mem_t"]).then_inc(s("reloaded").sem, s("reloaded").n(16))

        @block.vector
        def _(dve):
            dve.wait_ge(s("reloaded").sem, s("reloaded").at(16))
            split_chunks(K, dve, 8, width=N_MEM)
    K.end_block("mem")
    phase_stream(K, "xk", "xk", pe=lambda pe: stream_pe(K, pe, "xk", n=N_MEM),
                 act=copy_evac(K, lambda c: (A[:, 16 + c, :N_MEM], ACT.Copy, 1.0, None)))

    def take_v(act, t, g, slot):
        for j in range(2):
            wait_bank(K, act, g, j)
            nc.scalar.activation(A[:, 24 + 2 * j + t // 2, 256 * (t % 2):256 * (t % 2) + 256],
                                 K.ps[:, 2 * slot + j, :256], ACT.Copy).then_inc(*free_bank(K, j))
    phase_stream(K, "xv", "xv", pe=lambda pe: stream_pe_tokens(K, pe, "xv", 2), act=take_v)
    phase_stream(K, "xq", "xq", presplit=0, act=copy_evac(K, lambda c: (A[:, 32 + c, :], ACT.Copy, 1 / 16, None)))
    heads = []
    for h in range(XATTN_HEADS):
        heads.append({
            "out": [(slice(0, P), 40 + 2 * h), (slice(0, P), 41 + 2 * h)],
            "branches": [{
                "scores": lambda i, h=h: [(A[:, 32 + 2 * h + d, P * i:P * i + P], A[:, 16 + 2 * h + d, :]) for d in range(2)],
                "width": lambda i: N_MEM, "bias": None, "gate": None, "mask": None, "causal": False,
                "v": lambda m, o, h=h: A[:, 24 + 2 * m + h // 2, 256 * (h % 2) + P * o:256 * (h % 2) + P * o + P],
            }]})
    phase_attention(K, "xattn", heads, (A, 28), (A, 48))
    phase_residual(K, "xo", 40, reload=False)
    phase_layer_norm(K, "ln3", 0, "ln3_g", "ln3_b")


GATE = 0
W2K, W2V = 384, 512
HID, KCMP, VCMP = 768, 1024, 1056


def phase_rms(K, label, src, dst, n, matrix, gain, split=False):
    nc, s = K.nc, K.s
    sq = K.pair
    with nc.Block() as block:
        @block.scalar
        def _(act):
            for c in range(n):
                nc.scalar.activation(sq[:, c, :], K.A[:, src + c, :], ACT.Square).then_inc(s("squared").sem, s("squared").n())
            act.wait_ge(s("var_ready").sem, s("var_ready").at(1))
            nc.scalar.activation(sq[:, 9, :], K.ps[:, 5, :], ACT.Abs_reciprocal_sqrt,
                                 bias=K.eps(RMS_EPS)).then_inc(s("rstd_ready").sem, s("rstd_ready").n())

        @block.tensor
        def _(pe):
            for c in range(n):
                pe.wait_ge(s("squared").sem, s("squared").at(c + 1))
                last = nc.tensor.matmul(K.ps[:, 5, :], K.mat(matrix), sq[:, c, :], start=c == 0, stop=c == n - 1)
            last.then_inc(s("var_ready").sem, s("var_ready").n())

        @block.vector
        def _(dve):
            dve.wait_ge(s("rstd_ready").sem, s("rstd_ready").at(1))
            for c in range(n):
                nc.vector.scalar_tensor_tensor(K.A[:, dst + c, :], K.A[:, src + c, :], K.vec(gain, c), sq[:, 9, :],
                                               ALU.mult, ALU.mult).then_inc(s("scaled").sem, s("scaled").n())
            if split:
                dve.wait_ge(s("scaled").sem, s("scaled").at(n))
                split_chunks(K, dve, dst)
    K.end_block(label)


def phase_rope(K, label, chunks, matrix, cos, sin, load=None, rows=P):
    nc, s = K.nc, K.s
    A, W = K.A, K.pair
    with nc.Block() as block:
        @block.sync
        def _(sp):
            if load:
                load(sp)

        @block.tensor
        def _(pe):
            for x, c in enumerate(chunks):
                if x >= 2:
                    pe.wait_ge(s("rope_sin").sem, s("rope_sin").at(x - 1))
                nc.tensor.matmul(K.ps[:rows, x % 2, :], K.mat(matrix)[:rows, :rows], A[:rows, c, :], start=True, stop=True).then_inc(
                    s("rope_turned").sem, s("rope_turned").n())

        @block.vector
        def _(dve):
            if load:
                dve.wait_ge(s("reloaded").sem, s("reloaded").at(16))
            for x, c in enumerate(chunks):
                dve.wait_ge(s("rope_turned").sem, s("rope_turned").at(x + 1))
                nc.vector.tensor_tensor(W[:rows, 14 + x % 2, :], K.ps[:rows, x % 2, :], sin, ALU.mult).then_inc(
                    s("rope_sin").sem, s("rope_sin").n())
                nc.vector.tensor_tensor(A[:rows, c, :], A[:rows, c, :], cos, ALU.mult).then_inc(s("rope_cos").sem, s("rope_cos").n())
                dve.wait_ge(s("rope_sin").sem, s("rope_sin").at(x + 1))
                dve.wait_ge(s("rope_cos").sem, s("rope_cos").at(x + 1))
                nc.vector.tensor_tensor(A[:rows, c, :], A[:rows, c, :], W[:rows, 14 + x % 2, :], ALU.add)
    K.end_block(label)


def phase_in_2(K):
    nc, s = K.nc, K.s
    A = K.A
    names = ["rqk_2", "rv_2", "mid_2", "v_2"]

    def pe(pe):
        stream_pe(K, pe, "rqk_2")
        stream_pe_tokens(K, pe, "rv_2", t0=4)
        stream_pe(K, pe, "mid_2", t0=6)
        stream_pe_tokens(K, pe, "v_2", t0=14)
        for i in range(NT):
            for k in range(KC):
                last = nc.tensor.matmul(K.ps[:, 6, 24 * i:24 * i + 24], A[:, 8 + k, P * i:P * i + P],
                                        K.small[:, 128 + 24 * k:152 + 24 * k], start=k == 0, stop=k == KC - 1)
        last.then_inc(s("gl_ready").sem, s("gl_ready").n())

    def act(act, t, g, slot):
        for j in range(2):
            wait_bank(K, act, g, j)
            bank = K.ps[:, 2 * slot + j, :]
            func, scale = ACT.Copy, 1.0
            if t in (4, 5):
                out = A[:, 24 + 2 * j:26 + 2 * j, 256 * (t - 4):256 * (t - 4) + 256]
                bank = bank.rearrange("p (b n) -> p b n", n=256)
            elif t == 14:
                out = A[:, 44 + j, :]
            else:
                c = 2 * t + j
                out = A[:, 16 + c if t < 4 else 28 + c - 12, :]
                if t in (2, 3):
                    scale = HD ** -0.5
                if t in (6, 7, 10, 11):
                    func = ACT.Silu
            nc.scalar.activation(out, bank, func, scale=scale).then_inc(*free_bank(K, j))

    def dve(dve, t, g, slot):
        if t == 14:
            dve.wait_ge(s("gl_ready").sem, s("gl_ready").at(1))
            nc.vector.tensor_tensor(K.small[:, GATE:GATE + 96].rearrange("p (i c) -> p i c", c=24),
                                    K.ps[:, 6, 0:96].rearrange("p (i c) -> p i c", c=24),
                                    K.vec("b_gate_2", 0, 24).unsqueeze(1).broadcast_to([P, NT, 24]),
                                    ALU.add)
    phase_stream(K, "in_2", names, pe=pe, act=act, dve=dve)


def phase_compress(K, kind, w1):
    nc, s = K.nc, K.s
    A = K.A
    blocks = A[:, 46:48, :].rearrange("p a b -> p (a b)")[:, :CMP_BLOCK * N_CMP].rearrange("p (l n) -> p l n", n=N_CMP)
    src = A[:, 40 + kind, :]
    windows = bass.AP(tensor=src.tensor, offset=src.offset, ap=[src.ap[0], [1, CMP_BLOCK], [CMP_STRIDE, N_CMP]])
    pos = K.vec(("pos_k", "pos_v")[kind], 0, CMP_BLOCK).unsqueeze(2).broadcast_to([P, CMP_BLOCK, N_CMP])
    w2 = K.small[:, (W2K, W2V)[kind]:(W2K, W2V)[kind] + 128].rearrange("p (m d) -> p m d", d=HD)

    def hid(m, g):
        at = HID + 64 * m + 32 * g
        return K.small[:, at:at + N_CMP]
    with nc.Block() as block:
        @block.sync
        def _(sp):
            for part in range(2):
                sp.dma_start(w1(part), K.dram[("w1_k", "w1_v")[kind]][:, 16 * part:16 * part + 16, :]
                             .rearrange("p (u l) n -> p u (l n)", l=2)).then_inc(s("reloaded").sem, s("reloaded").n(16))
            if kind == 0:
                sp.dma_start(K.small[:, W2K:W2K + 256], K.dram["w2"]).then_inc(s("reloaded").sem, s("reloaded").n(16))

        @block.vector
        def _(dve):
            nc.vector.tensor_tensor(blocks, windows, pos, ALU.add).then_inc(s("cmp_blocks").sem, s("cmp_blocks").n())
            if kind == 0:
                dve.wait_ge(s("cmp_rstd").sem, s("cmp_rstd").at(1))
                nc.vector.scalar_tensor_tensor(K.small[:, KCMP:KCMP + N_CMP], K.ps[:, 1, 0:N_CMP], K.vec("k_cmp"),
                                               A[:, 46, 64:64 + N_CMP], ALU.mult, ALU.mult)
            else:
                dve.wait_ge(s("cmp_out").sem, s("cmp_out").at(1))
                nc.vector.tensor_copy(K.small[:N_CMP, VCMP:VCMP + 128], K.ps[:N_CMP, 1, 0:128])

        @block.scalar
        def _(act):
            if kind == 0:
                nc.scalar.activation(K.small[:, GATE:GATE + 96], K.small[:, GATE:GATE + 96], ACT.Sigmoid)
            act.wait_ge(s("cmp_hidden").sem, s("cmp_hidden").at(1))
            for m in range(2):
                for g in range(2):
                    last = nc.scalar.activation(hid(m, g), K.ps[:, 3 * g, 64 * m:64 * m + N_CMP], ACT.Silu)
            last.then_inc(s("cmp_silu").sem, s("cmp_silu").n())
            if kind == 0:
                act.wait_ge(s("cmp_out").sem, s("cmp_out").at(1))
                nc.scalar.activation(A[:, 46, 0:N_CMP], K.ps[:, 1, 0:N_CMP], ACT.Square).then_inc(s("cmp_sq").sem, s("cmp_sq").n())
                act.wait_ge(s("cmp_mean").sem, s("cmp_mean").at(1))
                nc.scalar.activation(A[:, 46, 64:64 + N_CMP], K.ps[:, 2, 0:N_CMP], ACT.Abs_reciprocal_sqrt,
                                     bias=K.eps(RMS_EPS)).then_inc(s("cmp_rstd").sem, s("cmp_rstd").n())

        @block.tensor
        def _(pe):
            pe.wait_ge(s("cmp_blocks").sem, s("cmp_blocks").at(1))
            pe.wait_ge(s("reloaded").sem, s("reloaded").at(48 if kind == 0 else 32))
            for m in range(2):
                for g in range(2):
                    rows = slice(HD * g, HD * g + HD)
                    for l in range(CMP_BLOCK):
                        w = w1(l // 16)[rows, (l % 16) // 2, 256 * (l % 2) + P * m:256 * (l % 2) + P * m + P]
                        last = nc.tensor.matmul(K.ps[:, 3 * g, 64 * m:64 * m + N_CMP], w, blocks[rows, l, :],
                                                start=l == 0, stop=l == CMP_BLOCK - 1)
            last.then_inc(s("cmp_hidden").sem, s("cmp_hidden").n())
            pe.wait_ge(s("cmp_silu").sem, s("cmp_silu").at(1))
            for g in range(2):
                for m in range(2):
                    if kind == 0:
                        last = nc.tensor.matmul(K.ps[HD * g:HD * g + HD, 1, 0:N_CMP], w2[:, m, :], hid(m, g),
                                                start=m == 0, stop=m == 1)
                    else:
                        last = nc.tensor.matmul(K.ps[:N_CMP, 1, HD * g:HD * g + HD], hid(m, g), w2[:, m, :],
                                                start=m == 0, stop=m == 1)
            last.then_inc(s("cmp_out").sem, s("cmp_out").n())
            if kind == 0:
                pe.wait_ge(s("cmp_sq").sem, s("cmp_sq").at(1))
                nc.tensor.matmul(K.ps[:, 2, 0:N_CMP], K.mat("mean64"), A[:, 46, 0:N_CMP], start=True, stop=True).then_inc(
                    s("cmp_mean").sem, s("cmp_mean").n())
    K.end_block(f"compress_{kind}")


def phase_retention(K):
    nc, s = K.nc, K.s
    A, W = K.A, K.pair
    items = [(h, i) for h in range(HEADS) for i in range(NT)]
    n = len(items)

    def place(h):
        return slice(HD * (h % 2), HD * (h % 2) + HD), h // 2
    with nc.Block() as block:
        @block.sync
        def _(sp):
            sp.dma_start(A[:, 48:56, :], K.dram["decay"]).then_inc(s("reloaded").sem, s("reloaded").n(16))

        @block.tensor
        def _(pe):
            def scores(x):
                h, i = items[x]
                rows, c = place(h)
                if x >= 2:
                    pe.wait_ge(s("ret_a").sem, s("ret_a").at(x - 1))
                nc.tensor.matmul(K.ps[:, x % 2, :T - P * i], A[rows, 20 + c, P * i:P * i + P], A[rows, 16 + c, P * i:],
                                 start=True, stop=True).then_inc(s("ret_scores").sem, s("ret_scores").n())
            scores(0)
            for x, (h, i) in enumerate(items):
                rows, c = place(h)
                if x + 1 < n:
                    scores(x + 1)
                pe.wait_ge(s("ret_a").sem, s("ret_a").at(x + 1))
                if i == 0 and h >= 2:
                    pe.wait_ge(s("ret_out").sem, s("ret_out").at(h - 1))
                nc.tensor.matmul(K.ps[rows, 2 + h % 2, P * i:], A[:, 24 + i, HD * h:HD * h + HD], W[:, x % 4, :T - P * i],
                                 start=i == 0, stop=i == NT - 1).then_inc(s("ret_o").sem, s("ret_o").n())

        @block.vector
        def _(dve):
            dve.wait_ge(s("reloaded").sem, s("reloaded").at(16))
            for x, (h, i) in enumerate(items):
                dve.wait_ge(s("ret_scores").sem, s("ret_scores").at(x + 1))
                if x >= 4:
                    dve.wait_ge(s("ret_o").sem, s("ret_o").at(x - 3))
                nc.vector.tensor_tensor(W[:, x % 4, :T - P * i], K.ps[:, x % 2, :T - P * i], A[:, 48 + h, :T - P * i],
                                        ALU.mult).then_inc(s("ret_a").sem, s("ret_a").n())

        @block.scalar
        def _(act):
            for h in range(HEADS):
                rows, c = place(h)
                act.wait_ge(s("ret_o").sem, s("ret_o").at(4 * h + 4))
                nc.scalar.activation(A[rows, 8 + c, :], K.ps[rows, 2 + h % 2, :], ACT.Copy).then_inc(s("ret_out").sem, s("ret_out").n())
    K.end_block("retention")


def block2(K):
    nc, s = K.nc, K.s
    A = K.A
    phase_rms(K, "norm_2", 0, 8, KC, "mean", "norm_2", split=True)
    phase_in_2(K)
    phase_compress(K, 0, lambda part: K.pair[:, 8 * part:8 * part + 8, :])
    phase_compress(K, 1, lambda part: A[:, 48:56, :] if part == 0 else A[:, 8:16, :])

    def tables(sp):
        sp.dma_start(A[:, 46:48, :], K.dram["rope_2"]).then_inc(s("reloaded").sem, s("reloaded").n(16))
    phase_rope(K, "rope_2", list(range(16, 24)), "rope64", A[:, 46, :], A[:, 47, :], tables)
    phase_retention(K)
    phase_head_norm(K, "norms_2", [(8 + c, "mean64", K.vec("ret_norm", c), 28 + c) for c in range(4)] +
                    [(32 + c, "chunk_ones", K.vec("q_norm_2")) for c in range(4)] +
                    [(42, "mean64", K.vec("k_slc")), (43, "mean64", K.vec("k_win"))], 48,
                    eps=lambda i: 64 * RMS_EPS if 4 <= i < 8 else RMS_EPS)
    masks = A[:, 46, :]

    def load(sp):
        sp.dma_start(masks[:, 0:384], K.dram["masks_2"]).then_inc(s("reloaded").sem, s("reloaded").n(16))

    def gate(b, h):
        return lambda i: K.small[:, GATE + 24 * i + 8 * b + h:GATE + 24 * i + 8 * b + h + 1]
    heads = []
    for c in range(4):
        for g in range(2):
            h, rows = c + 4 * g, slice(HD * g, HD * g + HD)

            def q(i, rows=rows, c=c):
                return A[rows, 32 + c, P * i:P * i + P]
            branches = [{
                "scores": lambda i, q=q, rows=rows: [(q(i), K.small[rows, KCMP:KCMP + N_CMP])],
                "width": lambda i: N_CMP, "causal": False, "gate": gate(0, h),
                "bias": lambda i: (slice(0, N_CMP), masks[:, 32 * i:32 * i + N_CMP]),
                "mask": lambda i: masks[:, 128 + 32 * i:128 + 32 * i + N_CMP],
                "v": lambda m, o, g=g: K.small[:N_CMP, VCMP + HD * g:VCMP + HD * g + HD],
            }]
            for b in (1, 2):
                branches.append({
                    "scores": lambda i, q=q, rows=rows, b=b: [(q(i), A[rows, 41 + b, :])],
                    "width": lambda i: P * (i + 1), "causal": True, "gate": gate(b, h), "mask": None,
                    "bias": lambda i: (slice(P * i, P * i + P), masks[:, 256:384]),
                    "v": lambda m, o, g=g, b=b: A[:, 44 + m // 2, 256 * (m % 2) + P * (b - 1) + HD * g:
                                                 256 * (m % 2) + P * (b - 1) + HD * g + HD],
                })
            heads.append({"out": [(rows, 12 + c)], "times": A[rows, 36 + c, :], "branches": branches})
    phase_attention(K, "nsa", heads, (A, 16), (A, 48), load)
    phase_residual(K, "out_2", 8, reload=False, alpha=1.0)


def phase_mla_in(K):
    nc, s = K.nc, K.s
    A, W = K.A, K.pair
    uq = W[:, 8:11, :].rearrange("p a b -> p (a b)").rearrange("p (k n) -> p k n", k=2)
    ukv = W[:, 11:13, :].rearrange("p a b -> p (a b)")
    with nc.Block() as block:
        @block.sync
        def _(sp):
            sp.dma_start(A[:, 52:54, :], K.dram["rope_3"]).then_inc(s("reloaded").sem, s("reloaded").n(16))

        @block.tensor
        def _(pe):
            for x in range(20):
                if x >= 4:
                    pe.wait_ge(s("mla_taken").sem, s("mla_taken").at(x - 3))
                if x < 8:
                    for k in range(2):
                        last = nc.tensor.matmul(K.ps[:MLA_QK, x % 4, :], uq[:, k, MLA_QK * x:MLA_QK * x + MLA_QK],
                                                A[:, 20 + k, :], start=k == 0, stop=k == 1)
                elif x < 16:
                    last = nc.tensor.matmul(K.ps[:HD, x % 4, :], ukv[:, HD * (x - 8):HD * (x - 7)], A[:, 22, :],
                                            start=True, stop=True)
                else:
                    last = nc.tensor.matmul(K.ps[:, x % 4, :], A[:, 22, P * (x - 16):P * (x - 15)], ukv[:, 512:],
                                            start=True, stop=True)
                last.then_inc(s("mla_ready").sem, s("mla_ready").n())

        @block.scalar
        def _(act):
            for x in range(20):
                act.wait_ge(s("mla_ready").sem, s("mla_ready").at(x + 1))
                rows, unit = (MLA_QK, 8 + x) if x < 8 else (HD, 44 + x - 8) if x < 16 else (P, x)
                nc.scalar.activation(A[:rows, unit, :], K.ps[:rows, x % 4, :], ACT.Copy,
                                     scale=MLA_QK ** -0.5 if x < 8 else 1.0).then_inc(s("mla_taken").sem, s("mla_taken").n())
            act.wait_ge(s("reloaded").sem, s("reloaded").at(16))
    K.end_block("mla_in")


def phase_branches_3(K):
    nc, s = K.nc, K.s
    A = K.A

    def pe(pe):
        for t in range(4):
            g = FIRST_TILE["branches_3"] + t
            slot = g % 2
            pe.wait_ge(K.s("lo_ready").sem, g + 1)
            if t >= 2:
                pe.wait_ge(s("branch_taken").sem, s("branch_taken").at(4 * (t - 1)))
            for m in range(4):
                for k in range(4):
                    c = 4 * (t // 2) + k
                    last = three_products(K, K.ps[:, 4 * (t % 2) + m, :], K.whi[:, slot, 4 * m + k, :],
                                          K.wlo[:, slot, 4 * m + k, :], K.xhi[:, c, :], K.xlo[:, c, :], k == 0, k == 3)
                if m in (1, 3):
                    last.then_inc(K.s(("first_done", "tile_done")[m // 2]).sem, 1)

    def dve(dve, t, g, slot):
        for m in range(4):
            wait_bank(K, dve, g, m // 2)
            c = 24 + 8 * (t // 2) + 4 * (t % 2) + m
            nc.vector.tensor_tensor(A[:, c, :], A[:, c, :], K.ps[:, 4 * (t % 2) + m, :], ALU.mult).then_inc(
                s("branch_taken").sem, s("branch_taken").n())
            if t >= 2:
                dve.wait_ge(s("branch_taken").sem, s("branch_taken").at(4 * t + m + 1))
                nc.vector.tensor_tensor(A[:, c - 8, :], A[:, c - 8, :], A[:, c, :], ALU.add)
    phase_stream(K, "branches_3", "branches_3", pe=pe, dve=dve, presplit=[40, 41, 42, 43, 8, 9, 10, 11])


def block3(K):
    nc, s = K.nc, K.s
    A = K.A
    names = ["qk_3", "v_3", "rest_3"]

    def pe(pe):
        stream_pe(K, pe, "qk_3")
        stream_pe_tokens(K, pe, "v_3", t0=4)
        stream_pe(K, pe, "rest_3", t0=6)

    def act(act, t, g, slot):
        for j in range(2):
            wait_bank(K, act, g, j)
            bank = K.ps[:, 2 * slot + j, :]
            c = 2 * t + j
            if t in (4, 5):
                out = A[:, 16 + 2 * j:18 + 2 * j, 256 * (t - 4):256 * (t - 4) + 256]
                nc.scalar.activation(out, bank.rearrange("p (b n) -> p b n", n=256), ACT.Copy).then_inc(*free_bank(K, j))
            elif t < 8:
                nc.scalar.activation(A[:, 8 + c, :], bank, ACT.Copy, scale=HD ** -0.5 if t < 2 else 1.0).then_inc(*free_bank(K, j))
            else:
                nc.scalar.activation(A[:, 8 + c, :], bank, ACT.Sigmoid, bias=K.vec("b_gate_3", c - 16)).then_inc(*free_bank(K, j))
    phase_stream(K, "in_3", names, pe=pe, act=act, presplit=0)

    def load(sp):
        sp.dma_start(A[:, 40:54, :], K.dram["na_bias"]).then_inc(s("reloaded").sem, s("reloaded").n(16))
    table = A[:, 40:54, :].rearrange("p a b -> p (a b)").rearrange("p (h j c) -> p h j c", h=HEADS, c=GRID_W)
    heads = []
    for h in range(HEADS):
        rows, c = slice(HD * (h % 2), HD * (h % 2) + HD), h // 2
        heads.append({"out": [(rows, 40 + c)], "branches": [{
            "scores": lambda i, rows=rows, c=c: [(A[rows, 8 + c, P * i:P * i + P], A[rows, 12 + c, :])],
            "width": lambda i: T, "causal": False, "gate": None, "mask": None,
            "bias": lambda i, h=h: (slice(0, T), table[:, h, 6 - 2 * i:14 - 2 * i, :]),
            "v": lambda m, o, h=h: A[:, 16 + m, HD * h:HD * h + HD],
        }]})
    phase_attention(K, "na", heads, (K.pair, 8), (K.pair, 0), load)

    phase_rms(K, "mla_q_norm", 20, 20, 2, "mean256", "mla_q")
    phase_rms(K, "mla_kv_norm", 22, 22, 1, "mean128", "mla_kv")
    with nc.Block() as block:
        @block.sync
        def _(sp):
            sp.dma_start(K.pair[:, 8:13, :], K.dram["mla_w"]).then_inc(s("reloaded").sem, s("reloaded").n(16))
            sp.wait_ge(s("reloaded").sem, s("reloaded").at(16))
    K.end_block("mla_w")
    phase_mla_in(K)
    phase_rope(K, "rope_3", list(range(8, 16)) + [23], "rope32", A[:MLA_QK, 52, :], A[:MLA_QK, 53, :], rows=MLA_QK)
    with nc.Block() as block:
        @block.vector
        def _(dve):
            for h in range(HEADS):
                nc.vector.tensor_copy(A[HD:MLA_QK, 44 + h, :], A[HD:MLA_QK, 23, :])
    K.end_block("mla_k")
    heads = []
    for h in range(HEADS):
        rows, c = slice(HD * (h % 2), HD * (h % 2) + HD), h // 2
        heads.append({"out": [(rows, 8 + c)], "branches": [{
            "scores": lambda i, h=h: [(A[:MLA_QK, 8 + h, P * i:P * i + P], A[:MLA_QK, 44 + h, :])],
            "width": lambda i: T, "causal": False, "gate": None, "mask": None, "bias": None,
            "v": lambda m, o, h=h: A[:, 16 + m, HD * h:HD * h + HD],
        }]})
    phase_attention(K, "mla", heads, (K.pair, 8), (K.pair, 0))
    phase_branches_3(K)
    phase_residual(K, "out_3", 24, reload=False)
    phase_layer_norm(K, "ln1_3", 0, "ln1_g_3", "ln1_b_3")
    phase_ffn_in(K, "ffn3_in", 1.0)
    phase_ffn_out(K, "ffn3_out")
    phase_layer_norm(K, "ln2_3", 0, "ln2_g_3", "ln2_b_3", split=False)


def program(nc, dram):
    ctx = ExitStack()
    with ctx:
        K = Kernel(nc, ctx, dram)
        try:
            phase_start(K)
            phase_ffn_in(K, "ffn1_in")
            phase_ffn_out(K, "ffn1_out")
            phase_layer_norm(K, "ln1", 0, "ln1_g", "ln1_b")
            block1_mixers(K)
            block1_memory(K)
            phase_ffn_in(K, "ffn2_in")
            phase_ffn_out(K, "ffn2_out")
            phase_layer_norm(K, "ln4", 0, "ln4_g", "ln4_b", split=False)
            block2(K)
            block3(K)
        except StopIteration:
            pass
        with nc.Block() as block:
            @block.sync
            def _(sp):
                sp.dma_start(dram["out"], K.A[:, 0:8, :]).then_inc(K.s("stored").sem, 16)
                if "dbg" in dram:
                    sp.dma_start(dram["dbg"], K.A[:, DBG[0]:DBG[1], :]).then_inc(K.s("stored").sem, 16)
                    sp.wait_ge(K.s("stored").sem, 32)
                else:
                    sp.wait_ge(K.s("stored").sem, 16)



def columns(w):
    k, m = w.shape
    return w.reshape(k // P, P, m // (2 * P), 2, P).transpose(2, 1, 3, 0, 4).reshape(-1, P, 16, P)


def pairs(wa, wb):
    k, m = wa.shape
    both = np.stack([w.reshape(k // P, P, m // P, P) for w in (wa, wb)])
    return both.transpose(3, 2, 0, 1, 4).reshape(-1, P, 16, P)


def rows(w):
    k, m = w.shape
    return w.reshape(k // (2 * P), 2, P, KC, P).transpose(0, 2, 1, 3, 4).reshape(-1, P, 16, P)


def halves(w):
    return w.reshape(4, P, 2, 4, P).transpose(2, 1, 3, 0, 4).reshape(-1, P, 16, P)


NSA_ORDER = np.concatenate([np.arange(HD * h, HD * h + HD) for c in range(4) for h in (c, c + 4)])
ORDER_2 = np.concatenate([np.arange(0, 2048), 2048 + NSA_ORDER, 2560 + NSA_ORDER, np.arange(3072, 3328),
                          np.arange(3328, 3456), np.arange(3584, 3712), np.arange(3456, 3584), np.arange(3712, 3840)])
ROWS_OUT_2 = np.concatenate([np.arange(0, 512), 512 + NSA_ORDER])


def rope_table(position, half):
    f, t = np.arange(P), np.arange(T)
    inv = 10000.0 ** (-(f % half).astype(np.float64) / half)
    angle = position(f[:, None], t[None, :]) * inv[:, None]
    return np.stack([np.cos(angle), np.sin(angle)], axis=1).astype(np.float32)


def tables():
    t = np.arange(T)
    decay = np.zeros((P, HEADS, T))
    p, x = np.arange(P)[:, None], t[None, :]
    for h in range(HEADS):
        decay[:, h, :] = np.where(x >= p, (1.0 - 2.0 ** (-5.0 - h)) ** np.maximum(x - p, 0).astype(np.float64), 0.0)
    masks = np.zeros((P, 384), np.float32)
    end = np.arange(N_CMP) * CMP_STRIDE + CMP_BLOCK - 1
    for i in range(NT):
        ok = end[None, :] <= (P * i + np.arange(P))[:, None]
        masks[:, 32 * i:32 * i + N_CMP] = np.where(ok, 0.0, NEG)
        masks[:, 128 + 32 * i:128 + 32 * i + N_CMP] = ok
    masks[:, 256:384] = np.where(np.arange(P)[None, :] <= np.arange(P)[:, None], 0.0, NEG)
    return {
        "rope_2": rope_table(lambda f, t: t + 0 * f, HD // 2),
        "rope_3": rope_table(lambda f, t: np.where(f < HD, 0, np.where(f // 16 % 2 == 0, t // GRID_W, t % GRID_W)), 8),
        "decay": decay.astype(np.float32), "masks_2": masks,
    }


def na_table(rpb):
    q, j, c = np.arange(P)[:, None, None], np.arange(1, 15)[None, :, None], np.arange(GRID_W)[None, None, :]
    row, col = q // GRID_W, q % GRID_W
    start = np.clip(col - NA_WIN_COLS // 2, 0, GRID_W - NA_WIN_COLS)
    inside = (c >= start) & (c < start + NA_WIN_COLS)
    taken = rpb[:, np.broadcast_to(j - row, (P, 14, GRID_W)), np.clip(c - col + NA_WIN_COLS - 1, 0, 30) + 0 * j]
    return np.where(inside[None], taken, np.float32(NEG)).transpose(1, 0, 2, 3).reshape(P, 14, T)


def per_feature(v):
    return v.reshape(-1, P).T


def feature_major(x):
    return x.T.reshape(-1, P, x.shape[0]).transpose(1, 0, 2)


def matrices():
    m = np.zeros((len(MATRICES), P, P), np.float32)
    i, j = np.meshgrid(np.arange(P), np.arange(P), indexing="ij")
    same = i // CHUNK == j // CHUNK
    m[MAT["ident"]] = i == j
    m[MAT["mean"]] = 1.0 / D
    m[MAT["ones"]] = 1.0
    m[MAT["mean128"]] = 1.0 / P
    m[MAT["mean256"]] = 1.0 / 256
    m[MAT["mean64"]] = (i // HD == j // HD) / HD
    m[MAT["chunk_tri"]] = same & (i <= j)
    m[MAT["chunk_strict"]] = same & (i < j)
    m[MAT["chunk_ones"]] = same
    for s in (1, 2, 4, 8, 16, 32):
        m[MAT[f"level{s}"]] = (i // (2 * s) == j // (2 * s)) & (i // s % 2 == 0) & (j // s % 2 == 1)
    for name, half, off, group in (("rope64", 32, 0, 64), ("rope32", 8, 0, 16)):
        r = np.zeros((P, P), np.float32)
        for o in range(P):
            w = o % group
            if w < half:
                r[o + half, o] = -1.0
            else:
                r[o - half, o] = 1.0
        m[MAT[name]] = r
    return m.transpose(1, 0, 2)


def kernel(**inputs):
    import concourse.bacc as bacc
    from concourse.bass_utils import run_bass_kernel_spmd as run

    w = {k: np.asarray(v)[0] if k != "mem" else np.asarray(v) for k, v in inputs.items()}
    win = w["w_in"]
    in_3 = w["w_in_3"]
    in_3 = np.concatenate([in_3[:, :1920]] + 4 * [in_3[:, 1920:1952]] + [in_3[:, 1952:]], axis=1)
    tiles = [
        pairs(w["ffn1_wg"], w["ffn1_wu"]), rows(w["ffn1_wd"]),
        pairs(win[:, 4112:5136], win[:, 5136:6160]), columns(win[:, 0:3072]), columns(win[:, 3072:4096]),
        columns(win[:, 6160:8208]), columns(w["w_conv_out"]), columns(w["w_gdn_out"]), columns(w["w_mix_out"]),
        columns(w["w_xkv"]), columns(w["w_xq"]), columns(w["w_xo"]),
        pairs(w["ffn2_wg"], w["ffn2_wu"]), rows(w["ffn2_wd"]),
        columns(w["w_in_2"][:, :3840][:, ORDER_2]), columns(w["w_out_2"][ROWS_OUT_2]),
        columns(in_3), halves(w["w_branch_na_3"]), halves(w["w_branch_mla_3"]), columns(w["w_out_3"]),
        pairs(w["w_ffn_in_3"][:, :DFF], w["w_ffn_in_3"][:, DFF:]), rows(w["w_ffn_out_3"]),
    ]
    stream = np.concatenate(tiles)
    parts = {}
    for n in ("ln1", "ln2", "ln3", "ln4"):
        parts[n + "_g"], parts[n + "_b"] = per_feature(w[n + "_g"]), per_feature(w[n + "_b"])
    parts["gdn_conv"] = w["gdn_conv_qkv"].reshape(4, 24, P).transpose(2, 1, 0).reshape(P, 96)
    parts["gdn_norm"] = per_feature(w["gdn_norm_g"])
    parts["conv_w"] = w["conv_dw_w"].reshape(31, 8, P).transpose(2, 0, 1).reshape(P, 248)
    for n, source in (("conv_b", "conv_dw_b"), ("conv_ln_g", "conv_ln_g"), ("conv_ln_b", "conv_ln_b"),
                      ("b_conv_out", "b_conv_out")):
        parts[n] = per_feature(w[source])
    for n, source in (("a_log", "gdn_a_log"), ("dt_bias", "gdn_dt_bias"), ("b_gate_2", "b_gate_2")):
        parts[n] = np.broadcast_to(w[source], (P, w[source].size))
    parts["eps"] = np.broadcast_to(np.array([LN_EPS, RMS_EPS, 1.0, 64 * RMS_EPS], np.float32), (P, 4))
    small = np.concatenate([
        win[:, 4096:4112].reshape(KC, P, 16).transpose(1, 0, 2).reshape(P, 128),
        w["w_in_2"][:, 3840:3864].reshape(KC, P, 24).transpose(1, 0, 2).reshape(P, 192)], axis=1)
    parts["norm_2"] = per_feature(w["norm_w_2"])
    parts["ret_norm"] = per_feature(w["ret_norm_w_2"])
    for n, source in (("q_norm_2", "q_norm_w_2"), ("k_cmp", "k_norm_cmp_2"), ("k_slc", "k_norm_slc_2"), ("k_win", "k_norm_win_2")):
        parts[n] = per_feature(np.tile(w[source], 2))
    parts["pos_k"], parts["pos_v"] = np.tile(w["cmp_pos_k_2"].T, (2, 1)), np.tile(w["cmp_pos_v_2"].T, (2, 1))
    parts["b_gate_3"] = per_feature(w["b_gate_3"])
    parts["mla_q"], parts["mla_kv"] = per_feature(w["mla_q_norm_3"]), per_feature(w["mla_kv_norm_3"])
    for n in ("ln1_g_3", "ln1_b_3", "ln2_g_3", "ln2_b_3"):
        parts[n] = per_feature(w[n])
    vecs = np.concatenate([parts[n] for n, k in VECTORS], axis=1)
    uq = w["mla_w_uq_3"]
    ukv = w["mla_w_ukv_3"].reshape(P, HEADS, 2, HD).transpose(0, 2, 1, 3).reshape(P, 1024)
    mla_w = np.concatenate([uq.reshape(2, P, 768).transpose(1, 0, 2).reshape(P, 1536), ukv], axis=1).reshape(P, 5, T)
    more = tables()
    for n in ("k", "v"):
        more["w1_" + n] = np.tile(w[f"cmp_w1_{n}_2"].reshape(CMP_BLOCK, HD, CMP_HIDDEN).transpose(1, 0, 2), (2, 1, 1))
    more["w2"] = np.concatenate([w[f"cmp_w2_{n}_2"].reshape(2, P, HD).transpose(1, 0, 2).reshape(P, P) for n in ("k", "v")], axis=1)
    more["mla_w"], more["na_bias"] = mla_w, na_table(w["na_rpb_3"])
    arrays = {
        **more, "x_t": feature_major(w["x"]), "stream": stream, "vecs": vecs, "mats": matrices(), "small": small, "mem_t": feature_major(w["mem"][0]),
    }
    nc = bacc.Bacc("TRN2", target_bir_lowering=False, num_devices=1)
    arrays = {k: np.ascontiguousarray(v) for k, v in arrays.items()}
    dram = {k: nc.dram_tensor("in_" + k, v.shape, F32, kind="ExternalInput").ap() for k, v in arrays.items()}
    dram["out"] = nc.dram_tensor("out_t", (P, KC, T), F32, kind="ExternalOutput").ap()
    if STOP_AFTER:
        dram["dbg"] = nc.dram_tensor("dbg", (P, DBG[1] - DBG[0], T), F32, kind="ExternalOutput").ap()
    dram["keep_x"] = nc.dram_tensor("keep_x", (P, KC, T), F32, kind="Internal").ap()
    dram["keep_yc"] = nc.dram_tensor("keep_yc", (P, KC, T), F32, kind="Internal").ap()
    dram["keep_gates"] = nc.dram_tensor("keep_gates", (24, P, T), F32, kind="Internal").ap()
    program(nc, dram)
    r = run(nc, [{"in_" + k: v for k, v in arrays.items()}], core_ids=[0])
    y = np.asarray(r.results[0]["out_t"])
    return y.transpose(2, 1, 0).reshape(1, T, D)
```

```python
from contextlib import ExitStack

import numpy as np

import concourse.bass as bass
from concourse import mybir

F32 = mybir.dt.float32
F32R = mybir.dt.float32r
ACT = mybir.ActivationFunctionType
ALU = mybir.AluOpType
AX = mybir.AxisListType

P = 128
T = 512
D = 1024
KC = D // P
NT = T // P
DFF = 2816
FC = DFF // P
N_MEM = 256
ALPHA = 2.0 ** 0.25
LN_EPS = 1e-5
RMS_EPS = 1e-6
NEG = -1e30

GDN_HEADS = 8
GDN_DK = 128
CHUNK = 64
SHORT_CONV = 4
CONV_WIDTH = 31
XATTN_HEADS = 4

HEADS = 8
HD = 64
CMP_BLOCK = 32
CMP_STRIDE = 16
N_CMP = (T - CMP_BLOCK) // CMP_STRIDE + 1
CMP_HIDDEN = 256
GRID_W = 64
NA_ROWS = T // GRID_W
NA_WIN_ROWS = 8
NA_WIN_COLS = 16
MLA_QK = 96

STREAM = [
    ("ffn1_in", 22), ("ffn1_out", 11),
    ("glu", 8), ("qkv", 12), ("z", 4), ("gates", 8), ("conv_out", 4), ("gdn_out", 4), ("mix_out", 4),
    ("xk", 4), ("xv", 4), ("xq", 4), ("xo", 4),
    ("ffn2_in", 22), ("ffn2_out", 11),
    ("rqk_2", 4), ("rv_2", 2), ("mid_2", 8), ("v_2", 1), ("out_2", 4),
    ("qk_3", 4), ("v_3", 2), ("rest_3", 10), ("branches_3", 4), ("out_3", 4),
    ("ffn3_in", 22), ("ffn3_out", 11),
]
FIRST_TILE, TILES = {}, {}
N_TILES = 0
for _name, _n in STREAM:
    FIRST_TILE[_name], TILES[_name] = N_TILES, _n
    N_TILES += _n

VECTORS = [
    ("ln1_g", 8), ("ln1_b", 8), ("ln2_g", 8), ("ln2_b", 8), ("ln3_g", 8), ("ln3_b", 8), ("ln4_g", 8), ("ln4_b", 8),
    ("gdn_conv", 4 * 24), ("gdn_norm", 1), ("conv_w", 31 * 8), ("conv_b", 8), ("conv_ln_g", 8), ("conv_ln_b", 8),
    ("b_conv_out", 8),
    ("norm_2", 8), ("ret_norm", 4), ("q_norm_2", 1), ("k_cmp", 1), ("k_slc", 1), ("k_win", 1),
    ("pos_k", 32), ("pos_v", 32),
    ("b_gate_3", 16), ("mla_q", 2), ("mla_kv", 1), ("ln1_g_3", 8), ("ln1_b_3", 8), ("ln2_g_3", 8), ("ln2_b_3", 8),
    ("a_log", 8), ("dt_bias", 8), ("b_gate_2", 24), ("eps", 4),
]
VEC, N_VEC = {}, 0
for _name, _n in VECTORS:
    VEC[_name] = N_VEC
    N_VEC += _n

MATRICES = ["ident", "mean", "ones", "mean128", "mean64", "chunk_tri", "chunk_strict", "chunk_ones",
            "level1", "level2", "level4", "level8", "level16", "level32", "rope64", "rope32", "mean256"]
MAT = {n: i for i, n in enumerate(MATRICES)}

STOP_AFTER = None
DBG = (0, 8)


class Signal:

    def __init__(self, sem):
        self.sem, self.base, self.pending, self.times = sem, 0, 0, 1

    def at(self, n):
        return n + self.base

    def n(self, by=1, times=1):
        self.pending += by * times
        return by


class Kernel:
    def __init__(self, nc, ctx, dram):
        self.nc, self.dram = nc, dram
        self.signals = {}
        self.ctx = ctx
        at = (nc.sbuf_base + 63) // 64 * 64

        def place(name, shape, dt, offset):
            return nc.alloc_sbuf_tensor_at(name, shape, dt, offset=offset)

        tile = 16 * P * 4
        self.raw = place("weights_raw", [P, 2, 16, P], F32, at)
        self.whi = place("weights_hi", [P, 2, 16, P], F32R, at + 2 * tile)
        self.wlo = place("weights_lo", [P, 2, 16, P], F32R, at + 4 * tile)
        at += 6 * tile
        self.xhi = place("x_hi", [P, KC, T], F32R, at)
        self.xlo = place("x_lo", [P, KC, T], F32R, at + KC * T * 4)
        self.pair = place("pair_scratch", [P, 2 * KC, T], F32, at)
        at += 2 * KC * T * 4
        self.A = place("arena", [P, 56, T], F32, at)
        self.hhi = place("h_hi", [P, FC, T], F32R, at + 8 * T * 4)
        self.hlo = place("h_lo", [P, FC, T], F32R, at + (8 + FC) * T * 4)
        at += 56 * T * 4
        self.mats = place("mats", [P, len(MATRICES), P], F32, at)
        at += len(MATRICES) * P * 4
        self.vecs = place("vecs", [P, N_VEC], F32, at)
        at += (N_VEC * 4 + 31) // 32 * 32
        self.small = place("small", [P, 1184], F32, at)
        at += 1184 * 4
        assert at <= nc.sbuf_usable_end
        self.ps = nc.alloc_psum_tensor("psum", [P, 8, 512], F32)

    def s(self, name):
        if name not in self.signals:
            self.signals[name] = Signal(self.nc.alloc_semaphore(name))
        return self.signals[name]

    def eps(self, value):
        return self.vec("eps", {LN_EPS: 0, RMS_EPS: 1, 1.0: 2, 64 * RMS_EPS: 3}[value])

    def mat(self, name):
        return self.mats[:, MAT[name], :]

    def vec(self, name, c=0, n=1):
        return self.vecs[:, VEC[name] + c:VEC[name] + c + n]

    def end_block(self, name):
        for s in self.signals.values():
            s.base += s.pending
            s.pending = 0
        if name == STOP_AFTER:
            raise StopIteration(name)


def span(names):
    names = [names] if isinstance(names, str) else names
    return FIRST_TILE[names[0]], sum(TILES[n] for n in names)


def tile_loop(eng, names, body, unroll=False, peeled=0):
    first, n = span(names)
    pairs = (n - peeled - 2) // 2
    done = peeled
    if pairs >= 2 and not unroll:
        with eng.Fori(0, pairs) as i:
            for j in range(2):
                g = first + peeled + j
                body(2 * i + (peeled + j), 2 * i + g, i + (g // 2 + 1), g % 2, pairs)
        done += 2 * pairs
    for t in range(done, n):
        g = first + t
        body(t, g, g // 2 + 1, g % 2, 1)



def stream_load(K, sp, name):
    raw_loaded, lo_ready = [K.s("raw_loaded_0"), K.s("raw_loaded_1")], K.s("lo_ready")

    def body(t, g, uses, slot, times):
        if isinstance(g, int) and g + 2 >= N_TILES:
            return
        sp.wait_ge(lo_ready.sem, g + 1)
        sp.dma_start(K.raw[:, slot, :, :], K.dram["stream"][bass.ds(g + 2, 1) if not isinstance(g, int)
                                                           else slice(g + 2, g + 3)].rearrange(
            "a p k n -> (a p) k n")).then_inc(raw_loaded[slot].sem, 16)
    tile_loop(sp, name, body)


def split_hi(K, act, g, uses, slot, times):
    if isinstance(g, int) and g >= N_TILES:
        return
    act.wait_ge(K.s(f"raw_loaded_{slot}").sem, uses * 16)
    if not isinstance(g, int) or g >= 2:
        act.wait_ge(K.s("tile_done").sem, g - 1)
    K.nc.scalar.activation(K.whi[:, slot, :, :], K.raw[:, slot, :, :], ACT.Copy).then_inc(K.s("hi_ready").sem, 1)


def stream_split_lo(K, pool, name):
    def body(t, g, uses, slot, times):
        if isinstance(g, int) and g + 1 >= N_TILES:
            return
        pool.wait_ge(K.s("hi_ready").sem, g + 2)
        K.nc.gpsimd.tensor_tensor(K.wlo[:, 1 - slot, :, :], K.raw[:, 1 - slot, :, :],
                                  K.whi[:, 1 - slot, :, :].bitcast(F32),
                                  ALU.subtract).then_inc(K.s("lo_ready").sem, 1)
    tile_loop(pool, name, body)


def stream_act(K, act, name, evac=None, unroll=False):
    def body(t, g, uses, slot, times):
        split_hi(K, act, g + 1, uses + slot, 1 - slot, times)
        if evac:
            evac(t, g, slot, times)
    tile_loop(act, name, body, unroll)


def stream_dve(K, dve, name, evac, unroll=False):
    tile_loop(dve, name, lambda t, g, uses, slot, times: evac(t, g, slot, times), unroll)


def three_products(K, out, whi, wlo, xhi, xlo, start, stop):
    K.nc.tensor.matmul(out, whi, xhi, start=start, stop=False)
    K.nc.tensor.matmul(out, whi, xlo, start=False, stop=False)
    return K.nc.tensor.matmul(out, wlo, xhi, start=False, stop=stop)


def stream_pe(K, pe, name, n=T, t0=0, split=False):
    xhi, xlo = K.xhi, K.xlo
    free = [K.s("bank_free_0"), K.s("bank_free_1")]
    done = [K.s("first_done"), K.s("tile_done")]

    def body(t, g, uses, slot, times):
        pe.wait_ge(K.s("lo_ready").sem, g + 1)
        for j in range(2):
            pe.wait_ge(free[j].sem, free[j].at(t + (t0 - 1)))
            for k in range(KC):
                last = three_products(K, K.ps[:, 2 * slot + j, :n], K.whi[:, slot, 8 * j + k, :],
                                      K.wlo[:, slot, 8 * j + k, :], xhi[:, k, :n], xlo[:, k, :n],
                                      k == 0, k == KC - 1)
            last.then_inc(done[j].sem, 1)

    if split:
        g = span(name)[0]
        slot = g % 2
        pe.wait_ge(K.s("lo_ready").sem, g + 1)
        for j in range(2):
            pe.wait_ge(free[j].sem, free[j].at(t0 - 1))
        for k in range(KC):
            pe.wait_ge(K.s("x_split").sem, K.s("x_split").at(k + 1))
            for j in range(2):
                last = three_products(K, K.ps[:, 2 * slot + j, :n], K.whi[:, slot, 8 * j + k, :],
                                      K.wlo[:, slot, 8 * j + k, :], xhi[:, k, :n], xlo[:, k, :n],
                                      k == 0, k == KC - 1)
                if k == KC - 1:
                    last.then_inc(done[j].sem, 1)
    tile_loop(pe, name, body, peeled=int(split))


def wait_bank(K, eng, g, j):
    eng.wait_ge(K.s(("first_done", "tile_done")[j]).sem, g + 1)



def phase_start(K):
    nc, dram = K.nc, K.dram
    with nc.Block() as block:
        @block.sync
        def _(sp):
            for i in range(2):
                sp.dma_start(K.raw[:, i, :, :], dram["stream"][i]).then_inc(K.s(f"raw_loaded_{i}").sem, 16)
            sp.dma_start(K.A[:, 0:8, :], dram["x_t"]).then_inc(K.s("x_in").sem, 16)
            sp.dma_start(K.vecs[:, :], dram["vecs"]).then_inc(K.s("loaded").sem, K.s("loaded").n(16))
            sp.dma_start(K.mats[:, :, :], dram["mats"]).then_inc(K.s("loaded").sem, K.s("loaded").n(16))
            sp.dma_start(K.small[:, 0:320], dram["small"]).then_inc(K.s("loaded").sem, K.s("loaded").n(16))
            sp.wait_ge(K.s("loaded").sem, 48)

        @block.scalar
        def _(act):
            split_hi(K, act, 0, 1, 0, 1)
            nc.scalar.nop().then_inc(K.s("bank_free_0").sem, K.s("bank_free_0").n(2))

        @block.gpsimd
        def _(pool):
            pool.wait_ge(K.s("hi_ready").sem, 1)
            nc.gpsimd.tensor_tensor(K.wlo[:, 0, :, :], K.raw[:, 0, :, :], K.whi[:, 0, :, :].bitcast(F32),
                                    ALU.subtract).then_inc(K.s("lo_ready").sem, 1)

        @block.vector
        def _(dve):
            nc.vector.nop().then_inc(K.s("bank_free_1").sem, K.s("bank_free_1").n(2))
            dve.wait_ge(K.s("x_in").sem, 16)
            split_chunks(K, dve, 0)
    K.end_block("start")


def split_chunks(K, dve, unit, n=KC, width=T):
    s = K.s("x_hi_done")
    units = unit if isinstance(unit, list) else [unit + c for c in range(n)]
    for c in range(n + 1):
        if c < n:
            K.nc.vector.tensor_copy(K.xhi[:, c, :width], K.A[:, units[c], :width]).then_inc(s.sem, s.n())
        if c == 0:
            continue
        c -= 1
        dve.wait_ge(s.sem, s.at(c + 1))
        K.nc.vector.tensor_tensor(K.xlo[:, c, :width], K.A[:, units[c], :width],
                                  K.xhi[:, c, :width].bitcast(F32), ALU.subtract).then_inc(
            K.s("x_split").sem, K.s("x_split").n())


def phase_ffn_in(K, name, weight=0.5, norm=None):
    nc = K.nc
    silu, h_ready, hhi_ready = K.s("silu_ready"), K.s("h_ready"), K.s("h_hi_ready")
    sg, h = K.A[:, 52:54, :], K.A[:, 54:56, :]
    with nc.Block() as block:
        @block.sync
        def _(sp):
            stream_load(K, sp, name)

        @block.gpsimd
        def _(pool):
            stream_split_lo(K, pool, name)

        @block.tensor
        def _(pe):
            stream_pe(K, pe, name, split=norm is not None)

        @block.scalar
        def _(act):
            if norm:
                norm.act(act)

            def evac(t, g, slot, times):
                wait_bank(K, act, g, 0)
                nc.scalar.activation(sg[:, slot, :], K.ps[:, 2 * slot, :], ACT.Silu).then_inc(silu.sem, silu.n(1, times))
            stream_act(K, act, name, evac)

        @block.vector
        def _(dve):
            if norm:
                norm.dve(dve)

            def evac(t, g, slot, times):
                wait_bank(K, dve, g, 1)
                dve.wait_ge(silu.sem, silu.at(t + 1))
                nc.vector.scalar_tensor_tensor(h[:, slot, :], sg[:, slot, :], weight, K.ps[:, 2 * slot + 1, :],
                                               ALU.mult, ALU.mult).then_inc(h_ready.sem, h_ready.n(1, times))
                dve.wait_ge(h_ready.sem, h_ready.at(t + 1))
                nc.vector.nop().then_inc(K.s("bank_free_0").sem, K.s("bank_free_0").n(1, times))
                nc.vector.nop().then_inc(K.s("bank_free_1").sem, K.s("bank_free_1").n(1, times))
                at = bass.ds(t, 1) if not isinstance(t, int) else slice(t, t + 1)
                nc.vector.tensor_copy(K.hhi[:, at, :], h[:, slot:slot + 1, :]).then_inc(hhi_ready.sem, hhi_ready.n(1, times))
                dve.wait_ge(hhi_ready.sem, hhi_ready.at(t + 1))
                nc.vector.tensor_tensor(K.hlo[:, at, :], h[:, slot:slot + 1, :], K.hhi[:, at, :].bitcast(F32),
                                        ALU.subtract)
            stream_dve(K, dve, name, evac)
    K.end_block(name)


def phase_ffn_out(K, name):
    nc, s = K.nc, K.s
    norm = LayerNorm(K, 0, mean_bank=0, var_bank=1)
    with nc.Block() as block:
        @block.sync
        def _(sp):
            stream_load(K, sp, name)

        @block.gpsimd
        def _(pool):
            stream_split_lo(K, pool, name)

        @block.scalar
        def _(act):
            stream_act(K, act, name)
            norm.stats_act(act)

        @block.tensor
        def _(pe):
            def body(t, g, uses, slot, times):
                pe.wait_ge(K.s("lo_ready").sem, g + 1)
                for j in range(2):
                    f = bass.ds(2 * t + j, 1) if not isinstance(t, int) else slice(2 * t + j, 2 * t + j + 1)
                    for m in range(KC):
                        last = three_products(K, K.ps[:, m:m + 1, :], K.whi[:, slot, 8 * j + m, :],
                                              K.wlo[:, slot, 8 * j + m, :], K.hhi[:, f, :], K.hlo[:, f, :],
                                              isinstance(t, int) and t == 0 and j == 0,
                                              isinstance(t, int) and t == TILES[name] - 1 and j == 1)
                        if isinstance(t, int) and t == TILES[name] - 1 and j == 1 and m < KC - 1:
                            last.then_inc(s("sum_ready").sem, s("sum_ready").n())
                    last.then_inc(K.s(("first_done", "tile_done")[j]).sem, 1)
            n, first = TILES[name], FIRST_TILE[name]
            body(0, first, 0, first % 2, 1)
            loops = (n - 3) // 2
            with pe.Fori(0, loops) as i:
                for j in range(2):
                    body(2 * i + (1 + j), 2 * i + (first + 1 + j), 0, (first + 1 + j) % 2, loops)
            for t in range(1 + 2 * loops, n):
                body(t, first + t, 0, (first + t) % 2, 1)
            norm.stats_pe(pe, lambda pe, c: pe.wait_ge(s("sum_taken").sem, s("sum_taken").at(c + 1)))

        @block.vector
        def _(dve):
            for m in range(KC):
                if m < KC - 1:
                    dve.wait_ge(s("sum_ready").sem, s("sum_ready").at(m + 1))
                else:
                    wait_bank(K, dve, FIRST_TILE[name] + TILES[name] - 1, 1)
                nc.vector.scalar_tensor_tensor(K.A[:, m, :], K.A[:, m, :], ALPHA, K.ps[:, m, :], ALU.mult,
                                               ALU.add).then_inc(s("sum_taken").sem, s("sum_taken").n())
            norm.stats_dve(dve)
    K.end_block(name)


class LayerNorm:
    FACTOR = 7

    def __init__(self, K, src, mean_bank=4, var_bank=5):
        self.K, self.src, self.mean_bank, self.var_bank = K, src, mean_bank, var_bank

    def stats_pe(self, pe, wait_chunk):
        K, s = self.K, self.K.s
        for c in range(KC):
            wait_chunk(pe, c)
            last = K.nc.tensor.matmul(K.ps[:, self.mean_bank, :], K.mat("mean"), K.A[:, self.src + c, :],
                                      start=c == 0, stop=c == KC - 1)
        last.then_inc(s("mean_ready").sem, s("mean_ready").n())
        for c in range(KC):
            pe.wait_ge(s("squared").sem, s("squared").at(c + 1))
            last = K.nc.tensor.matmul(K.ps[:, self.var_bank, :], K.mat("mean"), K.pair[:, c, :], start=c == 0,
                                      stop=c == KC - 1)
        last.then_inc(s("var_ready").sem, s("var_ready").n())

    def stats_act(self, act):
        K, s = self.K, self.K.s
        for c in range(KC):
            act.wait_ge(s("centred").sem, s("centred").at(c + 1))
            K.nc.scalar.activation(K.pair[:, c, :], K.A[:, self.src + c, :], ACT.Square).then_inc(
                s("squared").sem, s("squared").n())
        act.wait_ge(s("var_ready").sem, s("var_ready").at(1))
        K.nc.scalar.activation(K.ps[:, self.FACTOR, :], K.ps[:, self.var_bank, :], ACT.Abs_reciprocal_sqrt,
                               bias=K.eps(LN_EPS))

    def stats_dve(self, dve):
        K, s = self.K, self.K.s
        dve.wait_ge(s("mean_ready").sem, s("mean_ready").at(1))
        for c in range(KC):
            K.nc.vector.tensor_tensor(K.A[:, self.src + c, :], K.A[:, self.src + c, :], K.ps[:, self.mean_bank, :],
                                      ALU.subtract).then_inc(s("centred").sem, s("centred").n())


class Affine:

    def __init__(self, K, src, g, b, func=ACT.Identity, split=True):
        self.K, self.src, self.g, self.b, self.func, self.split = K, src, g, b, func, split

    def act(self, act):
        K, s = self.K, self.K.s
        for c in range(KC):
            act.wait_ge(s("scaled").sem, s("scaled").at(c + 1))
            x = K.A[:, self.src + c, :]
            outs = [K.xhi[:, c, :], x] if self.split else [x]
            for out in outs:
                last = K.nc.scalar.activation(out, x, self.func, bias=K.vec(self.b, c), scale=K.vec(self.g, c))
            last.then_inc(s("normed").sem, s("normed").n())

    def dve(self, dve):
        K, s = self.K, self.K.s
        for c in range(KC + 2):
            if c < KC:
                x = K.A[:, self.src + c, :]
                K.nc.vector.tensor_tensor(x, x, K.ps[:, LayerNorm.FACTOR, :], ALU.mult).then_inc(
                    s("scaled").sem, s("scaled").n())
            if self.split and c >= 2:
                dve.wait_ge(s("normed").sem, s("normed").at(c - 1))
                K.nc.vector.tensor_tensor(K.xlo[:, c - 2, :], K.A[:, self.src + c - 2, :],
                                          K.xhi[:, c - 2, :].bitcast(F32), ALU.subtract).then_inc(
                    s("x_split").sem, s("x_split").n())


def phase_stream(K, label, names, pe=None, act=None, dve=None, load=None, load_next=None, pe_last=None, presplit=None, width=T,
                 norm=None, stats=None, wait_chunk=None):
    with K.nc.Block() as block:
        @block.sync
        def _(sp):
            if load:
                load(sp)
            stream_load(K, sp, names)
            if load_next:
                load_next(sp)

        @block.gpsimd
        def _(pool):
            stream_split_lo(K, pool, names)

        @block.tensor
        def _(pe_):
            if pe:
                pe(pe_)
            else:
                stream_pe(K, pe_, names, split=presplit is not None or norm is not None)
            if pe_last:
                pe_last(pe_)
            if stats:
                stats.stats_pe(pe_, wait_chunk)

        @block.scalar
        def _(act_):
            if norm:
                norm.act(act_)
            stream_act(K, act_, names, act and (lambda t, g, slot, times: act(act_, t, g, slot)), True)
            if stats:
                stats.stats_act(act_)

        @block.vector
        def _(dve_):
            if presplit is not None:
                split_chunks(K, dve_, presplit, width=width)
            if norm:
                norm.dve(dve_)
            if dve:
                stream_dve(K, dve_, names, lambda t, g, slot, times: dve(dve_, t, g, slot), True)
            if stats:
                stats.stats_dve(dve_)
    K.end_block(label)


def free_bank(K, j):
    s = K.s(f"bank_free_{j}")
    return s.sem, s.n()


def phase_glu(K):
    nc, s = K.nc, K.s
    sg = K.A[:, 48:50, :]

    def act(act, t, g, slot):
        if t == 0:
            act.wait_ge(s("normed").sem, s("normed").at(KC))
            act.dma_start(K.dram["keep_x"], K.A[:, 0:8, :]).then_inc(s("spilled").sem, s("spilled").n(16))
        wait_bank(K, act, g, 1)
        if t >= 2:
            act.wait_ge(s("glu_ready").sem, s("glu_ready").at(t - 1))
        nc.scalar.activation(sg[:, slot, :], K.ps[:, 2 * slot + 1, :], ACT.Sigmoid).then_inc(s("sigmoid").sem, s("sigmoid").n())

    def dve(dve, t, g, slot):
        wait_bank(K, dve, g, 0)
        dve.wait_ge(s("sigmoid").sem, s("sigmoid").at(t + 1))
        nc.vector.tensor_tensor(K.A[:, 8 + t, :], K.ps[:, 2 * slot, :], sg[:, slot, :],
                                ALU.mult).then_inc(s("glu_ready").sem, s("glu_ready").n())
        dve.wait_ge(s("glu_ready").sem, s("glu_ready").at(t + 1))
        nc.vector.nop().then_inc(*free_bank(K, 0))
        nc.vector.nop().then_inc(*free_bank(K, 1))

    def pe_last(pe):
        for i in range(NT):
            for k in range(KC):
                last = nc.tensor.matmul(K.ps[:, 6, 16 * i:16 * i + 16], K.A[:, k, P * i:P * i + P],
                                        K.small[:, 16 * k:16 * k + 16], start=k == 0, stop=k == KC - 1)
        last.then_inc(s("ab_ready").sem, s("ab_ready").n())
        pe.wait_ge(s("spilled").sem, s("spilled").at(16))
    phase_stream(K, "glu", "glu", act=act, dve=dve, pe_last=pe_last, norm=Affine(K, 0, "ln1_g", "ln1_b"))


AB, G, BETA, GC, BG, KD, EGL, T1 = 320, 384, 416, 448, 480, 512, 544, 608


def phase_projections(K):
    nc, s = K.nc, K.s
    tmp = K.A[:, 48:56, :]
    names = ["qkv", "z", "gates"]

    def act(act, t, g, slot):
        for j in range(2):
            c = 2 * t + j
            if t < 12:
                act.wait_ge(s("short_done").sem, s("short_done").at(4 * (c + 1)))
                nc.scalar.activation(K.A[:, 24 + c, :], tmp[:, 2 * slot + j, :], ACT.Silu).then_inc(
                    s("qkv_ready").sem, s("qkv_ready").n())
            else:
                u = c - 24
                wait_bank(K, act, g, j)
                if u >= 4:
                    act.wait_ge(s(f"spilled_{u % 4}").sem, s(f"spilled_{u % 4}").at(16 * (u // 4)))
                nc.scalar.activation(tmp[:, 4 + u % 4, :], K.ps[:, 2 * slot + j, :],
                                     ACT.Silu if t < 16 else ACT.Sigmoid).then_inc(
                    s("gate_ready").sem, s("gate_ready").n())
                act.wait_ge(s("gate_ready").sem, s("gate_ready").at(u + 1))
                act.dma_start(K.dram["keep_gates"][u], tmp[:, 4 + u % 4, :]).then_inc(
                    s(f"spilled_{u % 4}").sem, s(f"spilled_{u % 4}").n(16))
        if t == 23:
            for r in range(4):
                act.wait_ge(s(f"spilled_{r}").sem, s(f"spilled_{r}").at(16 * 6))

    def long_conv():
        acc, src = 16, 8
        done = s("long_done")
        n = 0
        for tap in range(CONV_WIDTH - 1, -1, -1):
            back = CONV_WIDTH - 1 - tap
            for c in range(KC):
                w = K.vec("conv_w", 8 * tap + c)
                if back == 0:
                    nc.vector.tensor_scalar(K.A[:, acc + c, :], K.A[:, src + c, :], w, K.vec("conv_b", c),
                                            ALU.mult, ALU.add).then_inc(done.sem, done.n())
                else:
                    nc.vector.wait_ge(done.sem, done.at(n - KC + 1))
                    nc.vector.scalar_tensor_tensor(K.A[:, acc + c, back:], K.A[:, src + c, :T - back], w,
                                                   K.A[:, acc + c, back:], ALU.mult, ALU.add).then_inc(done.sem, done.n())
                n += 1
                yield

    conv = long_conv()

    def dve(dve, t, g, slot):
        if t < 12:
            short = s("short_done")
            for j in range(2):
                c = 2 * t + j
                bank, acc = K.ps[:, 2 * slot + j, :], tmp[:, 2 * slot + j, :]
                wait_bank(K, dve, g, j)
                if t >= 2:
                    dve.wait_ge(s("qkv_ready").sem, s("qkv_ready").at(c - 3))
                for tap in range(SHORT_CONV - 1, -1, -1):
                    back = SHORT_CONV - 1 - tap
                    w = K.vec("gdn_conv", 4 * c + tap)
                    if back == 0:
                        nc.vector.tensor_scalar(acc, bank, w, None, ALU.mult).then_inc(short.sem, short.n())
                    else:
                        dve.wait_ge(short.sem, short.at(4 * c + back))
                        nc.vector.scalar_tensor_tensor(acc[:, back:], bank[:, :T - back], w, acc[:, back:],
                                                       ALU.mult, ALU.add).then_inc(short.sem, short.n())
                dve.wait_ge(short.sem, short.at(4 * c + 4))
                nc.vector.nop().then_inc(*free_bank(K, j))
        else:
            for j in range(2):
                dve.wait_ge(s("gate_ready").sem, s("gate_ready").at(2 * t + j - 23))
                nc.vector.nop().then_inc(*free_bank(K, j))
        for _ in range(8 if t < 12 else 13):
            next(conv, None)
    phase_stream(K, "projections", names, act=act, dve=dve, stats=LayerNorm(K, 16), wait_chunk=lambda pe, c: pe.wait_ge(
        s("long_done").sem, s("long_done").at(KC * (CONV_WIDTH - 1) + c + 1)))


def phase_conv_out(K):
    nc, s = K.nc, K.s

    def load(sp):
        sp.dma_start(K.A[:, 0:8, :], K.dram["keep_gates"][16:24].rearrange("c p n -> p c n")).then_inc(
            s("reloaded").sem, s("reloaded").n(16))

    def dve(dve, t, g, slot):
        if t == 0:
            dve.wait_ge(s("reloaded").sem, s("reloaded").at(16))
        for j in range(2):
            c = 2 * t + j
            wait_bank(K, dve, g, j)
            nc.vector.scalar_tensor_tensor(K.A[:, 8 + c, :], K.ps[:, 2 * slot + j, :], K.vec("b_conv_out", c),
                                           K.A[:, c, :], ALU.add, ALU.mult).then_inc(*free_bank(K, j))
    phase_stream(K, "conv_out", "conv_out", dve=dve, load=load, norm=Affine(K, 16, "conv_ln_g", "conv_ln_b", ACT.Silu))
    with nc.Block() as block:
        @block.sync
        def _(sp):
            sp.dma_start(K.dram["keep_yc"], K.A[:, 8:16, :]).then_inc(s("spilled").sem, s("spilled").n(16))
            sp.wait_ge(s("spilled").sem, s("spilled").at(16))
    K.end_block("yc_spill")


def phase_gdn_gates(K):
    nc, s = K.nc, K.s

    def f(at, n=32):
        return K.small[:, at:at + n]

    def th(at):
        return K.small[:, at:at + 32].rearrange("p (i h) -> p i h", h=GDN_HEADS)

    a_in = K.ps[:, 6, 0:64].rearrange("p (i c) -> p i c", c=16)
    with nc.Block() as block:
        @block.vector
        def _(dve):
            step = s("gates_dve")

            def link(ins, n):
                ins.then_inc(step.sem, step.n())
                dve.wait_ge(step.sem, step.at(n))
            row = K.vec("dt_bias", 0, 8).unsqueeze(1).broadcast_to([P, NT, 8])
            link(nc.vector.tensor_tensor(th(T1), a_in[:, :, 0:8], row, ALU.add), 1)
            link(nc.vector.tensor_scalar(f(T1 + 32), f(T1), -1.0, None, ALU.mult), 2)
            link(nc.vector.tensor_tensor(f(T1 + 32), f(T1), f(T1 + 32), ALU.min), 3)
            dve.wait_ge(s("gates_act").sem, s("gates_act").at(2))
            link(nc.vector.scalar_tensor_tensor(f(T1), f(T1), 0.0, f(T1 + 64), ALU.max, ALU.add), 4)
            row = f(T1 + 96, 8).unsqueeze(1).broadcast_to([P, NT, 8])
            dve.wait_ge(s("gates_act").sem, s("gates_act").at(3))
            link(nc.vector.tensor_tensor(th(G), th(T1), row, ALU.mult), 5)
            link(nc.vector.tensor_scalar(f(G), f(G), -1.0, None, ALU.mult), 6)
            dve.wait_ge(s("gates_pe").sem, s("gates_pe").at(1))
            link(nc.vector.tensor_copy(f(GC), K.ps[:, 5, 0:32]), 7)
            link(nc.vector.tensor_tensor(f(KD), K.ps[:, 5, 32:64], f(GC), ALU.subtract), 8)
            dve.wait_ge(s("gates_act").sem, s("gates_act").at(5))
            link(nc.vector.tensor_tensor(f(BG), f(BG), f(BETA), ALU.mult), 9)

        @block.scalar
        def _(act):
            done, dve_done = s("gates_act"), s("gates_dve")
            act.wait_ge(dve_done.sem, dve_done.at(3))
            nc.scalar.activation(f(T1 + 32), f(T1 + 32), ACT.Exp).then_inc(done.sem, done.n())
            act.wait_ge(done.sem, done.at(1))
            nc.scalar.activation(f(T1 + 64), f(T1 + 32), ACT.Ln, bias=K.eps(1.0)).then_inc(done.sem, done.n())
            nc.scalar.activation(f(T1 + 96, 8), K.vec("a_log", 0, 8), ACT.Exp).then_inc(done.sem, done.n())
            nc.scalar.activation(th(BETA), a_in[:, :, 8:16], ACT.Sigmoid).then_inc(done.sem, done.n())
            act.wait_ge(dve_done.sem, dve_done.at(7))
            nc.scalar.activation(f(BG), f(GC), ACT.Exp).then_inc(done.sem, done.n())
            act.wait_ge(dve_done.sem, dve_done.at(8))
            nc.scalar.activation(f(KD), f(KD), ACT.Exp).then_inc(done.sem, done.n())

        @block.tensor
        def _(pe):
            pe.wait_ge(s("gates_dve").sem, s("gates_dve").at(6))
            nc.tensor.matmul(K.ps[:, 5, 0:32], K.mat("chunk_tri"), f(G), start=True, stop=True)
            nc.tensor.matmul(K.ps[:, 5, 32:64], K.mat("chunk_ones"), f(G), start=True, stop=True).then_inc(
                s("gates_pe").sem, s("gates_pe").n())
    K.end_block("gdn_gates")


def phase_head_norm(K, label, items, scratch, eps=RMS_EPS, after=None):
    nc, s = K.nc, K.s
    n = len(items)
    sq, rstd = K.A[:, scratch:scratch + 2, :], K.A[:, scratch + 2:scratch + 4, :]
    with nc.Block() as block:
        @block.scalar
        def _(act):
            def square(i):
                if i >= 2:
                    act.wait_ge(s("norm_sum").sem, s("norm_sum").at(i - 1))
                nc.scalar.activation(sq[:, i % 2, :], K.A[:, items[i][0], :], ACT.Square).then_inc(
                    s("norm_sq").sem, s("norm_sq").n())
            square(0)
            for i in range(n):
                if i + 1 < n:
                    square(i + 1)
                act.wait_ge(s("norm_sum").sem, s("norm_sum").at(i + 1))
                if i >= 2:
                    act.wait_ge(s("norm_out").sem, s("norm_out").at(i - 1))
                nc.scalar.activation(rstd[:, i % 2, :], K.ps[:, i % 4, :], ACT.Abs_reciprocal_sqrt,
                                     bias=K.eps(eps(i) if callable(eps) else eps)).then_inc(s("norm_rstd").sem, s("norm_rstd").n())

        @block.tensor
        def _(pe):
            for i in range(n):
                pe.wait_ge(s("norm_sq").sem, s("norm_sq").at(i + 1))
                if i >= 4:
                    pe.wait_ge(s("norm_rstd").sem, s("norm_rstd").at(i - 3))
                nc.tensor.matmul(K.ps[:, i % 4, :], K.mat(items[i][1]), sq[:, i % 2, :], start=True,
                                 stop=True).then_inc(s("norm_sum").sem, s("norm_sum").n())

        @block.sync
        def _(sp):
            if after:
                after(sp)

        @block.vector
        def _(dve):
            for i, (c, _, gain, *times) in enumerate(items):
                dve.wait_ge(s("norm_rstd").sem, s("norm_rstd").at(i + 1))
                nc.vector.scalar_tensor_tensor(K.A[:, c, :], K.A[:, c, :], gain, rstd[:, i % 2, :], ALU.mult,
                                               ALU.mult).then_inc(s("norm_out").sem, s("norm_out").n())
                if times:
                    if i == 0 and after:
                        dve.wait_ge(s("reloaded").sem, s("reloaded").at(16))
                    dve.wait_ge(s("norm_out").sem, s("norm_out").at(i + 1))
                    nc.vector.tensor_tensor(K.A[:, c, :], K.A[:, c, :], K.A[:, times[0], :], ALU.mult)
    K.end_block(label)


def tiles_of(ap):
    return ap.rearrange("p (i n) -> p i n", n=P)


def over_tiles(ap):
    return ap.unsqueeze(1).broadcast_to([P, NT, P])


def per_token(K, at, h):
    return K.small[:, at:at + 32].rearrange("p (i h) -> p i h", h=8)[:, :, h:h + 1].broadcast_to([P, NT, P])


UU, AT, MT, TT, QQ, KK, VV = 0, 8, 16, 48, 24, 32, 40


def phase_gdn_matrices(K):
    nc, s = K.nc, K.s
    A, W = K.A, K.pair

    def w(kind, h):
        return W[:, 2 * kind + h % 2, :]
    TRI, DIAG, DEC, EXPG, MD = range(5)
    with nc.Block() as block:
        @block.vector
        def _(dve):
            step = s("mat_dve")
            state = [0]

            def link(ins):
                ins.then_inc(step.sem, step.n())
                state[0] += 1

            def settle():
                dve.wait_ge(step.sem, step.at(state[0]))

            def first(h):
                if h >= 2:
                    dve.wait_ge(s("mat_pe").sem, s("mat_pe").at(2 * (h - 1)))
                link(nc.vector.tensor_tensor(tiles_of(w(TRI, h)), over_tiles(K.mat("chunk_tri")), per_token(K, G, h), ALU.mult))
                link(nc.vector.tensor_tensor(tiles_of(w(DIAG, h)), over_tiles(K.mat("ident")), per_token(K, BETA, h), ALU.mult))
                settle()
                nc.vector.nop().then_inc(s("mat_in").sem, s("mat_in").n())
            first(0)
            for h in range(GDN_HEADS):
                b = 4 * (h % 2)
                if h + 1 < GDN_HEADS:
                    first(h + 1)
                dve.wait_ge(s("mat_pe").sem, s("mat_pe").at(2 * h + 1))
                link(nc.vector.tensor_tensor(tiles_of(w(DEC, h)), tiles_of(K.ps[:, b, :]), per_token(K, GC, h), ALU.subtract))
                settle()
                link(nc.vector.tensor_scalar(w(DEC, h), w(DEC, h), 0.0, None, ALU.min))
                settle()
                nc.vector.nop().then_inc(s("mat_dec").sem, s("mat_dec").n())
                dve.wait_ge(s("mat_pe").sem, s("mat_pe").at(2 * h + 2))
                dve.wait_ge(s("mat_exp").sem, s("mat_exp").at(2 * h + 2))
                link(nc.vector.tensor_tensor(tiles_of(w(DEC, h)), tiles_of(w(DEC, h)), over_tiles(K.mat("chunk_tri")), ALU.mult))
                link(nc.vector.tensor_tensor(A[:, QQ + h, :], A[:, QQ + h, :], w(EXPG, h), ALU.mult))
                settle()
                link(nc.vector.tensor_tensor(A[:, AT + h, :], w(DEC, h), K.ps[:, b + 3, :], ALU.mult))
                link(nc.vector.tensor_tensor(w(MD, h), w(DEC, h), K.ps[:, b + 1, :], ALU.mult))
                settle()
                link(nc.vector.tensor_tensor(A[:, MT + h, :], w(MD, h), K.ps[:, b + 2, :], ALU.mult))
                settle()
                link(nc.vector.tensor_tensor(tiles_of(w(MD, h)), tiles_of(A[:, MT + h, :]), over_tiles(K.mat("level1")), ALU.mult))
                settle()
                link(nc.vector.tensor_tensor(tiles_of(A[:, UU + h, :]), over_tiles(K.mat("ident")), tiles_of(w(MD, h)), ALU.subtract))
                settle()
                nc.vector.nop().then_inc(s("mat_u").sem, s("mat_u").n())

        @block.scalar
        def _(act):
            for h in range(GDN_HEADS):
                b = 4 * (h % 2)
                act.wait_ge(s("mat_dec").sem, s("mat_dec").at(h + 1))
                nc.scalar.activation(w(DEC, h), w(DEC, h), ACT.Exp).then_inc(s("mat_exp").sem, s("mat_exp").n())
                nc.scalar.activation(w(EXPG, h), K.ps[:, b, :], ACT.Exp).then_inc(s("mat_exp").sem, s("mat_exp").n())
                nc.scalar.activation(K.small[:, EGL + 8 * h:EGL + 8 * h + 8],
                                     K.ps[:, b, :].rearrange("p (n c) -> p n c", c=CHUNK)[:, :, CHUNK - 1],
                                     ACT.Exp).then_inc(s("mat_egl").sem, s("mat_egl").n())
                act.wait_ge(s("mat_t").sem, s("mat_t").at(h + 1))
                nc.scalar.activation(A[:, TT + h, :], K.ps[:, b, :], ACT.Copy).then_inc(s("mat_tc").sem, s("mat_tc").n())

        @block.tensor
        def _(pe):
            def products(h):
                b = 4 * (h % 2)
                if h >= 2:
                    pe.wait_ge(s("mat_tc").sem, s("mat_tc").at(h - 1))
                    pe.wait_ge(s("mat_u").sem, s("mat_u").at(h - 1))
                pe.wait_ge(s("mat_in").sem, s("mat_in").at(h + 1))
                nc.tensor.matmul(K.ps[:, b, :], K.mat("ones"), w(TRI, h), start=True, stop=True).then_inc(
                    s("mat_pe").sem, s("mat_pe").n())
                nc.tensor.matmul(K.ps[:, b + 1, :], K.mat("ones"), w(DIAG, h), start=True, stop=True)
                for i in range(NT):
                    t = slice(P * i, P * i + P)
                    nc.tensor.matmul(K.ps[:, b + 2, t], A[:, KK + h, t], A[:, KK + h, t], start=True, stop=True)
                    last = nc.tensor.matmul(K.ps[:, b + 3, t], A[:, KK + h, t], A[:, QQ + h, t], start=True, stop=True)
                last.then_inc(s("mat_pe").sem, s("mat_pe").n())
            products(0)
            for h in range(GDN_HEADS):
                b = 4 * (h % 2)
                if h + 1 < GDN_HEADS:
                    products(h + 1)
                pe.wait_ge(s("mat_u").sem, s("mat_u").at(h + 1))
                pe.wait_ge(s("mat_egl").sem, s("mat_egl").at(h + 1))
                for i in range(NT):
                    t = slice(P * i, P * i + P)
                    last = nc.tensor.transpose(K.ps[:, b, t], A[:, UU + h, t], K.mat("ident"))
                last.then_inc(s("mat_t").sem, s("mat_t").n())
    K.end_block("gdn_matrices")


def phase_gdn_inverse(K):
    nc, s = K.nc, K.s
    A, W = K.A, K.pair
    items = [(level, h) for level in (2, 4, 8, 16, 32) for h in range(GDN_HEADS)]
    n = len(items)
    with nc.Block() as block:
        @block.gpsimd
        def _(pool):
            for x, (level, h) in enumerate(items):
                if x >= 3:
                    pool.wait_ge(s("inv_lt").sem, s("inv_lt").at(x - 2))
                nc.gpsimd.tensor_tensor(tiles_of(W[:, x % 3, :]), tiles_of(A[:, MT + h, :]),
                                        over_tiles(K.mat(f"level{level}")), ALU.mult).then_inc(s("inv_mask").sem, s("inv_mask").n())

        @block.vector
        def _(dve):
            for x, (level, h) in enumerate(items):
                dve.wait_ge(s("inv_tlt").sem, s("inv_tlt").at(x + 1))
                if level < 32:
                    nc.vector.tensor_tensor(A[:, TT + h, :], A[:, TT + h, :], K.ps[:, 2 + x % 2, :], ALU.subtract)
                nc.vector.tensor_tensor(A[:, UU + h, :], A[:, UU + h, :], K.ps[:, 4 + x % 2, :],
                                        ALU.subtract).then_inc(s("inv_done").sem, s("inv_done").n())

        @block.scalar
        def _(act):
            for x in range(n):
                act.wait_ge(s("inv_lt").sem, s("inv_lt").at(x + 1))
                if x >= 2:
                    act.wait_ge(s("inv_tlt").sem, s("inv_tlt").at(x - 1))
                nc.scalar.activation(W[:, 3 + x % 2, :], K.ps[:, x % 2, :], ACT.Copy).then_inc(s("inv_copy").sem, s("inv_copy").n())

        @block.tensor
        def _(pe):
            def lt(x):
                level, h = items[x]
                pe.wait_ge(s("inv_mask").sem, s("inv_mask").at(x + 1))
                if x >= 8:
                    pe.wait_ge(s("inv_done").sem, s("inv_done").at(x - 7))
                if x >= 2:
                    pe.wait_ge(s("inv_copy").sem, s("inv_copy").at(x - 1))
                for i in range(NT):
                    t = slice(P * i, P * i + P)
                    last = nc.tensor.matmul(K.ps[:, x % 2, t], W[:, x % 3, t], A[:, TT + h, t], start=True, stop=True)
                last.then_inc(s("inv_lt").sem, s("inv_lt").n())
            lt(0)
            for x, (level, h) in enumerate(items):
                if x + 1 < n:
                    lt(x + 1)
                pe.wait_ge(s("inv_copy").sem, s("inv_copy").at(x + 1))
                if x >= 2:
                    pe.wait_ge(s("inv_done").sem, s("inv_done").at(x - 1))
                for i in range(NT):
                    t = slice(P * i, P * i + P)
                    if level < 32:
                        nc.tensor.matmul(K.ps[:, 2 + x % 2, t], A[:, UU + h, t], W[:, 3 + x % 2, t], start=True, stop=True)
                    last = nc.tensor.matmul(K.ps[:, 4 + x % 2, t], W[:, 3 + x % 2, t], A[:, UU + h, t], start=True, stop=True)
                last.then_inc(s("inv_tlt").sem, s("inv_tlt").n())
    K.end_block("gdn_inverse")


def phase_gdn_tokens(K):
    nc, s = K.nc, K.s
    A, W = K.A, K.pair
    with nc.Block() as block:
        @block.tensor
        def _(pe):
            def turn(h):
                b = 3 * (h % 2)
                if h >= 2:
                    pe.wait_ge(s("tok_scaled").sem, s("tok_scaled").at(h - 1))
                for i in range(NT):
                    t = slice(P * i, P * i + P)
                    nc.tensor.transpose(K.ps[:, b, t], A[:, VV + h, t], K.mat("ident"))
                    last = nc.tensor.transpose(K.ps[:, b + 1, t], A[:, KK + h, t], K.mat("ident"))
                last.then_inc(s("tok_turned").sem, s("tok_turned").n())
            turn(0)
            for h in range(GDN_HEADS):
                if h + 1 < GDN_HEADS:
                    turn(h + 1)
                pe.wait_ge(s("tok_scaled").sem, s("tok_scaled").at(h + 1))
                if h >= 2:
                    pe.wait_ge(s("tok_w").sem, s("tok_w").at(h - 1))
                for i in range(NT):
                    t = slice(P * i, P * i + P)
                    last = nc.tensor.matmul(K.ps[:, 3 * (h % 2) + 2, t], W[:, h % 2, t], A[:, UU + h, t], start=True, stop=True)
                last.then_inc(s("tok_wt").sem, s("tok_wt").n())

        @block.vector
        def _(dve):
            for h in range(GDN_HEADS):
                b = 3 * (h % 2)
                dve.wait_ge(s("tok_turned").sem, s("tok_turned").at(h + 1))
                if h >= 2:
                    dve.wait_ge(s("tok_wt").sem, s("tok_wt").at(h - 1))
                nc.vector.tensor_tensor(tiles_of(A[:, VV + h, :]), tiles_of(K.ps[:, b, :]), per_token(K, BETA, h), ALU.mult)
                nc.vector.tensor_tensor(tiles_of(W[:, h % 2, :]), tiles_of(K.ps[:, b + 1, :]), per_token(K, BG, h), ALU.mult)
                nc.vector.tensor_tensor(tiles_of(A[:, MT + h, :]), tiles_of(K.ps[:, b + 1, :]), per_token(K, KD, h),
                                        ALU.mult).then_inc(s("tok_scaled").sem, s("tok_scaled").n())

        @block.scalar
        def _(act):
            for h in range(GDN_HEADS):
                act.wait_ge(s("tok_wt").sem, s("tok_wt").at(h + 1))
                nc.scalar.activation(A[:, KK + h, :], K.ps[:, 3 * (h % 2) + 2, :], ACT.Copy, scale=-1.0).then_inc(
                    s("tok_w").sem, s("tok_w").n())
    K.end_block("gdn_tokens")


def phase_gdn_scan(K):
    nc, s = K.nc, K.s
    A, W = K.A, K.pair
    state = A[:, TT:TT + 2, :].rearrange("p u (h n) -> p (u h) n", n=P)
    items = [(n, grp) for n in range(T // CHUNK) for grp in range(2)]
    with nc.Block() as block:
        @block.vector
        def _(dve):
            nc.vector.memset(A[:, TT:TT + 2, :], 0.0).then_inc(s("scan_zero").sem, s("scan_zero").n())
            dve.wait_ge(s("scan_zero").sem, s("scan_zero").at(1))
            for x, (n, grp) in enumerate(items):
                dve.wait_ge(s("scan_kv").sem, s("scan_kv").at(x + 1))
                for hh in range(4):
                    h = 4 * grp + hh
                    last = nc.vector.scalar_tensor_tensor(
                        state[:, h, :], state[:, h, :], K.small[:, EGL + 8 * h + n:EGL + 8 * h + n + 1],
                        K.ps[:, 4 + grp, P * hh:P * hh + P], ALU.mult, ALU.add)
                last.then_inc(s("scan_state").sem, s("scan_state").n())

        @block.scalar
        def _(act):
            for x, (n, grp) in enumerate(items):
                rows = slice(CHUNK * (n % 2), CHUNK * (n % 2) + CHUNK)
                act.wait_ge(s("scan_v").sem, s("scan_v").at(x + 1))
                nc.scalar.activation(W[rows, grp, :], K.ps[rows, grp, :], ACT.Copy).then_inc(s("scan_vc").sem, s("scan_vc").n())
                act.wait_ge(s("scan_kv").sem, s("scan_kv").at(x + 1))
                nc.scalar.activation(A[:, QQ + 4 * grp:QQ + 4 * grp + 4, CHUNK * n:CHUNK * n + CHUNK],
                                     K.ps[:, 2 + grp, 0:4 * CHUNK].rearrange("p (h c) -> p h c", c=CHUNK),
                                     ACT.Copy).then_inc(s("scan_o").sem, s("scan_o").n())

        @block.tensor
        def _(pe):
            pe.wait_ge(s("scan_zero").sem, s("scan_zero").at(1))

            def new_v(x):
                n, grp = items[x]
                i, rows, cols = n // 2, slice(CHUNK * (n % 2), CHUNK * (n % 2) + CHUNK), slice(CHUNK * n, CHUNK * n + CHUNK)
                if x >= 2:
                    pe.wait_ge(s("scan_state").sem, s("scan_state").at(x - 1))
                    pe.wait_ge(s("scan_vc").sem, s("scan_vc").at(x - 1))
                for hh in range(4):
                    h = 4 * grp + hh
                    out = K.ps[rows, grp, P * hh:P * hh + P]
                    nc.tensor.matmul(out, A[:, UU + h, cols], A[:, VV + h, P * i:P * i + P], start=True, stop=False)
                    last = nc.tensor.matmul(out, A[:, KK + h, cols], state[:, h, :], start=False, stop=True)
                last.then_inc(s("scan_v").sem, s("scan_v").n())
            new_v(0)
            for x, (n, grp) in enumerate(items):
                i, rows, cols = n // 2, slice(CHUNK * (n % 2), CHUNK * (n % 2) + CHUNK), slice(CHUNK * n, CHUNK * n + CHUNK)
                if x == 0:
                    new_v(1)
                pe.wait_ge(s("scan_vc").sem, s("scan_vc").at(x + 1))
                if x >= 2:
                    pe.wait_ge(s("scan_o").sem, s("scan_o").at(x - 1))
                for hh in range(4):
                    h = 4 * grp + hh
                    out = K.ps[:, 2 + grp, CHUNK * hh:CHUNK * hh + CHUNK]
                    nc.tensor.matmul(out, state[:, h, :], A[:, QQ + h, cols], start=True, stop=False)
                    nc.tensor.matmul(out, W[rows, grp, P * hh:P * hh + P], A[rows, AT + h, cols], start=False, stop=True)
                    last = nc.tensor.matmul(K.ps[:, 4 + grp, P * hh:P * hh + P], A[rows, MT + h, P * i:P * i + P],
                                            W[rows, grp, P * hh:P * hh + P], start=True, stop=True)
                last.then_inc(s("scan_kv").sem, s("scan_kv").n())
                if x >= 1 and x + 1 < len(items):
                    new_v(x + 1)
    K.end_block("gdn_scan")


def phase_gdn_out(K):
    nc, s = K.nc, K.s

    def load(sp):
        sp.dma_start(K.A[:, 8:16, :], K.dram["keep_gates"][8:16].rearrange("c p n -> p c n")).then_inc(
            s("reloaded").sem, s("reloaded").n(16))
        sp.dma_start(K.A[:, 16:24, :], K.dram["keep_yc"]).then_inc(s("reloaded").sem, s("reloaded").n(16))

    def dve(dve, t, g, slot):
        if t == 0:
            dve.wait_ge(s("reloaded").sem, s("reloaded").at(32))
        for j in range(2):
            c = 2 * t + j
            wait_bank(K, dve, g, j)
            nc.vector.tensor_tensor(K.A[:, 8 + c, :], K.A[:, 8 + c, :], K.ps[:, 2 * slot + j, :],
                                    ALU.mult).then_inc(*free_bank(K, j))
            dve.wait_ge(s(f"bank_free_{j}").sem, s(f"bank_free_{j}").at(t + 1))
            nc.vector.tensor_tensor(K.A[:, 8 + c, :], K.A[:, 8 + c, :], K.A[:, 16 + c, :], ALU.add).then_inc(
                s("y_ready").sem, s("y_ready").n())
    phase_stream(K, "gdn_out", "gdn_out", dve=dve, load=load, presplit=24)


def phase_residual(K, label, presplit, reload=True, alpha=ALPHA, stats=True, load_more=None):
    nc, s = K.nc, K.s

    def load(sp):
        if reload:
            sp.dma_start(K.A[:, 0:8, :], K.dram["keep_x"]).then_inc(s("reloaded").sem, s("reloaded").n(16))
        if load_more:
            load_more(sp)

    def dve(dve, t, g, slot):
        if t == 0 and reload:
            dve.wait_ge(s("reloaded").sem, s("reloaded").at(16))
        for j in range(2):
            c = 2 * t + j
            wait_bank(K, dve, g, j)
            nc.vector.scalar_tensor_tensor(K.A[:, c, :], K.A[:, c, :], alpha, K.ps[:, 2 * slot + j, :], ALU.mult,
                                           ALU.add).then_inc(*free_bank(K, j))
    phase_stream(K, label, label, dve=dve, load=load, presplit=presplit, stats=LayerNorm(K, 0) if stats else None,
                 wait_chunk=lambda pe, c: pe.wait_ge(s(f"bank_free_{c % 2}").sem, s(f"bank_free_{c % 2}").at(c // 2 + 1)))


def block1_mixers(K):
    phase_glu(K)
    phase_projections(K)
    phase_conv_out(K)
    phase_gdn_gates(K)
    phase_head_norm(K, "gdn_l2", [(QQ + h, "ones", GDN_DK ** -0.5) for h in range(8)] + [(KK + h, "ones", 1.0) for h in range(8)], 0)
    phase_gdn_matrices(K)
    phase_gdn_inverse(K)
    phase_gdn_tokens(K)
    phase_gdn_scan(K)

    def reload_z(sp):
        sp.dma_start(K.A[:, 0:8, :], K.dram["keep_gates"][0:8].rearrange("c p n -> p c n")).then_inc(
            K.s("reloaded").sem, K.s("reloaded").n(16))
    phase_head_norm(K, "gdn_norm", [(QQ + h, "mean128", K.vec("gdn_norm"), h) for h in range(8)], 40, after=reload_z)
    phase_gdn_out(K)

    def load_memory(sp):
        sp.dma_start(K.A[:, 48:56, 0:N_MEM], K.dram["mem_t"]).then_inc(K.s("mem_in").sem, 16)
        sp.wait_ge(K.s("mem_in").sem, 16)
    phase_residual(K, "mix_out", 8, load_more=load_memory)


def stream_pe_tokens(K, pe, names, n_tok=NT, t0=0):
    free = [K.s("bank_free_0"), K.s("bank_free_1")]
    done = [K.s("first_done"), K.s("tile_done")]

    def body(t, g, uses, slot, times):
        pe.wait_ge(K.s("lo_ready").sem, g + 1)
        whi = K.whi[:, slot, :, :].rearrange("p (j k) n -> p k j n", k=KC)
        wlo = K.wlo[:, slot, :, :].rearrange("p (j k) n -> p k j n", k=KC)
        for j in range(2):
            pe.wait_ge(free[j].sem, free[j].at(t + (t0 - 1)))
            for b in range(n_tok // 2):
                tok = slice(P * (n_tok // 2 * j + b), P * (n_tok // 2 * j + b) + P)
                out = K.ps[:, 2 * slot + j, 256 * b:256 * b + 256].rearrange("p (j n) -> p j n", n=P)
                for k in range(KC):
                    hi, lo = K.xhi[:, k, tok], K.xlo[:, k, tok]
                    K.nc.tensor.matmul(out, hi, whi[:, k], start=k == 0, stop=False)
                    K.nc.tensor.matmul(out, hi, wlo[:, k], start=False, stop=False)
                    last = K.nc.tensor.matmul(out, lo, whi[:, k], start=False, stop=k == KC - 1)
            last.then_inc(done[j].sem, 1)
    tile_loop(pe, names, body)


NMAX, SUMS, RSUM = 704, 708, 712


def phase_attention(K, label, heads, p_unit, pt_unit, load=None):
    nc, s = K.nc, K.s
    A = K.A
    groups = [(h, b) for h in range(len(heads)) for b in range(len(heads[h]["branches"]))]
    items = [(y, i) for y in range(len(groups)) for i in range(NT)]
    n = len(items)

    def br(y):
        h, b = groups[y]
        return heads[h]["branches"][b]

    def prob(x):
        return p_unit[0][:, p_unit[1] + x % 4, :]

    def turned(y, mt):
        return pt_unit[0][:, pt_unit[1] + 4 * (y % 2) + mt, :]

    def blocks(y, i):
        w = br(y)["width"](i)
        return [(m, min(P, w - P * m)) for m in range((w + P - 1) // P)]

    def out_bank(h, o):
        return 5 + (len(heads[h]["out"]) * h + o) % 3

    def col(at, x):
        return K.small[:, at + x % 4:at + x % 4 + 1]

    with nc.Block() as block:
        @block.sync
        def _(sp):
            if load:
                load(sp)

        @block.tensor
        def _(pe):
            def scores(x):
                y, i = items[x]
                w = br(y)["width"](i)
                if x >= 3:
                    pe.wait_ge(s("att_exp").sem, s("att_exp").at(x - 2))
                parts = br(y)["scores"](i)
                for p, (q, k) in enumerate(parts):
                    last = nc.tensor.matmul(K.ps[:, x % 3, :w], q, k[:, :w], start=p == 0, stop=p == len(parts) - 1)
                last.then_inc(s("att_scores").sem, s("att_scores").n())

            def turn(x):
                y, i = items[x]
                pe.wait_ge(s("att_prob").sem, s("att_prob").at(x + 1))
                if x >= 2:
                    pe.wait_ge(s("att_copied").sem, s("att_copied").at(x - 1))
                for m, w in blocks(y, i):
                    last = nc.tensor.transpose(K.ps[:w, 3 + x % 2, P * m:P * m + P], prob(x)[:, P * m:P * m + w], K.mat("ident"))
                last.then_inc(s("att_turned").sem, s("att_turned").n())

            def product(y):
                h, b = groups[y]
                head = heads[h]
                pe.wait_ge(s("att_copied").sem, s("att_copied").at(4 * y + 4))
                before = h - 1 if len(head["out"]) == 2 else h - 3
                if b == 0 and before >= 0:
                    pe.wait_ge(s("att_out").sem, s("att_out").at(before + 1))
                bl = blocks(y, NT - 1)
                for o, (rows, _) in enumerate(head["out"]):
                    for m, w in bl:
                        first = P * m if br(y)["causal"] else 0
                        last = nc.tensor.matmul(K.ps[rows, out_bank(h, o), first:], br(y)["v"](m, o), turned(y, m)[:w, first:],
                                                start=b == 0 and m == 0,
                                                stop=b == len(head["branches"]) - 1 and m == bl[-1][0])
                last.then_inc(s("att_pv").sem, s("att_pv").n())

            scores(0)
            scores(1)
            for x, (y, i) in enumerate(items):
                if x + 2 < n:
                    scores(x + 2)
                turn(x)
                if i == 0 and y >= 1:
                    product(y - 1)
            product(len(groups) - 1)

        @block.vector
        def _(dve):
            def before(x):
                y, i = items[x]
                w = br(y)["width"](i)
                dve.wait_ge(s("att_scores").sem, s("att_scores").at(x + 1))
                if br(y)["bias"]:
                    cols, bias = br(y)["bias"](i)
                    out = K.ps[:, x % 3, cols]
                    if len(bias.shape) == 3:
                        out = out.rearrange("p (r c) -> p r c", c=bias.shape[2])
                    nc.vector.tensor_tensor(out, out, bias, ALU.add).then_inc(s("att_bias").sem, s("att_bias").n())
                    dve.wait_ge(s("att_bias").sem, s("att_bias").base + s("att_bias").pending)
                nc.vector.tensor_reduce(col(NMAX, x), K.ps[:, x % 3, :w], AX.X, ALU.max, negate=True).then_inc(
                    s("att_max").sem, s("att_max").n())

            def after(x):
                y, i = items[x]
                w = br(y)["width"](i)
                step = s("att_dve")
                dve.wait_ge(s("att_exp").sem, s("att_exp").at(x + 1))
                nc.vector.reciprocal(col(RSUM, x), col(SUMS, x)).then_inc(step.sem, step.n())
                dve.wait_ge(step.sem, step.base + step.pending)
                if br(y)["gate"]:
                    nc.vector.tensor_tensor(col(RSUM, x), col(RSUM, x), br(y)["gate"](i), ALU.mult).then_inc(step.sem, step.n())
                    dve.wait_ge(step.sem, step.base + step.pending)
                if br(y)["mask"]:
                    last = nc.vector.scalar_tensor_tensor(prob(x)[:, :w], prob(x)[:, :w], col(RSUM, x), br(y)["mask"](i),
                                                          ALU.mult, ALU.mult)
                else:
                    last = nc.vector.tensor_scalar(prob(x)[:, :w], prob(x)[:, :w], col(RSUM, x), None, ALU.mult)
                last.then_inc(s("att_prob").sem, s("att_prob").n())

            def evacuate(y):
                h, b = groups[y]
                if b < len(heads[h]["branches"]) - 1:
                    return
                dve.wait_ge(s("att_pv").sem, s("att_pv").at(y + 1))
                for o, (rows, unit) in enumerate(heads[h]["out"]):
                    if "times" in heads[h]:
                        last = nc.vector.tensor_tensor(A[rows, unit, :], K.ps[rows, out_bank(h, o), :],
                                                       heads[h]["times"], ALU.mult)
                        continue
                    last = nc.vector.tensor_copy(A[rows, unit, :], K.ps[rows, out_bank(h, o), :])
                last.then_inc(s("att_out").sem, s("att_out").n())

            if load:
                dve.wait_ge(s("reloaded").sem, s("reloaded").at(16))
            before(0)
            before(1)
            for x, (y, i) in enumerate(items):
                after(x)
                if x + 2 < n:
                    before(x + 2)
                if i == 1 and y >= 1:
                    evacuate(y - 1)
            evacuate(len(groups) - 1)

        @block.scalar
        def _(act):
            def exponential(x):
                y, i = items[x]
                w = br(y)["width"](i)
                act.wait_ge(s("att_max").sem, s("att_max").at(x + 1))
                if x >= 4:
                    act.wait_ge(s("att_turned").sem, s("att_turned").at(x - 3))
                nc.scalar.activation(prob(x)[:, :w], K.ps[:, x % 3, :w], ACT.Exp, bias=col(NMAX, x),
                                     accum_out=col(SUMS, x)).then_inc(s("att_exp").sem, s("att_exp").n())

            def copy(x):
                y, i = items[x]
                bl = blocks(y, i)
                act.wait_ge(s("att_turned").sem, s("att_turned").at(x + 1))
                if i == 0 and y >= 2:
                    act.wait_ge(s("att_pv").sem, s("att_pv").at(y - 1))
                w = bl[-1][1]
                at = pt_unit[1] + 4 * (y % 2)
                nc.scalar.activation(pt_unit[0][:w, at:at + len(bl), P * i:P * i + P],
                                     K.ps[:w, 3 + x % 2, :P * len(bl)].rearrange("p (m c) -> p m c", c=P),
                                     ACT.Copy).then_inc(s("att_copied").sem, s("att_copied").n())
            exponential(0)
            exponential(1)
            for x in range(n):
                copy(x)
                if x + 2 < n:
                    exponential(x + 2)
    K.end_block(label)


def copy_evac(K, unit_of, scale=1.0, func=ACT.Copy, bias=None):
    def act(act, t, g, slot):
        for j in range(2):
            c = 2 * t + j
            unit, f, sc, b = unit_of(c)
            wait_bank(K, act, g, j)
            kw = {"bias": b} if b is not None else {}
            K.nc.scalar.activation(unit, K.ps[:, 2 * slot + j, :unit.shape[-1]], f, scale=sc, **kw).then_inc(*free_bank(K, j))
    return act


def block1_memory(K):
    nc, s = K.nc, K.s
    A = K.A
    phase_stream(K, "xk", "xk", presplit=48, width=N_MEM, pe=lambda pe: stream_pe(K, pe, "xk", n=N_MEM, split=True),
                 act=copy_evac(K, lambda c: (A[:, 16 + c, :N_MEM], ACT.Copy, 1.0, None)))

    def take_v(act, t, g, slot):
        for j in range(2):
            wait_bank(K, act, g, j)
            nc.scalar.activation(A[:, 24 + 2 * j + t // 2, 256 * (t % 2):256 * (t % 2) + 256],
                                 K.ps[:, 2 * slot + j, :256], ACT.Copy).then_inc(*free_bank(K, j))
    phase_stream(K, "xv", "xv", pe=lambda pe: stream_pe_tokens(K, pe, "xv", 2), act=take_v)
    phase_stream(K, "xq", "xq", norm=Affine(K, 0, "ln2_g", "ln2_b"), act=copy_evac(K, lambda c: (A[:, 32 + c, :], ACT.Copy, 1 / 16, None)))
    heads = []
    for h in range(XATTN_HEADS):
        heads.append({
            "out": [(slice(0, P), 40 + 2 * h), (slice(0, P), 41 + 2 * h)],
            "branches": [{
                "scores": lambda i, h=h: [(A[:, 32 + 2 * h + d, P * i:P * i + P], A[:, 16 + 2 * h + d, :]) for d in range(2)],
                "width": lambda i: N_MEM, "bias": None, "gate": None, "mask": None, "causal": False,
                "v": lambda m, o, h=h: A[:, 24 + 2 * m + h // 2, 256 * (h % 2) + P * o:256 * (h % 2) + P * o + P],
            }]})
    phase_attention(K, "xattn", heads, (A, 28), (A, 48))
    phase_residual(K, "xo", 40, reload=False)


GATE = 0
W2K, W2V = 384, 512
HID, KCMP, VCMP = 768, 1024, 1056


def phase_rms(K, label, src, dst, n, matrix, gain, split=False):
    nc, s = K.nc, K.s
    sq = K.pair
    with nc.Block() as block:
        @block.scalar
        def _(act):
            for c in range(n):
                nc.scalar.activation(sq[:, c, :], K.A[:, src + c, :], ACT.Square).then_inc(s("squared").sem, s("squared").n())
            act.wait_ge(s("var_ready").sem, s("var_ready").at(1))
            nc.scalar.activation(sq[:, 9, :], K.ps[:, 5, :], ACT.Abs_reciprocal_sqrt,
                                 bias=K.eps(RMS_EPS)).then_inc(s("rstd_ready").sem, s("rstd_ready").n())

        @block.tensor
        def _(pe):
            for c in range(n):
                pe.wait_ge(s("squared").sem, s("squared").at(c + 1))
                last = nc.tensor.matmul(K.ps[:, 5, :], K.mat(matrix), sq[:, c, :], start=c == 0, stop=c == n - 1)
            last.then_inc(s("var_ready").sem, s("var_ready").n())

        @block.vector
        def _(dve):
            dve.wait_ge(s("rstd_ready").sem, s("rstd_ready").at(1))
            for c in range(n):
                nc.vector.scalar_tensor_tensor(K.A[:, dst + c, :], K.A[:, src + c, :], K.vec(gain, c), sq[:, 9, :],
                                               ALU.mult, ALU.mult).then_inc(s("scaled").sem, s("scaled").n())
            if split:
                dve.wait_ge(s("scaled").sem, s("scaled").at(n))
                split_chunks(K, dve, dst)
    K.end_block(label)


def phase_rope(K, label, chunks, matrix, cos, sin, load=None, rows=P):
    nc, s = K.nc, K.s
    A, W = K.A, K.pair
    with nc.Block() as block:
        @block.sync
        def _(sp):
            if load:
                load(sp)

        @block.tensor
        def _(pe):
            for x, c in enumerate(chunks):
                if x >= 2:
                    pe.wait_ge(s("rope_sin").sem, s("rope_sin").at(x - 1))
                nc.tensor.matmul(K.ps[:rows, x % 2, :], K.mat(matrix)[:rows, :rows], A[:rows, c, :], start=True, stop=True).then_inc(
                    s("rope_turned").sem, s("rope_turned").n())

        @block.vector
        def _(dve):
            if load:
                dve.wait_ge(s("reloaded").sem, s("reloaded").at(16))
            for x, c in enumerate(chunks):
                dve.wait_ge(s("rope_turned").sem, s("rope_turned").at(x + 1))
                nc.vector.tensor_tensor(W[:rows, 14 + x % 2, :], K.ps[:rows, x % 2, :], sin, ALU.mult).then_inc(
                    s("rope_sin").sem, s("rope_sin").n())
                nc.vector.tensor_tensor(A[:rows, c, :], A[:rows, c, :], cos, ALU.mult).then_inc(s("rope_cos").sem, s("rope_cos").n())
                dve.wait_ge(s("rope_sin").sem, s("rope_sin").at(x + 1))
                dve.wait_ge(s("rope_cos").sem, s("rope_cos").at(x + 1))
                nc.vector.tensor_tensor(A[:rows, c, :], A[:rows, c, :], W[:rows, 14 + x % 2, :], ALU.add)
    K.end_block(label)


def phase_norm_2(K):
    nc, s = K.nc, K.s
    with nc.Block() as block:
        @block.vector
        def _(dve):
            Affine(K, 0, "ln4_g", "ln4_b", split=False).dve(dve)

        @block.scalar
        def _(act):
            Affine(K, 0, "ln4_g", "ln4_b", split=False).act(act)
            for c in range(KC):
                act.wait_ge(s("normed").sem, s("normed").at(c + 1))
                nc.scalar.activation(K.pair[:, c, :], K.A[:, c, :], ACT.Square).then_inc(s("squared").sem, s("squared").n())
            act.wait_ge(s("var_ready").sem, s("var_ready").at(1))
            nc.scalar.activation(K.ps[:, LayerNorm.FACTOR, :], K.ps[:, 5, :], ACT.Abs_reciprocal_sqrt, bias=K.eps(RMS_EPS))

        @block.tensor
        def _(pe):
            for c in range(KC):
                pe.wait_ge(s("squared").sem, s("squared").at(c + 1))
                last = nc.tensor.matmul(K.ps[:, 5, :], K.mat("mean"), K.pair[:, c, :], start=c == 0, stop=c == KC - 1)
            last.then_inc(s("var_ready").sem, s("var_ready").n())
    K.end_block("norm_2")


class Rms2:

    def __init__(self, K):
        self.K = K

    def act(self, act):
        K, s = self.K, self.K.s
        for c in range(KC):
            act.wait_ge(s("scaled").sem, s("scaled").at(c + 1))
            K.nc.scalar.activation(K.xhi[:, c, :], K.A[:, 8 + c, :], ACT.Copy).then_inc(s("normed").sem, s("normed").n())

    def dve(self, dve):
        K, s = self.K, self.K.s
        for c in range(KC + 2):
            if c < KC:
                K.nc.vector.scalar_tensor_tensor(K.A[:, 8 + c, :], K.A[:, c, :], K.vec("norm_2", c),
                                                 K.ps[:, LayerNorm.FACTOR, :], ALU.mult, ALU.mult).then_inc(
                    s("scaled").sem, s("scaled").n())
            if c >= 2:
                dve.wait_ge(s("normed").sem, s("normed").at(c - 1))
                K.nc.vector.tensor_tensor(K.xlo[:, c - 2, :], K.A[:, 6 + c, :], K.xhi[:, c - 2, :].bitcast(F32),
                                          ALU.subtract).then_inc(s("x_split").sem, s("x_split").n())


def phase_in_2(K):
    nc, s = K.nc, K.s
    A = K.A
    names = ["rqk_2", "rv_2", "mid_2", "v_2"]

    def pe(pe):
        stream_pe(K, pe, "rqk_2", split=True)
        stream_pe_tokens(K, pe, "rv_2", t0=4)
        stream_pe(K, pe, "mid_2", t0=6)
        stream_pe_tokens(K, pe, "v_2", t0=14)
        for i in range(NT):
            for k in range(KC):
                last = nc.tensor.matmul(K.ps[:, 6, 24 * i:24 * i + 24], A[:, 8 + k, P * i:P * i + P],
                                        K.small[:, 128 + 24 * k:152 + 24 * k], start=k == 0, stop=k == KC - 1)
        last.then_inc(s("gl_ready").sem, s("gl_ready").n())

    def act(act, t, g, slot):
        for j in range(2):
            wait_bank(K, act, g, j)
            bank = K.ps[:, 2 * slot + j, :]
            func, scale = ACT.Copy, 1.0
            if t in (4, 5):
                out = A[:, 24 + 2 * j:26 + 2 * j, 256 * (t - 4):256 * (t - 4) + 256]
                bank = bank.rearrange("p (b n) -> p b n", n=256)
            elif t == 14:
                out = A[:, 44 + j, :]
            else:
                c = 2 * t + j
                out = A[:, 16 + c if t < 4 else 28 + c - 12, :]
                if t in (2, 3):
                    scale = HD ** -0.5
                if t in (6, 7, 10, 11):
                    func = ACT.Silu
            nc.scalar.activation(out, bank, func, scale=scale).then_inc(*free_bank(K, j))

    def dve(dve, t, g, slot):
        if t == 14:
            dve.wait_ge(s("gl_ready").sem, s("gl_ready").at(1))
            nc.vector.tensor_tensor(K.small[:, GATE:GATE + 96].rearrange("p (i c) -> p i c", c=24),
                                    K.ps[:, 6, 0:96].rearrange("p (i c) -> p i c", c=24),
                                    K.vec("b_gate_2", 0, 24).unsqueeze(1).broadcast_to([P, NT, 24]),
                                    ALU.add)

    def compression(sp):
        load_w1(K, sp, 0, 0, A[:, 48:56, :])
        sp.dma_start(K.small[:, W2K:W2K + 256], K.dram["w2"]).then_inc(s("w2_in").sem, 16)
    phase_stream(K, "in_2", names, pe=pe, act=act, dve=dve, load_next=compression, norm=Rms2(K))


def load_w1(K, eng, kind, part, to):
    eng.dma_start(to, K.dram[("w1_k", "w1_v")[kind]][:, 16 * part:16 * part + 16, :].rearrange(
        "p (u l) n -> p u (l n)", l=2)).then_inc(K.s(f"w1_in_{2 * kind + part}").sem, 16)


def phase_compress(K):
    nc, s = K.nc, K.s
    A, W = K.A, K.pair
    w1 = [A[:, 48:56, :], W[:, 0:8, :], W[:, 8:16, :], A[:, 8:16, :]]
    PART = 8
    both = [K.ps[:2 * 32, 1 + kind, 0:256] for kind in range(2)]
    silu = [W[:2 * 32, kind, 0:256] for kind in range(2)]

    def blocks(x):
        return A[:, 46 + x % 2, :].rearrange("p (l n) -> p l n", n=2 * 32)

    def w2(kind, m):
        at = (W2K, W2V)[kind] + HD * m
        return K.small[:, at:at + HD]

    def hid(kind, m, g):
        at = HID + 128 * kind + 64 * m + 32 * g
        return K.small[:, at:at + N_CMP]
    with nc.Block() as block:
        @block.sync
        def _(sp):
            for i in range(1, 4):
                load_w1(K, sp, i // 2, i % 2, w1[i])

        @block.vector
        def _(dve):
            nc.vector.memset(A[:, 46:48, :], 0.0).then_inc(s("cmp_zero").sem, s("cmp_zero").n())
            dve.wait_ge(s("cmp_zero").sem, s("cmp_zero").at(1))
            for x in range(8):
                kind, l0 = x // 4, PART * (x % 4)
                if x >= 2:
                    dve.wait_ge(s("cmp_part").sem, s("cmp_part").at(x - 1))
                for g in range(2):
                    rows = slice(HD * g, HD * g + HD)
                    src = A[rows, 40 + kind, l0:l0 + 1]
                    windows = bass.AP(tensor=src.tensor, offset=src.offset, ap=[src.ap[0], [1, PART], [CMP_STRIDE, N_CMP]])
                    pos = K.vec(("pos_k", "pos_v")[kind], l0, PART)[rows].unsqueeze(2).broadcast_to([HD, PART, N_CMP])
                    nc.vector.tensor_tensor(blocks(x)[rows, :, 32 * g:32 * g + N_CMP], windows, pos,
                                            ALU.add).then_inc(s("cmp_blocks").sem, s("cmp_blocks").n())
            for kind in range(2):
                dve.wait_ge(s("cmp_turned").sem, s("cmp_turned").at(kind + 1))
                nc.vector.tensor_copy(K.small[:, HID + 128 * kind:HID + 128 * kind + 128],
                                      K.ps[:, 3 + kind, 0:128]).then_inc(s("cmp_hid").sem, s("cmp_hid").n())
                if kind == 0:
                    dve.wait_ge(s("cmp_rstd").sem, s("cmp_rstd").at(1))
                    nc.vector.scalar_tensor_tensor(K.small[:, KCMP:KCMP + N_CMP], K.ps[:, 5, 0:N_CMP], K.vec("k_cmp"),
                                                   W[:, 3, 0:N_CMP], ALU.mult, ALU.mult)
            dve.wait_ge(s("cmp_out").sem, s("cmp_out").at(2))
            nc.vector.tensor_copy(K.small[:N_CMP, VCMP:VCMP + 128], K.ps[:N_CMP, 6, 0:128])

        @block.scalar
        def _(act):
            nc.scalar.activation(K.small[:, GATE:GATE + 96], K.small[:, GATE:GATE + 96], ACT.Sigmoid)
            act.wait_ge(s("cmp_part").sem, s("cmp_part").at(4))
            nc.scalar.activation(silu[0], both[0], ACT.Silu).then_inc(s("cmp_silu").sem, s("cmp_silu").n())
            act.wait_ge(s("cmp_out").sem, s("cmp_out").at(1))
            nc.scalar.activation(W[:, 2, 0:N_CMP], K.ps[:, 5, 0:N_CMP], ACT.Square).then_inc(s("cmp_sq").sem, s("cmp_sq").n())
            act.wait_ge(s("cmp_part").sem, s("cmp_part").at(8))
            nc.scalar.activation(silu[1], both[1], ACT.Silu).then_inc(s("cmp_silu").sem, s("cmp_silu").n())
            act.wait_ge(s("cmp_mean").sem, s("cmp_mean").at(1))
            nc.scalar.activation(W[:, 3, 0:N_CMP], K.ps[:, 7, 0:N_CMP], ACT.Abs_reciprocal_sqrt,
                                 bias=K.eps(RMS_EPS)).then_inc(s("cmp_rstd").sem, s("cmp_rstd").n())

        @block.tensor
        def _(pe):
            def part(x):
                kind = x // 4
                if x % 2 == 0:
                    pe.wait_ge(s(f"w1_in_{x // 2}").sem, 16)
                pe.wait_ge(s("cmp_blocks").sem, s("cmp_blocks").at(2 * x + 2))
                for i in range(PART):
                    l = PART * (x % 2) + i
                    last = nc.tensor.matmul(both[kind], blocks(x)[:, i, :],
                                            w1[x // 2][:, l // 2, 256 * (l % 2):256 * (l % 2) + 256],
                                            start=x % 4 == 0 and i == 0, stop=x % 4 == 3 and i == PART - 1)
                last.then_inc(s("cmp_part").sem, s("cmp_part").n())

            def turn(kind):
                pe.wait_ge(s("cmp_silu").sem, s("cmp_silu").at(kind + 1))
                for m in range(2):
                    last = nc.tensor.transpose(K.ps[:, 3 + kind, 64 * m:64 * m + 64], silu[kind][:, P * m:P * m + P],
                                               K.mat("ident")[:2 * 32, :2 * 32])
                last.then_inc(s("cmp_turned").sem, s("cmp_turned").n())

            def second(kind):
                pe.wait_ge(s("cmp_hid").sem, s("cmp_hid").at(kind + 1))
                for g in range(2):
                    for m in range(2):
                        if kind == 0:
                            last = nc.tensor.matmul(K.ps[HD * g:HD * g + HD, 5, 0:N_CMP], w2(0, m), hid(0, m, g),
                                                    start=m == 0, stop=m == 1)
                        else:
                            last = nc.tensor.matmul(K.ps[:N_CMP, 6, HD * g:HD * g + HD], hid(1, m, g), w2(1, m),
                                                    start=m == 0, stop=m == 1)
                last.then_inc(s("cmp_out").sem, s("cmp_out").n())
            pe.wait_ge(s("w2_in").sem, 16)
            for x in range(6):
                part(x)
            turn(0)
            part(6)
            second(0)
            part(7)
            pe.wait_ge(s("cmp_sq").sem, s("cmp_sq").at(1))
            nc.tensor.matmul(K.ps[:, 7, 0:N_CMP], K.mat("mean64"), W[:, 2, 0:N_CMP], start=True, stop=True).then_inc(
                s("cmp_mean").sem, s("cmp_mean").n())
            turn(1)
            second(1)
    K.end_block("compress")


def phase_retention(K):
    nc, s = K.nc, K.s
    A, W = K.A, K.pair
    items = [(h, i) for h in range(HEADS) for i in range(NT)]
    n = len(items)

    def place(h):
        return slice(HD * (h % 2), HD * (h % 2) + HD), h // 2
    with nc.Block() as block:
        @block.sync
        def _(sp):
            sp.dma_start(A[:, 48:56, :], K.dram["decay"]).then_inc(s("reloaded").sem, s("reloaded").n(16))

        @block.tensor
        def _(pe):
            def scores(x):
                h, i = items[x]
                rows, c = place(h)
                if x >= 2:
                    pe.wait_ge(s("ret_a").sem, s("ret_a").at(x - 1))
                nc.tensor.matmul(K.ps[:, x % 2, :T - P * i], A[rows, 20 + c, P * i:P * i + P], A[rows, 16 + c, P * i:],
                                 start=True, stop=True).then_inc(s("ret_scores").sem, s("ret_scores").n())
            scores(0)
            for x, (h, i) in enumerate(items):
                rows, c = place(h)
                if x + 1 < n:
                    scores(x + 1)
                pe.wait_ge(s("ret_a").sem, s("ret_a").at(x + 1))
                if i == 0 and h >= 2:
                    pe.wait_ge(s("ret_out").sem, s("ret_out").at(h - 1))
                nc.tensor.matmul(K.ps[rows, 2 + h % 2, P * i:], A[:, 24 + i, HD * h:HD * h + HD], W[:, x % 4, :T - P * i],
                                 start=i == 0, stop=i == NT - 1).then_inc(s("ret_o").sem, s("ret_o").n())

        @block.vector
        def _(dve):
            dve.wait_ge(s("reloaded").sem, s("reloaded").at(16))
            for x, (h, i) in enumerate(items):
                dve.wait_ge(s("ret_scores").sem, s("ret_scores").at(x + 1))
                if x >= 4:
                    dve.wait_ge(s("ret_o").sem, s("ret_o").at(x - 3))
                nc.vector.tensor_tensor(W[:, x % 4, :T - P * i], K.ps[:, x % 2, :T - P * i], A[:, 48 + h, :T - P * i],
                                        ALU.mult).then_inc(s("ret_a").sem, s("ret_a").n())

        @block.scalar
        def _(act):
            for h in range(HEADS):
                rows, c = place(h)
                act.wait_ge(s("ret_o").sem, s("ret_o").at(4 * h + 4))
                nc.scalar.activation(A[rows, 8 + c, :], K.ps[rows, 2 + h % 2, :], ACT.Copy).then_inc(s("ret_out").sem, s("ret_out").n())
    K.end_block("retention")


def block2(K):
    nc, s = K.nc, K.s
    A = K.A
    phase_norm_2(K)
    phase_in_2(K)
    phase_compress(K)

    def tables(sp):
        sp.dma_start(A[:, 46:48, :], K.dram["rope_2"]).then_inc(s("reloaded").sem, s("reloaded").n(16))
    phase_rope(K, "rope_2", list(range(16, 24)), "rope64", A[:, 46, :], A[:, 47, :], tables)
    phase_retention(K)
    phase_head_norm(K, "norms_2", [(8 + c, "mean64", K.vec("ret_norm", c), 28 + c) for c in range(4)] +
                    [(32 + c, "chunk_ones", K.vec("q_norm_2")) for c in range(4)] +
                    [(42, "mean64", K.vec("k_slc")), (43, "mean64", K.vec("k_win"))], 48,
                    eps=lambda i: 64 * RMS_EPS if 4 <= i < 8 else RMS_EPS)
    masks = A[:, 46, :]

    def load(sp):
        sp.dma_start(masks[:, 0:384], K.dram["masks_2"]).then_inc(s("reloaded").sem, s("reloaded").n(16))

    def gate(b, h):
        return lambda i: K.small[:, GATE + 24 * i + 8 * b + h:GATE + 24 * i + 8 * b + h + 1]
    heads = []
    for c in range(4):
        for g in range(2):
            h, rows = c + 4 * g, slice(HD * g, HD * g + HD)

            def q(i, rows=rows, c=c):
                return A[rows, 32 + c, P * i:P * i + P]
            branches = [{
                "scores": lambda i, q=q, rows=rows: [(q(i), K.small[rows, KCMP:KCMP + N_CMP])],
                "width": lambda i: N_CMP, "causal": False, "gate": gate(0, h),
                "bias": lambda i: (slice(0, N_CMP), masks[:, 32 * i:32 * i + N_CMP]),
                "mask": lambda i: masks[:, 128 + 32 * i:128 + 32 * i + N_CMP],
                "v": lambda m, o, g=g: K.small[:N_CMP, VCMP + HD * g:VCMP + HD * g + HD],
            }]
            for b in (1, 2):
                branches.append({
                    "scores": lambda i, q=q, rows=rows, b=b: [(q(i), A[rows, 41 + b, :])],
                    "width": lambda i: P * (i + 1), "causal": True, "gate": gate(b, h), "mask": None,
                    "bias": lambda i: (slice(P * i, P * i + P), masks[:, 256:384]),
                    "v": lambda m, o, g=g, b=b: A[:, 44 + m // 2, 256 * (m % 2) + P * (b - 1) + HD * g:
                                                 256 * (m % 2) + P * (b - 1) + HD * g + HD],
                })
            heads.append({"out": [(rows, 12 + c)], "times": A[rows, 36 + c, :], "branches": branches})
    phase_attention(K, "nsa", heads, (A, 16), (A, 48), load)
    phase_residual(K, "out_2", 8, reload=False, alpha=1.0, stats=False)


def phase_mla_in(K):
    nc, s = K.nc, K.s
    A, W = K.A, K.pair
    uq = W[:, 8:11, :].rearrange("p a b -> p (a b)").rearrange("p (k n) -> p k n", k=2)
    ukv = W[:, 11:13, :].rearrange("p a b -> p (a b)")
    with nc.Block() as block:
        @block.sync
        def _(sp):
            sp.dma_start(A[:, 52:54, :], K.dram["rope_3"]).then_inc(s("reloaded").sem, s("reloaded").n(16))

        @block.tensor
        def _(pe):
            for x in range(20):
                if x >= 4:
                    pe.wait_ge(s("mla_taken").sem, s("mla_taken").at(x - 3))
                if x < 8:
                    for k in range(2):
                        last = nc.tensor.matmul(K.ps[:MLA_QK, x % 4, :], uq[:, k, MLA_QK * x:MLA_QK * x + MLA_QK],
                                                A[:, 20 + k, :], start=k == 0, stop=k == 1)
                elif x < 16:
                    last = nc.tensor.matmul(K.ps[:HD, x % 4, :], ukv[:, HD * (x - 8):HD * (x - 7)], A[:, 22, :],
                                            start=True, stop=True)
                else:
                    last = nc.tensor.matmul(K.ps[:, x % 4, :], A[:, 22, P * (x - 16):P * (x - 15)], ukv[:, 512:],
                                            start=True, stop=True)
                last.then_inc(s("mla_ready").sem, s("mla_ready").n())

        @block.scalar
        def _(act):
            for x in range(20):
                act.wait_ge(s("mla_ready").sem, s("mla_ready").at(x + 1))
                rows, unit = (MLA_QK, 8 + x) if x < 8 else (HD, 44 + x - 8) if x < 16 else (P, x)
                nc.scalar.activation(A[:rows, unit, :], K.ps[:rows, x % 4, :], ACT.Copy,
                                     scale=MLA_QK ** -0.5 if x < 8 else 1.0).then_inc(s("mla_taken").sem, s("mla_taken").n())
            act.wait_ge(s("reloaded").sem, s("reloaded").at(16))
    K.end_block("mla_in")


def phase_branches_3(K):
    nc, s = K.nc, K.s
    A = K.A

    def pe(pe):
        for t in range(4):
            g = FIRST_TILE["branches_3"] + t
            slot = g % 2
            pe.wait_ge(K.s("lo_ready").sem, g + 1)
            if t >= 2:
                pe.wait_ge(s("branch_taken").sem, s("branch_taken").at(4 * (t - 1)))
            for m in range(4):
                for k in range(4):
                    c = 4 * (t // 2) + k
                    if m == 0 and t % 2 == 0:
                        pe.wait_ge(K.s("x_split").sem, K.s("x_split").at(c + 1))
                    last = three_products(K, K.ps[:, 4 * (t % 2) + m, :], K.whi[:, slot, 4 * m + k, :],
                                          K.wlo[:, slot, 4 * m + k, :], K.xhi[:, c, :], K.xlo[:, c, :], k == 0, k == 3)
                if m in (1, 3):
                    last.then_inc(K.s(("first_done", "tile_done")[m // 2]).sem, 1)

    def dve(dve, t, g, slot):
        for m in range(4):
            wait_bank(K, dve, g, m // 2)
            c = 24 + 8 * (t // 2) + 4 * (t % 2) + m
            nc.vector.tensor_tensor(A[:, c, :], A[:, c, :], K.ps[:, 4 * (t % 2) + m, :], ALU.mult).then_inc(
                s("branch_taken").sem, s("branch_taken").n())
            if t >= 2:
                dve.wait_ge(s("branch_taken").sem, s("branch_taken").at(4 * t + m + 1))
                nc.vector.tensor_tensor(A[:, c - 8, :], A[:, c - 8, :], A[:, c, :], ALU.add)
    phase_stream(K, "branches_3", "branches_3", pe=pe, dve=dve, presplit=[40, 41, 42, 43, 8, 9, 10, 11])


def block3(K):
    nc, s = K.nc, K.s
    A = K.A
    names = ["qk_3", "v_3", "rest_3"]

    def pe(pe):
        stream_pe(K, pe, "qk_3", split=True)
        stream_pe_tokens(K, pe, "v_3", t0=4)
        stream_pe(K, pe, "rest_3", t0=6)

    def act(act, t, g, slot):
        for j in range(2):
            wait_bank(K, act, g, j)
            bank = K.ps[:, 2 * slot + j, :]
            c = 2 * t + j
            if t in (4, 5):
                out = A[:, 16 + 2 * j:18 + 2 * j, 256 * (t - 4):256 * (t - 4) + 256]
                nc.scalar.activation(out, bank.rearrange("p (b n) -> p b n", n=256), ACT.Copy).then_inc(*free_bank(K, j))
            elif t < 8:
                nc.scalar.activation(A[:, 8 + c, :], bank, ACT.Copy, scale=HD ** -0.5 if t < 2 else 1.0).then_inc(*free_bank(K, j))
            else:
                nc.scalar.activation(A[:, 8 + c, :], bank, ACT.Sigmoid, bias=K.vec("b_gate_3", c - 16)).then_inc(*free_bank(K, j))
    phase_stream(K, "in_3", names, pe=pe, act=act, presplit=0)

    def load(sp):
        sp.dma_start(A[:, 40:54, :], K.dram["na_bias"]).then_inc(s("reloaded").sem, s("reloaded").n(16))
    table = A[:, 40:54, :].rearrange("p a b -> p (a b)").rearrange("p (h j c) -> p h j c", h=HEADS, c=GRID_W)
    heads = []
    for h in range(HEADS):
        rows, c = slice(HD * (h % 2), HD * (h % 2) + HD), h // 2
        heads.append({"out": [(rows, 40 + c)], "branches": [{
            "scores": lambda i, rows=rows, c=c: [(A[rows, 8 + c, P * i:P * i + P], A[rows, 12 + c, :])],
            "width": lambda i: T, "causal": False, "gate": None, "mask": None,
            "bias": lambda i, h=h: (slice(0, T), table[:, h, 6 - 2 * i:14 - 2 * i, :]),
            "v": lambda m, o, h=h: A[:, 16 + m, HD * h:HD * h + HD],
        }]})
    phase_attention(K, "na", heads, (K.pair, 8), (K.pair, 0), load)

    phase_rms(K, "mla_q_norm", 20, 20, 2, "mean256", "mla_q")
    phase_rms(K, "mla_kv_norm", 22, 22, 1, "mean128", "mla_kv")
    with nc.Block() as block:
        @block.sync
        def _(sp):
            sp.dma_start(K.pair[:, 8:13, :], K.dram["mla_w"]).then_inc(s("reloaded").sem, s("reloaded").n(16))
            sp.wait_ge(s("reloaded").sem, s("reloaded").at(16))
    K.end_block("mla_w")
    phase_mla_in(K)
    phase_rope(K, "rope_3", list(range(8, 16)) + [23], "rope32", A[:MLA_QK, 52, :], A[:MLA_QK, 53, :], rows=MLA_QK)
    with nc.Block() as block:
        @block.vector
        def _(dve):
            for h in range(HEADS):
                nc.vector.tensor_copy(A[HD:MLA_QK, 44 + h, :], A[HD:MLA_QK, 23, :])
    K.end_block("mla_k")
    heads = []
    for h in range(HEADS):
        rows, c = slice(HD * (h % 2), HD * (h % 2) + HD), h // 2
        heads.append({"out": [(rows, 8 + c)], "branches": [{
            "scores": lambda i, h=h: [(A[:MLA_QK, 8 + h, P * i:P * i + P], A[:MLA_QK, 44 + h, :])],
            "width": lambda i: T, "causal": False, "gate": None, "mask": None, "bias": None,
            "v": lambda m, o, h=h: A[:, 16 + m, HD * h:HD * h + HD],
        }]})
    phase_attention(K, "mla", heads, (K.pair, 8), (K.pair, 0))
    phase_branches_3(K)
    phase_residual(K, "out_3", 24, reload=False)
    phase_ffn_in(K, "ffn3_in", 1.0, norm=Affine(K, 0, "ln1_g_3", "ln1_b_3"))
    phase_ffn_out(K, "ffn3_out")


def program(nc, dram):
    ctx = ExitStack()
    with ctx:
        K = Kernel(nc, ctx, dram)
        try:
            phase_start(K)
            phase_ffn_in(K, "ffn1_in")
            phase_ffn_out(K, "ffn1_out")
            block1_mixers(K)
            block1_memory(K)
            phase_ffn_in(K, "ffn2_in", norm=Affine(K, 0, "ln3_g", "ln3_b"))
            phase_ffn_out(K, "ffn2_out")
            block2(K)
            block3(K)
        except StopIteration:
            pass
        last = Affine(K, 0, "ln2_g_3", "ln2_b_3", split=False)
        with nc.Block() as block:
            @block.vector
            def _(dve):
                if "dbg" not in dram or STOP_AFTER == "ln2_3":
                    last.dve(dve)

            @block.scalar
            def _(act):
                if "dbg" not in dram or STOP_AFTER == "ln2_3":
                    last.act(act)

            @block.sync
            def _(sp):
                if "dbg" in dram:
                    if STOP_AFTER == "ln2_3":
                        sp.wait_ge(K.s("normed").sem, K.s("normed").at(KC))
                    sp.dma_start(dram["dbg"], K.A[:, DBG[0]:DBG[1], :]).then_inc(K.s("stored").sem, 16)
                    sp.wait_ge(K.s("stored").sem, 16)
                else:
                    for c in range(KC):
                        sp.wait_ge(K.s("normed").sem, K.s("normed").at(c + 1))
                        sp.dma_start(dram["out"][:, c, :], K.A[:, c, :]).then_inc(K.s("stored").sem, 16)
                    sp.wait_ge(K.s("stored").sem, 16 * KC)



def columns(w):
    k, m = w.shape
    return w.reshape(k // P, P, m // (2 * P), 2, P).transpose(2, 1, 3, 0, 4).reshape(-1, P, 16, P)


def pairs(wa, wb):
    k, m = wa.shape
    both = np.stack([w.reshape(k // P, P, m // P, P) for w in (wa, wb)])
    return both.transpose(3, 2, 0, 1, 4).reshape(-1, P, 16, P)


def rows(w):
    k, m = w.shape
    return w.reshape(k // (2 * P), 2, P, KC, P).transpose(0, 2, 1, 3, 4).reshape(-1, P, 16, P)


def halves(w):
    return w.reshape(4, P, 2, 4, P).transpose(2, 1, 3, 0, 4).reshape(-1, P, 16, P)


NSA_ORDER = np.concatenate([np.arange(HD * h, HD * h + HD) for c in range(4) for h in (c, c + 4)])
ORDER_2 = np.concatenate([np.arange(0, 2048), 2048 + NSA_ORDER, 2560 + NSA_ORDER, np.arange(3072, 3328),
                          np.arange(3328, 3456), np.arange(3584, 3712), np.arange(3456, 3584), np.arange(3712, 3840)])
ROWS_OUT_2 = np.concatenate([np.arange(0, 512), 512 + NSA_ORDER])


def rope_table(position, half):
    f, t = np.arange(P), np.arange(T)
    inv = 10000.0 ** (-(f % half).astype(np.float64) / half)
    angle = position(f[:, None], t[None, :]) * inv[:, None]
    return np.stack([np.cos(angle), np.sin(angle)], axis=1).astype(np.float32)


def tables():
    t = np.arange(T)
    decay = np.zeros((P, HEADS, T))
    p, x = np.arange(P)[:, None], t[None, :]
    for h in range(HEADS):
        decay[:, h, :] = np.where(x >= p, (1.0 - 2.0 ** (-5.0 - h)) ** np.maximum(x - p, 0).astype(np.float64), 0.0)
    masks = np.zeros((P, 384), np.float32)
    end = np.arange(N_CMP) * CMP_STRIDE + CMP_BLOCK - 1
    for i in range(NT):
        ok = end[None, :] <= (P * i + np.arange(P))[:, None]
        masks[:, 32 * i:32 * i + N_CMP] = np.where(ok, 0.0, NEG)
        masks[:, 128 + 32 * i:128 + 32 * i + N_CMP] = ok
    masks[:, 256:384] = np.where(np.arange(P)[None, :] <= np.arange(P)[:, None], 0.0, NEG)
    return {
        "rope_2": rope_table(lambda f, t: t + 0 * f, HD // 2),
        "rope_3": rope_table(lambda f, t: np.where(f < HD, 0, np.where(f // 16 % 2 == 0, t // GRID_W, t % GRID_W)), 8),
        "decay": decay.astype(np.float32), "masks_2": masks,
    }


def na_table(rpb):
    q, j, c = np.arange(P)[:, None, None], np.arange(1, 15)[None, :, None], np.arange(GRID_W)[None, None, :]
    row, col = q // GRID_W, q % GRID_W
    start = np.clip(col - NA_WIN_COLS // 2, 0, GRID_W - NA_WIN_COLS)
    inside = (c >= start) & (c < start + NA_WIN_COLS)
    taken = rpb[:, np.broadcast_to(j - row, (P, 14, GRID_W)), np.clip(c - col + NA_WIN_COLS - 1, 0, 30) + 0 * j]
    return np.where(inside[None], taken, np.float32(NEG)).transpose(1, 0, 2, 3).reshape(P, 14, T)


def per_feature(v):
    return v.reshape(-1, P).T


def feature_major(x):
    return x.T.reshape(-1, P, x.shape[0]).transpose(1, 0, 2)


def matrices():
    m = np.zeros((len(MATRICES), P, P), np.float32)
    i, j = np.meshgrid(np.arange(P), np.arange(P), indexing="ij")
    same = i // CHUNK == j // CHUNK
    m[MAT["ident"]] = i == j
    m[MAT["mean"]] = 1.0 / D
    m[MAT["ones"]] = 1.0
    m[MAT["mean128"]] = 1.0 / P
    m[MAT["mean256"]] = 1.0 / 256
    m[MAT["mean64"]] = (i // HD == j // HD) / HD
    m[MAT["chunk_tri"]] = same & (i <= j)
    m[MAT["chunk_strict"]] = same & (i < j)
    m[MAT["chunk_ones"]] = same
    for s in (1, 2, 4, 8, 16, 32):
        m[MAT[f"level{s}"]] = (i // (2 * s) == j // (2 * s)) & (i // s % 2 == 0) & (j // s % 2 == 1)
    for name, half, off, group in (("rope64", 32, 0, 64), ("rope32", 8, 0, 16)):
        r = np.zeros((P, P), np.float32)
        for o in range(P):
            w = o % group
            if w < half:
                r[o + half, o] = -1.0
            else:
                r[o - half, o] = 1.0
        m[MAT[name]] = r
    return m.transpose(1, 0, 2)


def kernel(**inputs):
    import concourse.bacc as bacc
    from concourse.bass_utils import run_bass_kernel_spmd as run

    w = {k: np.asarray(v)[0] if k != "mem" else np.asarray(v) for k, v in inputs.items()}
    win = w["w_in"]
    in_3 = w["w_in_3"]
    in_3 = np.concatenate([in_3[:, :1920]] + 4 * [in_3[:, 1920:1952]] + [in_3[:, 1952:]], axis=1)
    tiles = [
        pairs(w["ffn1_wg"], w["ffn1_wu"]), rows(w["ffn1_wd"]),
        pairs(win[:, 4112:5136], win[:, 5136:6160]), columns(win[:, 0:3072]), columns(win[:, 3072:4096]),
        columns(win[:, 6160:8208]), columns(w["w_conv_out"]), columns(w["w_gdn_out"]), columns(w["w_mix_out"]),
        columns(w["w_xkv"]), columns(w["w_xq"]), columns(w["w_xo"]),
        pairs(w["ffn2_wg"], w["ffn2_wu"]), rows(w["ffn2_wd"]),
        columns(w["w_in_2"][:, :3840][:, ORDER_2]), columns(w["w_out_2"][ROWS_OUT_2]),
        columns(in_3), halves(w["w_branch_na_3"]), halves(w["w_branch_mla_3"]), columns(w["w_out_3"]),
        pairs(w["w_ffn_in_3"][:, :DFF], w["w_ffn_in_3"][:, DFF:]), rows(w["w_ffn_out_3"]),
    ]
    stream = np.concatenate(tiles)
    parts = {}
    for n in ("ln1", "ln2", "ln3", "ln4"):
        parts[n + "_g"], parts[n + "_b"] = per_feature(w[n + "_g"]), per_feature(w[n + "_b"])
    parts["gdn_conv"] = w["gdn_conv_qkv"].reshape(4, 24, P).transpose(2, 1, 0).reshape(P, 96)
    parts["gdn_norm"] = per_feature(w["gdn_norm_g"])
    parts["conv_w"] = w["conv_dw_w"].reshape(31, 8, P).transpose(2, 0, 1).reshape(P, 248)
    for n, source in (("conv_b", "conv_dw_b"), ("conv_ln_g", "conv_ln_g"), ("conv_ln_b", "conv_ln_b"),
                      ("b_conv_out", "b_conv_out")):
        parts[n] = per_feature(w[source])
    for n, source in (("a_log", "gdn_a_log"), ("dt_bias", "gdn_dt_bias"), ("b_gate_2", "b_gate_2")):
        parts[n] = np.broadcast_to(w[source], (P, w[source].size))
    parts["eps"] = np.broadcast_to(np.array([LN_EPS, RMS_EPS, 1.0, 64 * RMS_EPS], np.float32), (P, 4))
    small = np.concatenate([
        win[:, 4096:4112].reshape(KC, P, 16).transpose(1, 0, 2).reshape(P, 128),
        w["w_in_2"][:, 3840:3864].reshape(KC, P, 24).transpose(1, 0, 2).reshape(P, 192)], axis=1)
    parts["norm_2"] = per_feature(w["norm_w_2"])
    parts["ret_norm"] = per_feature(w["ret_norm_w_2"])
    for n, source in (("q_norm_2", "q_norm_w_2"), ("k_cmp", "k_norm_cmp_2"), ("k_slc", "k_norm_slc_2"), ("k_win", "k_norm_win_2")):
        parts[n] = per_feature(np.tile(w[source], 2))
    parts["pos_k"], parts["pos_v"] = np.tile(w["cmp_pos_k_2"].T, (2, 1)), np.tile(w["cmp_pos_v_2"].T, (2, 1))
    parts["b_gate_3"] = per_feature(w["b_gate_3"])
    parts["mla_q"], parts["mla_kv"] = per_feature(w["mla_q_norm_3"]), per_feature(w["mla_kv_norm_3"])
    for n in ("ln1_g_3", "ln1_b_3", "ln2_g_3", "ln2_b_3"):
        parts[n] = per_feature(w[n])
    vecs = np.concatenate([parts[n] for n, k in VECTORS], axis=1)
    uq = w["mla_w_uq_3"]
    ukv = w["mla_w_ukv_3"].reshape(P, HEADS, 2, HD).transpose(0, 2, 1, 3).reshape(P, 1024)
    mla_w = np.concatenate([uq.reshape(2, P, 768).transpose(1, 0, 2).reshape(P, 1536), ukv], axis=1).reshape(P, 5, T)
    more = tables()
    for n in ("k", "v"):
        more["w1_" + n] = np.tile(w[f"cmp_w1_{n}_2"].reshape(CMP_BLOCK, HD, CMP_HIDDEN).transpose(1, 0, 2), (2, 1, 1))
    more["w2"] = np.concatenate([w[f"cmp_w2_{n}_2"].reshape(2, P, HD).transpose(1, 0, 2).reshape(P, P) for n in ("k", "v")], axis=1)
    more["mla_w"], more["na_bias"] = mla_w, na_table(w["na_rpb_3"])
    arrays = {
        **more, "x_t": feature_major(w["x"]), "stream": stream, "vecs": vecs, "mats": matrices(), "small": small, "mem_t": feature_major(w["mem"][0]),
    }
    nc = bacc.Bacc("TRN2", target_bir_lowering=False, num_devices=1)
    arrays = {k: np.ascontiguousarray(v) for k, v in arrays.items()}
    dram = {k: nc.dram_tensor("in_" + k, v.shape, F32, kind="ExternalInput").ap() for k, v in arrays.items()}
    dram["out"] = nc.dram_tensor("out_t", (P, KC, T), F32, kind="ExternalOutput").ap()
    if STOP_AFTER:
        dram["dbg"] = nc.dram_tensor("dbg", (P, DBG[1] - DBG[0], T), F32, kind="ExternalOutput").ap()
    dram["keep_x"] = nc.dram_tensor("keep_x", (P, KC, T), F32, kind="Internal").ap()
    dram["keep_yc"] = nc.dram_tensor("keep_yc", (P, KC, T), F32, kind="Internal").ap()
    dram["keep_gates"] = nc.dram_tensor("keep_gates", (24, P, T), F32, kind="Internal").ap()
    program(nc, dram)
    r = run(nc, [{"in_" + k: v for k, v in arrays.items()}], core_ids=[0])
    y = np.asarray(r.results[0]["out_t"])
    return y.transpose(2, 1, 0).reshape(1, T, D)
```

```python
import numpy as np

import concourse.bass as bass
from concourse import mybir

F32 = mybir.dt.float32
F32R = mybir.dt.float32r
ACT = mybir.ActivationFunctionType
ALU = mybir.AluOpType
AX = mybir.AxisListType

P = 128
T = 512
D = 1024
KC = D // P
NT = T // P
DFF = 2816
FC = DFF // P
N_MEM = 256
ALPHA = 2.0 ** 0.25
LN_EPS = 1e-5
RMS_EPS = 1e-6
NEG = -1e30

GDN_HEADS = 8
GDN_DK = 128
CHUNK = 64
SHORT_CONV = 4
CONV_WIDTH = 31
XATTN_HEADS = 4

HEADS = 8
HD = 64
CMP_BLOCK = 32
CMP_STRIDE = 16
N_CMP = (T - CMP_BLOCK) // CMP_STRIDE + 1
CMP_HIDDEN = 256
GRID_W = 64
NA_ROWS = T // GRID_W
NA_WIN_ROWS = 8
NA_WIN_COLS = 16
MLA_QK = 96

STREAM = [
    ("ffn1_in", 22), ("ffn1_out", 11),
    ("glu", 8), ("qkv", 12), ("z", 4), ("gates", 8), ("conv_out", 4), ("gdn_out", 4), ("mix_out", 4),
    ("xk", 4), ("xv", 4), ("xq", 4), ("xo", 4),
    ("ffn2_in", 22), ("ffn2_out", 11),
    ("rqk_2", 4), ("rv_2", 2), ("mid_2", 8), ("v_2", 1), ("out_2", 4),
    ("qk_3", 4), ("v_3", 2), ("rest_3", 10), ("branches_3", 4), ("out_3", 4),
    ("ffn3_in", 22), ("ffn3_out", 11),
]
FIRST_TILE, TILES = {}, {}
N_TILES = 0
for _name, _n in STREAM:
    FIRST_TILE[_name], TILES[_name] = N_TILES, _n
    N_TILES += _n

VECTORS = [
    ("ln1_g", 8), ("ln1_b", 8), ("ln2_g", 8), ("ln2_b", 8), ("ln3_g", 8), ("ln3_b", 8), ("ln4_g", 8), ("ln4_b", 8),
    ("gdn_conv", 4 * 24), ("gdn_norm", 1), ("conv_w", 31 * 8), ("conv_b", 8), ("conv_ln_g", 8), ("conv_ln_b", 8),
    ("b_conv_out", 8),
    ("norm_2", 8), ("ret_norm", 4), ("q_norm_2", 1), ("k_cmp", 1), ("k_slc", 1), ("k_win", 1),
    ("pos_k", 32), ("pos_v", 32),
    ("b_gate_3", 16), ("mla_q", 2), ("mla_kv", 1), ("ln1_g_3", 8), ("ln1_b_3", 8), ("ln2_g_3", 8), ("ln2_b_3", 8),
    ("a_log", 8), ("dt_bias", 8), ("b_gate_2", 24), ("eps", 4),
]
VEC, N_VEC = {}, 0
for _name, _n in VECTORS:
    VEC[_name] = N_VEC
    N_VEC += _n

MATRICES = ["ident", "mean", "ones", "mean128", "mean64", "chunk_tri", "chunk_strict", "chunk_ones",
            "level1", "level2", "level4", "level8", "level16", "level32", "rope64", "rope32", "mean256"]
MAT = {n: i for i, n in enumerate(MATRICES)}


class Signal:

    def __init__(self, sem):
        self.sem, self.base, self.pending, self.times = sem, 0, 0, 1

    def at(self, n):
        return n + self.base

    def n(self, by=1, times=1):
        self.pending += by * times
        return by


class Kernel:
    def __init__(self, nc, dram):
        self.nc, self.dram = nc, dram
        self.signals = {}
        at = (nc.sbuf_base + 63) // 64 * 64

        def place(name, shape, dt, offset):
            return nc.alloc_sbuf_tensor_at(name, shape, dt, offset=offset)

        tile = 16 * P * 4
        self.raw = place("weights_raw", [P, 2, 16, P], F32, at)
        self.whi = place("weights_hi", [P, 2, 16, P], F32R, at + 2 * tile)
        self.wlo = place("weights_lo", [P, 2, 16, P], F32R, at + 4 * tile)
        at += 6 * tile
        self.xhi = place("x_hi", [P, KC, T], F32R, at)
        self.xlo = place("x_lo", [P, KC, T], F32R, at + KC * T * 4)
        self.pair = place("pair_scratch", [P, 2 * KC, T], F32, at)
        at += 2 * KC * T * 4
        self.A = place("arena", [P, 56, T], F32, at)
        self.hhi = place("h_hi", [P, FC, T], F32R, at + 8 * T * 4)
        self.hlo = place("h_lo", [P, FC, T], F32R, at + (8 + FC) * T * 4)
        at += 56 * T * 4
        self.mats = place("mats", [P, len(MATRICES), P], F32, at)
        at += len(MATRICES) * P * 4
        self.vecs = place("vecs", [P, N_VEC], F32, at)
        at += (N_VEC * 4 + 31) // 32 * 32
        self.small = place("small", [P, 1184], F32, at)
        at += 1184 * 4
        assert at <= nc.sbuf_usable_end
        self.ps = nc.alloc_psum_tensor("psum", [P, 8, 512], F32)

    def s(self, name):
        if name not in self.signals:
            self.signals[name] = Signal(self.nc.alloc_semaphore(name))
        return self.signals[name]

    def eps(self, value):
        return self.vec("eps", {LN_EPS: 0, RMS_EPS: 1, 1.0: 2, 64 * RMS_EPS: 3}[value])

    def mat(self, name):
        return self.mats[:, MAT[name], :]

    def vec(self, name, c=0, n=1):
        return self.vecs[:, VEC[name] + c:VEC[name] + c + n]

    def end_block(self):
        for s in self.signals.values():
            s.base += s.pending
            s.pending = 0


def span(names):
    names = [names] if isinstance(names, str) else names
    return FIRST_TILE[names[0]], sum(TILES[n] for n in names)


def tile_loop(eng, names, body, unroll=False, peeled=0):
    first, n = span(names)
    pairs = (n - peeled - 2) // 2
    done = peeled
    if pairs >= 2 and not unroll:
        with eng.Fori(0, pairs) as i:
            for j in range(2):
                g = first + peeled + j
                body(2 * i + (peeled + j), 2 * i + g, i + (g // 2 + 1), g % 2, pairs)
        done += 2 * pairs
    for t in range(done, n):
        g = first + t
        body(t, g, g // 2 + 1, g % 2, 1)



def stream_load(K, sp, name):
    raw_loaded, lo_ready = [K.s("raw_loaded_0"), K.s("raw_loaded_1")], K.s("lo_ready")

    def body(t, g, uses, slot, times):
        if isinstance(g, int) and g + 2 >= N_TILES:
            return
        sp.wait_ge(lo_ready.sem, g + 1)
        sp.dma_start(K.raw[:, slot, :, :], K.dram["stream"][bass.ds(g + 2, 1) if not isinstance(g, int)
                                                           else slice(g + 2, g + 3)].rearrange(
            "a p k n -> (a p) k n")).then_inc(raw_loaded[slot].sem, 16)
    tile_loop(sp, name, body)


def split_hi(K, act, g, uses, slot, times):
    if isinstance(g, int) and g >= N_TILES:
        return
    act.wait_ge(K.s(f"raw_loaded_{slot}").sem, uses * 16)
    if not isinstance(g, int) or g >= 2:
        act.wait_ge(K.s("tile_done").sem, g - 1)
    K.nc.scalar.activation(K.whi[:, slot, :, :], K.raw[:, slot, :, :], ACT.Copy).then_inc(K.s("hi_ready").sem, 1)


def stream_split_lo(K, pool, name):
    def body(t, g, uses, slot, times):
        if isinstance(g, int) and g + 1 >= N_TILES:
            return
        pool.wait_ge(K.s("hi_ready").sem, g + 2)
        K.nc.gpsimd.tensor_tensor(K.wlo[:, 1 - slot, :, :], K.raw[:, 1 - slot, :, :],
                                  K.whi[:, 1 - slot, :, :].bitcast(F32),
                                  ALU.subtract).then_inc(K.s("lo_ready").sem, 1)
    tile_loop(pool, name, body)


def stream_act(K, act, name, evac=None, unroll=False):
    def body(t, g, uses, slot, times):
        split_hi(K, act, g + 1, uses + slot, 1 - slot, times)
        if evac:
            evac(t, g, slot, times)
    tile_loop(act, name, body, unroll)


def stream_dve(K, dve, name, evac, unroll=False):
    tile_loop(dve, name, lambda t, g, uses, slot, times: evac(t, g, slot, times), unroll)


def three_products(K, out, whi, wlo, xhi, xlo, start, stop):
    K.nc.tensor.matmul(out, whi, xhi, start=start, stop=False)
    K.nc.tensor.matmul(out, whi, xlo, start=False, stop=False)
    return K.nc.tensor.matmul(out, wlo, xhi, start=False, stop=stop)


def stream_pe(K, pe, name, n=T, t0=0, split=False):
    xhi, xlo = K.xhi, K.xlo
    free = [K.s("bank_free_0"), K.s("bank_free_1")]
    done = [K.s("first_done"), K.s("tile_done")]

    def body(t, g, uses, slot, times):
        pe.wait_ge(K.s("lo_ready").sem, g + 1)
        for j in range(2):
            pe.wait_ge(free[j].sem, free[j].at(t + (t0 - 1)))
            for k in range(KC):
                last = three_products(K, K.ps[:, 2 * slot + j, :n], K.whi[:, slot, 8 * j + k, :],
                                      K.wlo[:, slot, 8 * j + k, :], xhi[:, k, :n], xlo[:, k, :n],
                                      k == 0, k == KC - 1)
            last.then_inc(done[j].sem, 1)

    if split:
        g = span(name)[0]
        slot = g % 2
        pe.wait_ge(K.s("lo_ready").sem, g + 1)
        for j in range(2):
            pe.wait_ge(free[j].sem, free[j].at(t0 - 1))
        for k in range(KC):
            pe.wait_ge(K.s("x_split").sem, K.s("x_split").at(k + 1))
            for j in range(2):
                last = three_products(K, K.ps[:, 2 * slot + j, :n], K.whi[:, slot, 8 * j + k, :],
                                      K.wlo[:, slot, 8 * j + k, :], xhi[:, k, :n], xlo[:, k, :n],
                                      k == 0, k == KC - 1)
                if k == KC - 1:
                    last.then_inc(done[j].sem, 1)
    tile_loop(pe, name, body, peeled=int(split))


def wait_bank(K, eng, g, j):
    eng.wait_ge(K.s(("first_done", "tile_done")[j]).sem, g + 1)



def phase_start(K):
    nc, dram = K.nc, K.dram
    with nc.Block() as block:
        @block.sync
        def _(sp):
            sp.dma_start(K.raw[:, 0, :, :], dram["stream"][0]).then_inc(K.s("raw_loaded_0").sem, 16)
            for i in range(2):
                sp.dma_start(K.A[:, 4 * i:4 * i + 4, :], dram["x_t"][:, 4 * i:4 * i + 4, :]).then_inc(K.s(f"x_in_{i}").sem, 16)
            sp.dma_start(K.raw[:, 1, :, :], dram["stream"][1]).then_inc(K.s("raw_loaded_1").sem, 16)
            sp.dma_start(K.vecs[:, :], dram["vecs"]).then_inc(K.s("loaded").sem, 16)
            sp.dma_start(K.mats[:, :, :], dram["mats"]).then_inc(K.s("loaded").sem, 16)
            sp.dma_start(K.small[:, 0:320], dram["small"]).then_inc(K.s("loaded").sem, 16)

        @block.scalar
        def _(act):
            split_hi(K, act, 0, 1, 0, 1)
            nc.scalar.nop().then_inc(K.s("bank_free_0").sem, K.s("bank_free_0").n(2))

        @block.vector
        def _(dve):
            nc.vector.nop().then_inc(K.s("bank_free_1").sem, K.s("bank_free_1").n(2))
    K.end_block()


class FirstSplit:

    def __init__(self, K):
        self.K = K

    def pool(self, pool):
        K = self.K
        pool.wait_ge(K.s("hi_ready").sem, 1)
        K.nc.gpsimd.tensor_tensor(K.wlo[:, 0, :, :], K.raw[:, 0, :, :], K.whi[:, 0, :, :].bitcast(F32),
                                  ALU.subtract).then_inc(K.s("lo_ready").sem, 1)

    def act(self, act):
        pass

    def dve(self, dve):
        for i in range(2):
            dve.wait_ge(self.K.s(f"x_in_{i}").sem, 16)
        split_chunks(self.K, dve, 0)


def split_chunks(K, dve, unit, n=KC, width=T):
    s = K.s("x_hi_done")
    units = unit if isinstance(unit, list) else [unit + c for c in range(n)]
    for c in range(n + 1):
        if c < n:
            K.nc.vector.tensor_copy(K.xhi[:, c, :width], K.A[:, units[c], :width]).then_inc(s.sem, s.n())
        if c == 0:
            continue
        c -= 1
        dve.wait_ge(s.sem, s.at(c + 1))
        K.nc.vector.tensor_tensor(K.xlo[:, c, :width], K.A[:, units[c], :width],
                                  K.xhi[:, c, :width].bitcast(F32), ALU.subtract).then_inc(
            K.s("x_split").sem, K.s("x_split").n())


def phase_ffn_in(K, name, weight=0.5, norm=None):
    nc = K.nc
    silu, h_ready, hhi_ready = K.s("silu_ready"), K.s("h_ready"), K.s("h_hi_ready")
    sg, h = K.A[:, 52:54, :], K.A[:, 54:56, :]
    with nc.Block() as block:
        @block.sync
        def _(sp):
            stream_load(K, sp, name)
            if isinstance(norm, FirstSplit):
                sp.wait_ge(K.s("loaded").sem, 48)

        @block.gpsimd
        def _(pool):
            if norm:
                norm.pool(pool)
            stream_split_lo(K, pool, name)

        @block.tensor
        def _(pe):
            stream_pe(K, pe, name, split=norm is not None)

        @block.scalar
        def _(act):
            if norm:
                norm.act(act)

            def evac(t, g, slot, times):
                wait_bank(K, act, g, 0)
                nc.scalar.activation(sg[:, slot, :], K.ps[:, 2 * slot, :], ACT.Silu).then_inc(silu.sem, silu.n(1, times))
            stream_act(K, act, name, evac)

        @block.vector
        def _(dve):
            if norm:
                norm.dve(dve)

            def evac(t, g, slot, times):
                wait_bank(K, dve, g, 1)
                dve.wait_ge(silu.sem, silu.at(t + 1))
                nc.vector.scalar_tensor_tensor(h[:, slot, :], sg[:, slot, :], weight, K.ps[:, 2 * slot + 1, :],
                                               ALU.mult, ALU.mult).then_inc(h_ready.sem, h_ready.n(1, times))
                dve.wait_ge(h_ready.sem, h_ready.at(t + 1))
                nc.vector.nop().then_inc(K.s("bank_free_0").sem, K.s("bank_free_0").n(1, times))
                nc.vector.nop().then_inc(K.s("bank_free_1").sem, K.s("bank_free_1").n(1, times))
                at = bass.ds(t, 1) if not isinstance(t, int) else slice(t, t + 1)
                nc.vector.tensor_copy(K.hhi[:, at, :], h[:, slot:slot + 1, :]).then_inc(hhi_ready.sem, hhi_ready.n(1, times))
                dve.wait_ge(hhi_ready.sem, hhi_ready.at(t + 1))
                nc.vector.tensor_tensor(K.hlo[:, at, :], h[:, slot:slot + 1, :], K.hhi[:, at, :].bitcast(F32),
                                        ALU.subtract)
            stream_dve(K, dve, name, evac)
    K.end_block()


def phase_ffn_out(K, name):
    nc, s = K.nc, K.s
    norm = LayerNorm(K, 0, lambda eng, c: eng.wait_ge(s("sum_taken").sem, s("sum_taken").at(c + 1)),
                     K.pair[:, 8:12, :], mean_bank=0, var_bank=1)
    with nc.Block() as block:
        @block.sync
        def _(sp):
            stream_load(K, sp, name)

        @block.gpsimd
        def _(pool):
            stream_split_lo(K, pool, name)
            norm.stats_pool(pool)

        @block.scalar
        def _(act):
            stream_act(K, act, name)
            norm.stats_act(act)

        @block.tensor
        def _(pe):
            def body(t, g, uses, slot, times):
                pe.wait_ge(K.s("lo_ready").sem, g + 1)
                for j in range(2):
                    f = bass.ds(2 * t + j, 1) if not isinstance(t, int) else slice(2 * t + j, 2 * t + j + 1)
                    for m in range(KC):
                        last = three_products(K, K.ps[:, m:m + 1, :], K.whi[:, slot, 8 * j + m, :],
                                              K.wlo[:, slot, 8 * j + m, :], K.hhi[:, f, :], K.hlo[:, f, :],
                                              isinstance(t, int) and t == 0 and j == 0,
                                              isinstance(t, int) and t == TILES[name] - 1 and j == 1)
                        if isinstance(t, int) and t == TILES[name] - 1 and j == 1 and m < KC - 1:
                            last.then_inc(s("sum_ready").sem, s("sum_ready").n())
                    last.then_inc(K.s(("first_done", "tile_done")[j]).sem, 1)
            n, first = TILES[name], FIRST_TILE[name]
            body(0, first, 0, first % 2, 1)
            loops = (n - 3) // 2
            with pe.Fori(0, loops) as i:
                for j in range(2):
                    body(2 * i + (1 + j), 2 * i + (first + 1 + j), 0, (first + 1 + j) % 2, loops)
            for t in range(1 + 2 * loops, n):
                body(t, first + t, 0, (first + t) % 2, 1)
            norm.stats_pe(pe)

        @block.vector
        def _(dve):
            for m in range(KC):
                if m < KC - 1:
                    dve.wait_ge(s("sum_ready").sem, s("sum_ready").at(m + 1))
                else:
                    wait_bank(K, dve, FIRST_TILE[name] + TILES[name] - 1, 1)
                nc.vector.scalar_tensor_tensor(K.A[:, m, :], K.A[:, m, :], ALPHA, K.ps[:, m, :], ALU.mult,
                                               ALU.add).then_inc(s("sum_taken").sem, s("sum_taken").n())
            norm.stats_dve(dve)
    K.end_block()


class LayerNorm:
    FACTOR = 7

    def __init__(self, K, src, wait_chunk, scratch, mean_bank=4, var_bank=5):
        self.K, self.src, self.mean_bank, self.var_bank = K, src, mean_bank, var_bank
        self.wait_chunk = wait_chunk
        self.sums = scratch

    def stats_pool(self, pool):
        s = self.K.s
        for p in range(KC // 2):
            for c in (2 * p, 2 * p + 1):
                self.wait_chunk(pool, c)
            self.K.nc.gpsimd.tensor_tensor(self.sums[:, p, :], self.K.A[:, self.src + 2 * p, :],
                                           self.K.A[:, self.src + 2 * p + 1, :], ALU.add).then_inc(
                s("pair_summed").sem, s("pair_summed").n())

    def stats_pe(self, pe):
        K, s = self.K, self.K.s
        for p in range(KC // 2):
            pe.wait_ge(s("pair_summed").sem, s("pair_summed").at(p + 1))
            last = K.nc.tensor.matmul(K.ps[:, self.mean_bank, :], K.mat("mean"), self.sums[:, p, :],
                                      start=p == 0, stop=p == KC // 2 - 1)
        last.then_inc(s("mean_ready").sem, s("mean_ready").n())
        for c in range(KC):
            pe.wait_ge(s("squared").sem, s("squared").at(c + 1))
            last = K.nc.tensor.matmul(K.ps[:, self.var_bank, :], K.mat("mean"), K.pair[:, c, :], start=c == 0,
                                      stop=c == KC - 1)
        last.then_inc(s("var_ready").sem, s("var_ready").n())

    def stats_act(self, act):
        K, s = self.K, self.K.s
        for c in range(KC):
            act.wait_ge(s("centred").sem, s("centred").at(c + 1))
            K.nc.scalar.activation(K.pair[:, c, :], K.A[:, self.src + c, :], ACT.Square).then_inc(
                s("squared").sem, s("squared").n())
        act.wait_ge(s("var_ready").sem, s("var_ready").at(1))
        K.nc.scalar.activation(K.ps[:, self.FACTOR, :], K.ps[:, self.var_bank, :], ACT.Abs_reciprocal_sqrt,
                               bias=K.eps(LN_EPS))

    def stats_dve(self, dve):
        K, s = self.K, self.K.s
        dve.wait_ge(s("mean_ready").sem, s("mean_ready").at(1))
        for c in range(KC):
            K.nc.vector.tensor_tensor(K.A[:, self.src + c, :], K.A[:, self.src + c, :], K.ps[:, self.mean_bank, :],
                                      ALU.subtract).then_inc(s("centred").sem, s("centred").n())


def split_one(K, dve, c, unit, ready, n):
    dve.wait_ge(ready.sem, ready.at(n))
    K.nc.vector.tensor_copy(K.xhi[:, c, :], K.A[:, unit, :]).then_inc(K.s("x_hi_done").sem, K.s("x_hi_done").n())


def split_lows(K, pool, first_unit):
    for c in range(KC):
        pool.wait_ge(K.s("x_hi_done").sem, K.s("x_hi_done").at(c + 1))
        K.nc.gpsimd.tensor_tensor(K.xlo[:, c, :], K.A[:, first_unit + c, :], K.xhi[:, c, :].bitcast(F32),
                                  ALU.subtract).then_inc(K.s("x_split").sem, K.s("x_split").n())


class Affine:

    def __init__(self, K, src, g, b, func=ACT.Identity, split=True):
        self.K, self.src, self.g, self.b, self.func, self.split = K, src, g, b, func, split

    def act(self, act):
        K, s = self.K, self.K.s
        for c in range(KC):
            act.wait_ge(s("scaled").sem, s("scaled").at(c + 1))
            x = K.A[:, self.src + c, :]
            K.nc.scalar.activation(x, x, self.func, bias=K.vec(self.b, c), scale=K.vec(self.g, c)).then_inc(
                s("normed").sem, s("normed").n())

    def dve(self, dve):
        K, s = self.K, self.K.s
        for c in range(KC + 2):
            if c < KC:
                x = K.A[:, self.src + c, :]
                K.nc.vector.tensor_tensor(x, x, K.ps[:, LayerNorm.FACTOR, :], ALU.mult).then_inc(
                    s("scaled").sem, s("scaled").n())
            if self.split and c >= 2:
                split_one(K, dve, c - 2, self.src + c - 2, s("normed"), c - 1)

    def pool(self, pool):
        split_lows(self.K, pool, self.src)


def phase_stream(K, label, names, pe=None, act=None, dve=None, load=None, load_next=None, pe_last=None, presplit=None, width=T,
                 norm=None, stats=None, beside=None):
    with K.nc.Block() as block:
        @block.sync
        def _(sp):
            if load:
                load(sp)
            stream_load(K, sp, names)
            if load_next:
                load_next(sp)

        @block.gpsimd
        def _(pool):
            if norm:
                norm.pool(pool)
            stream_split_lo(K, pool, names)
            if stats:
                stats.stats_pool(pool)

        @block.tensor
        def _(pe_):
            if pe:
                pe(pe_)
            else:
                stream_pe(K, pe_, names, split=presplit is not None or norm is not None)
            if pe_last:
                pe_last(pe_)
            if beside:
                beside.pe_last(pe_)
            if stats:
                stats.stats_pe(pe_)

        @block.scalar
        def _(act_):
            if norm:
                norm.act(act_)
            stream_act(K, act_, names, act and (lambda t, g, slot, times: act(act_, t, g, slot)), True)
            if beside:
                beside.act_last(act_)
            if stats:
                stats.stats_act(act_)

        @block.vector
        def _(dve_):
            if presplit is not None:
                split_chunks(K, dve_, presplit, width=width)
            if norm:
                norm.dve(dve_)
            if beside:
                beside.dve_first(dve_)
            if dve:
                stream_dve(K, dve_, names, lambda t, g, slot, times: dve(dve_, t, g, slot), True)
            if beside:
                beside.dve_last(dve_)
            if stats:
                stats.stats_dve(dve_)
    K.end_block()


def free_bank(K, j):
    s = K.s(f"bank_free_{j}")
    return s.sem, s.n()


def phase_glu(K):
    nc, s = K.nc, K.s
    sg = K.A[:, 48:50, :]

    def act(act, t, g, slot):
        if t == 0:
            act.wait_ge(s("normed").sem, s("normed").at(KC))
            act.dma_start(K.dram["keep_x"], K.A[:, 0:8, :]).then_inc(s("spilled").sem, s("spilled").n(16))
        wait_bank(K, act, g, 1)
        if t >= 2:
            act.wait_ge(s("glu_ready").sem, s("glu_ready").at(t - 1))
        nc.scalar.activation(sg[:, slot, :], K.ps[:, 2 * slot + 1, :], ACT.Sigmoid).then_inc(s("sigmoid").sem, s("sigmoid").n())

    def dve(dve, t, g, slot):
        wait_bank(K, dve, g, 0)
        dve.wait_ge(s("sigmoid").sem, s("sigmoid").at(t + 1))
        nc.vector.tensor_tensor(K.A[:, 8 + t, :], K.ps[:, 2 * slot, :], sg[:, slot, :],
                                ALU.mult).then_inc(s("glu_ready").sem, s("glu_ready").n())
        dve.wait_ge(s("glu_ready").sem, s("glu_ready").at(t + 1))
        nc.vector.nop().then_inc(*free_bank(K, 0))
        nc.vector.nop().then_inc(*free_bank(K, 1))

    def pe_last(pe):
        for i in range(NT):
            for k in range(KC):
                last = nc.tensor.matmul(K.ps[:, 6, 16 * i:16 * i + 16], K.A[:, k, P * i:P * i + P],
                                        K.small[:, 16 * k:16 * k + 16], start=k == 0, stop=k == KC - 1)
        last.then_inc(s("ab_ready").sem, s("ab_ready").n())
        pe.wait_ge(s("spilled").sem, s("spilled").at(16))
    phase_stream(K, "glu", "glu", act=act, dve=dve, pe_last=pe_last, norm=Affine(K, 0, "ln1_g", "ln1_b"))


AB, G, BETA, GC, BG, KD, EGL, T1 = 320, 384, 416, 448, 480, 512, 544, 608


def phase_projections(K):
    nc, s = K.nc, K.s
    tmp = K.A[:, 48:56, :]
    names = ["qkv", "z", "gates"]

    def act(act, t, g, slot):
        for j in range(2):
            c = 2 * t + j
            if t < 12:
                act.wait_ge(s("short_done").sem, s("short_done").at(4 * (c + 1)))
                nc.scalar.activation(K.A[:, 24 + c, :], tmp[:, 2 * slot + j, :], ACT.Silu).then_inc(
                    s("qkv_ready").sem, s("qkv_ready").n())
            else:
                u = c - 24
                wait_bank(K, act, g, j)
                if u >= 4:
                    act.wait_ge(s(f"spilled_{u % 4}").sem, s(f"spilled_{u % 4}").at(16 * (u // 4)))
                nc.scalar.activation(tmp[:, 4 + u % 4, :], K.ps[:, 2 * slot + j, :],
                                     ACT.Silu if t < 16 else ACT.Sigmoid).then_inc(
                    s("gate_ready").sem, s("gate_ready").n())
                act.wait_ge(s("gate_ready").sem, s("gate_ready").at(u + 1))
                act.dma_start(K.dram["keep_gates"][u], tmp[:, 4 + u % 4, :]).then_inc(
                    s(f"spilled_{u % 4}").sem, s(f"spilled_{u % 4}").n(16))
        if t == 23:
            for r in range(4):
                act.wait_ge(s(f"spilled_{r}").sem, s(f"spilled_{r}").at(16 * 6))

    def long_conv():
        acc, src = 16, 8
        done = s("long_done")
        n = 0
        for tap in range(CONV_WIDTH - 1, -1, -1):
            back = CONV_WIDTH - 1 - tap
            for c in range(KC):
                w = K.vec("conv_w", 8 * tap + c)
                if back == 0:
                    nc.vector.tensor_scalar(K.A[:, acc + c, :], K.A[:, src + c, :], w, K.vec("conv_b", c),
                                            ALU.mult, ALU.add).then_inc(done.sem, done.n())
                else:
                    nc.vector.wait_ge(done.sem, done.at(n - KC + 1))
                    nc.vector.scalar_tensor_tensor(K.A[:, acc + c, back:], K.A[:, src + c, :T - back], w,
                                                   K.A[:, acc + c, back:], ALU.mult, ALU.add).then_inc(done.sem, done.n())
                n += 1
                yield

    conv = long_conv()

    def dve(dve, t, g, slot):
        if t < 12:
            short = s("short_done")
            for j in range(2):
                c = 2 * t + j
                bank, acc = K.ps[:, 2 * slot + j, :], tmp[:, 2 * slot + j, :]
                wait_bank(K, dve, g, j)
                if t >= 2:
                    dve.wait_ge(s("qkv_ready").sem, s("qkv_ready").at(c - 3))
                for tap in range(SHORT_CONV - 1, -1, -1):
                    back = SHORT_CONV - 1 - tap
                    w = K.vec("gdn_conv", 4 * c + tap)
                    if back == 0:
                        nc.vector.tensor_scalar(acc, bank, w, None, ALU.mult).then_inc(short.sem, short.n())
                    else:
                        dve.wait_ge(short.sem, short.at(4 * c + back))
                        nc.vector.scalar_tensor_tensor(acc[:, back:], bank[:, :T - back], w, acc[:, back:],
                                                       ALU.mult, ALU.add).then_inc(short.sem, short.n())
                dve.wait_ge(short.sem, short.at(4 * c + 4))
                nc.vector.nop().then_inc(*free_bank(K, j))
        else:
            for j in range(2):
                dve.wait_ge(s("gate_ready").sem, s("gate_ready").at(2 * t + j - 23))
                nc.vector.nop().then_inc(*free_bank(K, j))
        for _ in range(7 if t < 12 else 15):
            next(conv, None)
    phase_stream(K, "projections", names, act=act, dve=dve, stats=LayerNorm(
        K, 16, lambda eng, c: eng.wait_ge(s("long_done").sem, s("long_done").at(KC * (CONV_WIDTH - 1) + c + 1)),
        K.A[:, 8:12, :]))


def phase_conv_out(K):
    nc, s = K.nc, K.s

    def load(sp):
        sp.dma_start(K.A[:, 0:8, :], K.dram["keep_gates"][16:24].rearrange("c p n -> p c n")).then_inc(
            s("reloaded").sem, s("reloaded").n(16))

    def dve(dve, t, g, slot):
        if t == 0:
            dve.wait_ge(s("reloaded").sem, s("reloaded").at(16))
        for j in range(2):
            c = 2 * t + j
            wait_bank(K, dve, g, j)
            nc.vector.scalar_tensor_tensor(K.A[:, 8 + c, :], K.ps[:, 2 * slot + j, :], K.vec("b_conv_out", c),
                                           K.A[:, c, :], ALU.add, ALU.mult).then_inc(*free_bank(K, j))
    gates = GdnGates(K)
    phase_stream(K, "conv_out", "conv_out", dve=dve, load=load, beside=gates,
                 act=lambda act, t, g, slot: gates.act_first(act) if t == 0 else None,
                 norm=Affine(K, 16, "conv_ln_g", "conv_ln_b", ACT.Silu))


class GdnGates:

    def __init__(self, K):
        self.K, self.a_in = K, K.ps[:, 6, 0:64].rearrange("p (i c) -> p i c", c=16)

    def f(self, at, n=32):
        return self.K.small[:, at:at + n]

    def th(self, at):
        return self.K.small[:, at:at + 32].rearrange("p (i h) -> p i h", h=GDN_HEADS)

    def link(self, dve, ins, n):
        step = self.K.s("gates_dve")
        ins.then_inc(step.sem, step.n())
        dve.wait_ge(step.sem, step.at(n))

    def dve_first(self, dve):
        K, f, th, link, v = self.K, self.f, self.th, self.link, self.K.nc.vector
        s = K.s
        row = K.vec("dt_bias", 0, 8).unsqueeze(1).broadcast_to([P, NT, 8])
        link(dve, v.tensor_tensor(th(T1), self.a_in[:, :, 0:8], row, ALU.add), 1)
        link(dve, v.tensor_scalar(f(T1 + 32), f(T1), -1.0, None, ALU.mult), 2)
        link(dve, v.tensor_tensor(f(T1 + 32), f(T1), f(T1 + 32), ALU.min), 3)
        dve.wait_ge(s("gates_act").sem, s("gates_act").at(2))
        link(dve, v.scalar_tensor_tensor(f(T1), f(T1), 0.0, f(T1 + 64), ALU.max, ALU.add), 4)
        row = f(T1 + 96, 8).unsqueeze(1).broadcast_to([P, NT, 8])
        dve.wait_ge(s("gates_act").sem, s("gates_act").at(3))
        link(dve, v.tensor_tensor(th(G), th(T1), row, ALU.mult), 5)
        link(dve, v.tensor_scalar(f(G), f(G), -1.0, None, ALU.mult), 6)

    def dve_last(self, dve):
        K, f, link, v = self.K, self.f, self.link, self.K.nc.vector
        s = K.s
        dve.wait_ge(s("gates_pe").sem, s("gates_pe").at(1))
        link(dve, v.tensor_copy(f(GC), K.ps[:, 5, 0:32]), 7)
        link(dve, v.tensor_tensor(f(KD), K.ps[:, 5, 32:64], f(GC), ALU.subtract), 8)
        dve.wait_ge(s("gates_act").sem, s("gates_act").at(5))
        link(dve, v.tensor_tensor(f(BG), f(BG), f(BETA), ALU.mult), 9)

    def act_first(self, act):
        K, f, a = self.K, self.f, self.K.nc.scalar
        done, dve_done = K.s("gates_act"), K.s("gates_dve")
        act.wait_ge(dve_done.sem, dve_done.at(3))
        a.activation(f(T1 + 32), f(T1 + 32), ACT.Exp).then_inc(done.sem, done.n())
        act.wait_ge(done.sem, done.at(1))
        a.activation(f(T1 + 64), f(T1 + 32), ACT.Ln, bias=K.eps(1.0)).then_inc(done.sem, done.n())
        a.activation(f(T1 + 96, 8), K.vec("a_log", 0, 8), ACT.Exp).then_inc(done.sem, done.n())
        a.activation(self.th(BETA), self.a_in[:, :, 8:16], ACT.Sigmoid).then_inc(done.sem, done.n())

    def act_last(self, act):
        K, f, a = self.K, self.f, self.K.nc.scalar
        done, dve_done = K.s("gates_act"), K.s("gates_dve")
        act.wait_ge(dve_done.sem, dve_done.at(7))
        a.activation(f(BG), f(GC), ACT.Exp).then_inc(done.sem, done.n())
        act.wait_ge(dve_done.sem, dve_done.at(8))
        a.activation(f(KD), f(KD), ACT.Exp).then_inc(done.sem, done.n())

    def pe_last(self, pe):
        K = self.K
        pe.wait_ge(K.s("gates_dve").sem, K.s("gates_dve").at(6))
        K.nc.tensor.matmul(K.ps[:, 5, 0:32], K.mat("chunk_tri"), self.f(G), start=True, stop=True)
        K.nc.tensor.matmul(K.ps[:, 5, 32:64], K.mat("chunk_ones"), self.f(G), start=True, stop=True).then_inc(
            K.s("gates_pe").sem, K.s("gates_pe").n())


def phase_head_norm(K, label, items, scratch, eps=RMS_EPS, after=None, store=False):
    nc, s = K.nc, K.s
    n = len(items)
    sq, rstd = K.A[:, scratch:scratch + 2, :], K.A[:, scratch + 2:scratch + 4, :]
    with nc.Block() as block:
        @block.scalar
        def _(act):
            def square(i):
                if i >= 2:
                    act.wait_ge(s("norm_sum").sem, s("norm_sum").at(i - 1))
                nc.scalar.activation(sq[:, i % 2, :], K.A[:, items[i][0], :], ACT.Square).then_inc(
                    s("norm_sq").sem, s("norm_sq").n())
            square(0)
            for i in range(n):
                if i + 1 < n:
                    square(i + 1)
                act.wait_ge(s("norm_sum").sem, s("norm_sum").at(i + 1))
                if i >= 2:
                    act.wait_ge(s("norm_out").sem, s("norm_out").at(i - 1))
                nc.scalar.activation(rstd[:, i % 2, :], K.ps[:, i % 4, :], ACT.Abs_reciprocal_sqrt,
                                     bias=K.eps(eps(i) if callable(eps) else eps)).then_inc(s("norm_rstd").sem, s("norm_rstd").n())

        @block.tensor
        def _(pe):
            for i in range(n):
                pe.wait_ge(s("norm_sq").sem, s("norm_sq").at(i + 1))
                if i >= 4:
                    pe.wait_ge(s("norm_rstd").sem, s("norm_rstd").at(i - 3))
                nc.tensor.matmul(K.ps[:, i % 4, :], K.mat(items[i][1]), sq[:, i % 2, :], start=True,
                                 stop=True).then_inc(s("norm_sum").sem, s("norm_sum").n())

        @block.sync
        def _(sp):
            if after:
                after(sp)
            if store:
                sp.dma_start(K.dram["keep_yc"], K.A[:, 8:16, :]).then_inc(s("spilled").sem, s("spilled").n(16))
                sp.wait_ge(s("spilled").sem, s("spilled").at(16))

        @block.vector
        def _(dve):
            for i, (c, _, gain, *times) in enumerate(items):
                dve.wait_ge(s("norm_rstd").sem, s("norm_rstd").at(i + 1))
                nc.vector.scalar_tensor_tensor(K.A[:, c, :], K.A[:, c, :], gain, rstd[:, i % 2, :], ALU.mult,
                                               ALU.mult).then_inc(s("norm_out").sem, s("norm_out").n())
                if times:
                    if i == 0 and after:
                        dve.wait_ge(s("reloaded").sem, s("reloaded").at(16))
                    dve.wait_ge(s("norm_out").sem, s("norm_out").at(i + 1))
                    nc.vector.tensor_tensor(K.A[:, c, :], K.A[:, c, :], K.A[:, times[0], :], ALU.mult)
    K.end_block()


def tiles_of(ap):
    return ap.rearrange("p (i n) -> p i n", n=P)


def over_tiles(ap):
    return ap.unsqueeze(1).broadcast_to([P, NT, P])


def per_token(K, at, h):
    return K.small[:, at:at + 32].rearrange("p (i h) -> p i h", h=8)[:, :, h:h + 1].broadcast_to([P, NT, P])


UU, AT, MT, TT, QQ, KK, VV = 0, 8, 16, 48, 24, 32, 40


def phase_gdn_matrices(K):
    nc, s = K.nc, K.s
    A, W = K.A, K.pair

    def w(kind, h):
        return W[:, 2 * kind + h % 2, :]
    TRI, DIAG, DEC, EXPG, MD = range(5)
    with nc.Block() as block:
        @block.gpsimd
        def _(pool):
            def first(h):
                if h >= 2:
                    pool.wait_ge(s("mat_prod").sem, s("mat_prod").at(h - 1))
                nc.gpsimd.tensor_tensor(tiles_of(w(TRI, h)), over_tiles(K.mat("chunk_tri")), per_token(K, G, h),
                                        ALU.mult).then_inc(s("mat_in").sem, s("mat_in").n())
                nc.gpsimd.tensor_tensor(tiles_of(w(DIAG, h)), over_tiles(K.mat("ident")), per_token(K, BETA, h),
                                        ALU.mult).then_inc(s("mat_in").sem, s("mat_in").n())
            first(0)
            first(1)
            for h in range(GDN_HEADS):
                if h + 2 < GDN_HEADS:
                    first(h + 2)
                pool.wait_ge(s("mat_prod").sem, s("mat_prod").at(h + 1))
                pool.wait_ge(s("mat_exp").sem, s("mat_exp").at(2 * h + 2))
                nc.gpsimd.tensor_tensor(A[:, QQ + h, :], A[:, QQ + h, :], w(EXPG, h), ALU.mult).then_inc(
                    s("mat_q").sem, s("mat_q").n())

        @block.vector
        def _(dve):
            step = s("mat_dve")
            state = [0]

            def link(ins):
                ins.then_inc(step.sem, step.n())
                state[0] += 1

            def settle():
                dve.wait_ge(step.sem, step.at(state[0]))

            def decay(h):
                dve.wait_ge(s("mat_sum").sem, s("mat_sum").at(h + 1))
                link(nc.vector.tensor_tensor(tiles_of(w(DEC, h)), tiles_of(K.ps[:, 4 * (h % 2), :]), per_token(K, GC, h), ALU.subtract))
                settle()
                link(nc.vector.tensor_scalar(w(DEC, h), w(DEC, h), 0.0, None, ALU.min))
                settle()
                nc.vector.nop().then_inc(s("mat_dec").sem, s("mat_dec").n())
            decay(0)
            for h in range(GDN_HEADS):
                b = 4 * (h % 2)
                if h + 1 < GDN_HEADS:
                    decay(h + 1)
                dve.wait_ge(s("mat_prod").sem, s("mat_prod").at(h + 1))
                dve.wait_ge(s("mat_exp").sem, s("mat_exp").at(2 * h + 2))
                link(nc.vector.tensor_tensor(tiles_of(w(DEC, h)), tiles_of(w(DEC, h)), over_tiles(K.mat("chunk_tri")), ALU.mult))
                settle()
                link(nc.vector.tensor_tensor(A[:, AT + h, :], w(DEC, h), K.ps[:, b + 3, :], ALU.mult))
                link(nc.vector.tensor_tensor(w(MD, h), w(DEC, h), K.ps[:, b + 1, :], ALU.mult))
                settle()
                link(nc.vector.tensor_tensor(A[:, MT + h, :], w(MD, h), K.ps[:, b + 2, :], ALU.mult))
                settle()
                link(nc.vector.tensor_tensor(tiles_of(w(MD, h)), tiles_of(A[:, MT + h, :]), over_tiles(K.mat("level1")), ALU.mult))
                settle()
                link(nc.vector.tensor_tensor(tiles_of(A[:, UU + h, :]), over_tiles(K.mat("ident")), tiles_of(w(MD, h)), ALU.subtract))
                settle()
                nc.vector.nop().then_inc(s("mat_u").sem, s("mat_u").n())

        @block.scalar
        def _(act):
            def take_t(h):
                act.wait_ge(s("mat_t").sem, s("mat_t").at(h + 1))
                nc.scalar.activation(A[:, TT + h, :], K.ps[:, 4 * (h % 2) + 3, :], ACT.Copy).then_inc(s("mat_tc").sem, s("mat_tc").n())
            for h in range(GDN_HEADS):
                b = 4 * (h % 2)
                act.wait_ge(s("mat_dec").sem, s("mat_dec").at(h + 1))
                nc.scalar.activation(w(DEC, h), w(DEC, h), ACT.Exp).then_inc(s("mat_exp").sem, s("mat_exp").n())
                if h >= 2:
                    act.wait_ge(s("mat_q").sem, s("mat_q").at(h - 1))
                nc.scalar.activation(w(EXPG, h), K.ps[:, b, :], ACT.Exp).then_inc(s("mat_exp").sem, s("mat_exp").n())
                nc.scalar.activation(K.small[:, EGL + 8 * h:EGL + 8 * h + 8],
                                     K.ps[:, b, :].rearrange("p (n c) -> p n c", c=CHUNK)[:, :, CHUNK - 1],
                                     ACT.Exp).then_inc(s("mat_egl").sem, s("mat_egl").n())
                if h >= 1:
                    take_t(h - 1)
            take_t(GDN_HEADS - 1)

        @block.tensor
        def _(pe):
            def sums(h):
                if h >= 2:
                    pe.wait_ge(s("mat_egl").sem, s("mat_egl").at(h - 1))
                pe.wait_ge(s("mat_in").sem, s("mat_in").at(2 * h + 1))
                nc.tensor.matmul(K.ps[:, 4 * (h % 2), :], K.mat("ones"), w(TRI, h), start=True, stop=True).then_inc(
                    s("mat_sum").sem, s("mat_sum").n())

            def products(h):
                b = 4 * (h % 2)
                if h >= 2:
                    pe.wait_ge(s("mat_tc").sem, s("mat_tc").at(h - 1))
                pe.wait_ge(s("mat_in").sem, s("mat_in").at(2 * h + 2))
                nc.tensor.matmul(K.ps[:, b + 1, :], K.mat("ones"), w(DIAG, h), start=True, stop=True)
                for i in range(NT):
                    t = slice(P * i, P * i + P)
                    nc.tensor.matmul(K.ps[:, b + 2, t], A[:, KK + h, t], A[:, KK + h, t], start=True, stop=True)
                    last = nc.tensor.matmul(K.ps[:, b + 3, t], A[:, KK + h, t], A[:, QQ + h, t], start=True, stop=True)
                last.then_inc(s("mat_prod").sem, s("mat_prod").n())
            for h in range(2):
                sums(h)
                products(h)
            for h in range(GDN_HEADS):
                if h + 2 < GDN_HEADS:
                    sums(h + 2)
                pe.wait_ge(s("mat_u").sem, s("mat_u").at(h + 1))
                for i in range(NT):
                    t = slice(P * i, P * i + P)
                    last = nc.tensor.transpose(K.ps[:, 4 * (h % 2) + 3, t], A[:, UU + h, t], K.mat("ident"))
                last.then_inc(s("mat_t").sem, s("mat_t").n())
                if h + 2 < GDN_HEADS:
                    products(h + 2)
    K.end_block()


def phase_gdn_inverse(K):
    nc, s = K.nc, K.s
    A, W = K.A, K.pair
    items = [(level, h) for level in (2, 4, 8, 16, 32) for h in range(GDN_HEADS)]
    n = len(items)
    with nc.Block() as block:
        @block.gpsimd
        def _(pool):
            for x, (level, h) in enumerate(items):
                if x >= 3:
                    pool.wait_ge(s("inv_lt").sem, s("inv_lt").at(x - 2))
                nc.gpsimd.tensor_tensor(tiles_of(W[:, x % 3, :]), tiles_of(A[:, MT + h, :]),
                                        over_tiles(K.mat(f"level{level}")), ALU.mult).then_inc(s("inv_mask").sem, s("inv_mask").n())

        @block.vector
        def _(dve):
            for x, (level, h) in enumerate(items):
                dve.wait_ge(s("inv_tlt").sem, s("inv_tlt").at(x + 1))
                if level < 32:
                    nc.vector.tensor_tensor(A[:, TT + h, :], A[:, TT + h, :], K.ps[:, 2 + x % 2, :], ALU.subtract)
                nc.vector.tensor_tensor(A[:, UU + h, :], A[:, UU + h, :], K.ps[:, 4 + x % 2, :],
                                        ALU.subtract).then_inc(s("inv_done").sem, s("inv_done").n())

        @block.scalar
        def _(act):
            for x in range(n):
                act.wait_ge(s("inv_lt").sem, s("inv_lt").at(x + 1))
                if x >= 2:
                    act.wait_ge(s("inv_tlt").sem, s("inv_tlt").at(x - 1))
                nc.scalar.activation(W[:, 3 + x % 2, :], K.ps[:, x % 2, :], ACT.Copy).then_inc(s("inv_copy").sem, s("inv_copy").n())

        @block.tensor
        def _(pe):
            def lt(x):
                level, h = items[x]
                pe.wait_ge(s("inv_mask").sem, s("inv_mask").at(x + 1))
                if x >= 8:
                    pe.wait_ge(s("inv_done").sem, s("inv_done").at(x - 7))
                if x >= 2:
                    pe.wait_ge(s("inv_copy").sem, s("inv_copy").at(x - 1))
                for i in range(NT):
                    t = slice(P * i, P * i + P)
                    last = nc.tensor.matmul(K.ps[:, x % 2, t], W[:, x % 3, t], A[:, TT + h, t], start=True, stop=True)
                last.then_inc(s("inv_lt").sem, s("inv_lt").n())
            lt(0)
            for x, (level, h) in enumerate(items):
                if x + 1 < n:
                    lt(x + 1)
                pe.wait_ge(s("inv_copy").sem, s("inv_copy").at(x + 1))
                if x >= 2:
                    pe.wait_ge(s("inv_done").sem, s("inv_done").at(x - 1))
                for i in range(NT):
                    t = slice(P * i, P * i + P)
                    if level < 32:
                        nc.tensor.matmul(K.ps[:, 2 + x % 2, t], A[:, UU + h, t], W[:, 3 + x % 2, t], start=True, stop=True)
                    last = nc.tensor.matmul(K.ps[:, 4 + x % 2, t], W[:, 3 + x % 2, t], A[:, UU + h, t], start=True, stop=True)
                last.then_inc(s("inv_tlt").sem, s("inv_tlt").n())
    K.end_block()


def phase_gdn_tokens(K):
    nc, s = K.nc, K.s
    A, W = K.A, K.pair
    with nc.Block() as block:
        @block.tensor
        def _(pe):
            def turn(h):
                b = 3 * (h % 2)
                if h >= 2:
                    pe.wait_ge(s("tok_scaled").sem, s("tok_scaled").at(h - 1))
                for i in range(NT):
                    t = slice(P * i, P * i + P)
                    nc.tensor.transpose(K.ps[:, b, t], A[:, VV + h, t], K.mat("ident"))
                    last = nc.tensor.transpose(K.ps[:, b + 1, t], A[:, KK + h, t], K.mat("ident"))
                last.then_inc(s("tok_turned").sem, s("tok_turned").n())
            turn(0)
            for h in range(GDN_HEADS):
                if h + 1 < GDN_HEADS:
                    turn(h + 1)
                pe.wait_ge(s("tok_scaled").sem, s("tok_scaled").at(h + 1))
                if h >= 2:
                    pe.wait_ge(s("tok_w").sem, s("tok_w").at(h - 1))
                for i in range(NT):
                    t = slice(P * i, P * i + P)
                    last = nc.tensor.matmul(K.ps[:, 3 * (h % 2) + 2, t], W[:, h % 2, t], A[:, UU + h, t], start=True, stop=True)
                last.then_inc(s("tok_wt").sem, s("tok_wt").n())

        @block.vector
        def _(dve):
            for h in range(GDN_HEADS):
                b = 3 * (h % 2)
                dve.wait_ge(s("tok_turned").sem, s("tok_turned").at(h + 1))
                if h >= 2:
                    dve.wait_ge(s("tok_wt").sem, s("tok_wt").at(h - 1))
                nc.vector.tensor_tensor(tiles_of(A[:, VV + h, :]), tiles_of(K.ps[:, b, :]), per_token(K, BETA, h), ALU.mult)
                nc.vector.tensor_tensor(tiles_of(W[:, h % 2, :]), tiles_of(K.ps[:, b + 1, :]), per_token(K, BG, h), ALU.mult)
                nc.vector.tensor_tensor(tiles_of(A[:, MT + h, :]), tiles_of(K.ps[:, b + 1, :]), per_token(K, KD, h),
                                        ALU.mult).then_inc(s("tok_scaled").sem, s("tok_scaled").n())

        @block.scalar
        def _(act):
            for h in range(GDN_HEADS):
                act.wait_ge(s("tok_wt").sem, s("tok_wt").at(h + 1))
                nc.scalar.activation(A[:, KK + h, :], K.ps[:, 3 * (h % 2) + 2, :], ACT.Copy, scale=-1.0).then_inc(
                    s("tok_w").sem, s("tok_w").n())
    K.end_block()


def phase_gdn_scan(K):
    nc, s = K.nc, K.s
    A, W = K.A, K.pair
    state = A[:, TT:TT + 2, :].rearrange("p u (h n) -> p (u h) n", n=P)
    items = [(n, grp) for n in range(T // CHUNK) for grp in range(2)]
    with nc.Block() as block:
        @block.vector
        def _(dve):
            nc.vector.memset(A[:, TT:TT + 2, :], 0.0).then_inc(s("scan_zero").sem, s("scan_zero").n())
            dve.wait_ge(s("scan_zero").sem, s("scan_zero").at(1))
            for x, (n, grp) in enumerate(items):
                dve.wait_ge(s("scan_kv").sem, s("scan_kv").at(x + 1))
                for hh in range(4):
                    h = 4 * grp + hh
                    last = nc.vector.scalar_tensor_tensor(
                        state[:, h, :], state[:, h, :], K.small[:, EGL + 8 * h + n:EGL + 8 * h + n + 1],
                        K.ps[:, 4 + grp, P * hh:P * hh + P], ALU.mult, ALU.add)
                last.then_inc(s("scan_state").sem, s("scan_state").n())

        @block.scalar
        def _(act):
            for x, (n, grp) in enumerate(items):
                rows = slice(CHUNK * (n % 2), CHUNK * (n % 2) + CHUNK)
                act.wait_ge(s("scan_v").sem, s("scan_v").at(x + 1))
                nc.scalar.activation(W[rows, grp, :], K.ps[rows, grp, :], ACT.Copy).then_inc(s("scan_vc").sem, s("scan_vc").n())
                act.wait_ge(s("scan_kv").sem, s("scan_kv").at(x + 1))
                nc.scalar.activation(A[:, QQ + 4 * grp:QQ + 4 * grp + 4, CHUNK * n:CHUNK * n + CHUNK],
                                     K.ps[:, 2 + grp, 0:4 * CHUNK].rearrange("p (h c) -> p h c", c=CHUNK),
                                     ACT.Copy).then_inc(s("scan_o").sem, s("scan_o").n())

        @block.tensor
        def _(pe):
            pe.wait_ge(s("scan_zero").sem, s("scan_zero").at(1))

            def new_v(x):
                n, grp = items[x]
                i, rows, cols = n // 2, slice(CHUNK * (n % 2), CHUNK * (n % 2) + CHUNK), slice(CHUNK * n, CHUNK * n + CHUNK)
                if x >= 2:
                    pe.wait_ge(s("scan_state").sem, s("scan_state").at(x - 1))
                    pe.wait_ge(s("scan_vc").sem, s("scan_vc").at(x - 1))
                for hh in range(4):
                    h = 4 * grp + hh
                    out = K.ps[rows, grp, P * hh:P * hh + P]
                    nc.tensor.matmul(out, A[:, UU + h, cols], A[:, VV + h, P * i:P * i + P], start=True, stop=False)
                    last = nc.tensor.matmul(out, A[:, KK + h, cols], state[:, h, :], start=False, stop=True)
                last.then_inc(s("scan_v").sem, s("scan_v").n())
            new_v(0)
            for x, (n, grp) in enumerate(items):
                i, rows, cols = n // 2, slice(CHUNK * (n % 2), CHUNK * (n % 2) + CHUNK), slice(CHUNK * n, CHUNK * n + CHUNK)
                if x == 0:
                    new_v(1)
                pe.wait_ge(s("scan_vc").sem, s("scan_vc").at(x + 1))
                if x >= 2:
                    pe.wait_ge(s("scan_o").sem, s("scan_o").at(x - 1))
                for hh in range(4):
                    h = 4 * grp + hh
                    out = K.ps[:, 2 + grp, CHUNK * hh:CHUNK * hh + CHUNK]
                    nc.tensor.matmul(out, state[:, h, :], A[:, QQ + h, cols], start=True, stop=False)
                    nc.tensor.matmul(out, W[rows, grp, P * hh:P * hh + P], A[rows, AT + h, cols], start=False, stop=True)
                    last = nc.tensor.matmul(K.ps[:, 4 + grp, P * hh:P * hh + P], A[rows, MT + h, P * i:P * i + P],
                                            W[rows, grp, P * hh:P * hh + P], start=True, stop=True)
                last.then_inc(s("scan_kv").sem, s("scan_kv").n())
                if x >= 1 and x + 1 < len(items):
                    new_v(x + 1)
    K.end_block()


def phase_gdn_out(K):
    nc, s = K.nc, K.s

    def load(sp):
        sp.dma_start(K.A[:, 8:16, :], K.dram["keep_gates"][8:16].rearrange("c p n -> p c n")).then_inc(
            s("reloaded").sem, s("reloaded").n(16))
        sp.dma_start(K.A[:, 16:24, :], K.dram["keep_yc"]).then_inc(s("reloaded").sem, s("reloaded").n(16))

    def dve(dve, t, g, slot):
        if t == 0:
            dve.wait_ge(s("reloaded").sem, s("reloaded").at(32))
        for j in range(2):
            c = 2 * t + j
            wait_bank(K, dve, g, j)
            nc.vector.tensor_tensor(K.A[:, 8 + c, :], K.A[:, 8 + c, :], K.ps[:, 2 * slot + j, :],
                                    ALU.mult).then_inc(*free_bank(K, j))
            dve.wait_ge(s(f"bank_free_{j}").sem, s(f"bank_free_{j}").at(t + 1))
            nc.vector.tensor_tensor(K.A[:, 8 + c, :], K.A[:, 8 + c, :], K.A[:, 16 + c, :], ALU.add).then_inc(
                s("y_ready").sem, s("y_ready").n())
    phase_stream(K, "gdn_out", "gdn_out", dve=dve, load=load, presplit=24)


def phase_residual(K, label, presplit, reload=True, alpha=ALPHA, stats=True, load_more=None):
    nc, s = K.nc, K.s

    def load(sp):
        if reload:
            sp.dma_start(K.A[:, 0:8, :], K.dram["keep_x"]).then_inc(s("reloaded").sem, s("reloaded").n(16))
        if load_more:
            load_more(sp)

    def dve(dve, t, g, slot):
        if t == 0 and reload:
            dve.wait_ge(s("reloaded").sem, s("reloaded").at(16))
        for j in range(2):
            c = 2 * t + j
            wait_bank(K, dve, g, j)
            nc.vector.scalar_tensor_tensor(K.A[:, c, :], K.A[:, c, :], alpha, K.ps[:, 2 * slot + j, :], ALU.mult,
                                           ALU.add).then_inc(*free_bank(K, j))
    phase_stream(K, label, label, dve=dve, load=load, presplit=presplit, stats=LayerNorm(
        K, 0, lambda eng, c: eng.wait_ge(s(f"bank_free_{c % 2}").sem, s(f"bank_free_{c % 2}").at(c // 2 + 1)),
        K.A[:, 32:36, :]) if stats else None)


def block1_mixers(K):
    phase_glu(K)
    phase_projections(K)
    phase_conv_out(K)
    phase_head_norm(K, "gdn_l2", [(QQ + h, "ones", GDN_DK ** -0.5) for h in range(8)] + [(KK + h, "ones", 1.0) for h in range(8)], 0, store=True)
    phase_gdn_matrices(K)
    phase_gdn_inverse(K)
    phase_gdn_tokens(K)
    phase_gdn_scan(K)

    def reload_z(sp):
        sp.dma_start(K.A[:, 0:8, :], K.dram["keep_gates"][0:8].rearrange("c p n -> p c n")).then_inc(
            K.s("reloaded").sem, K.s("reloaded").n(16))
    phase_head_norm(K, "gdn_norm", [(QQ + h, "mean128", K.vec("gdn_norm"), h) for h in range(8)], 40, after=reload_z)
    phase_gdn_out(K)

    def load_memory(sp):
        sp.dma_start(K.A[:, 48:56, 0:N_MEM], K.dram["mem_t"]).then_inc(K.s("mem_in").sem, 16)
        sp.wait_ge(K.s("mem_in").sem, 16)
    phase_residual(K, "mix_out", 8, load_more=load_memory)


def stream_pe_tokens(K, pe, names, n_tok=NT, t0=0):
    free = [K.s("bank_free_0"), K.s("bank_free_1")]
    done = [K.s("first_done"), K.s("tile_done")]

    def body(t, g, uses, slot, times):
        pe.wait_ge(K.s("lo_ready").sem, g + 1)
        whi = K.whi[:, slot, :, :].rearrange("p (j k) n -> p k j n", k=KC)
        wlo = K.wlo[:, slot, :, :].rearrange("p (j k) n -> p k j n", k=KC)
        for j in range(2):
            pe.wait_ge(free[j].sem, free[j].at(t + (t0 - 1)))
            for b in range(n_tok // 2):
                tok = slice(P * (n_tok // 2 * j + b), P * (n_tok // 2 * j + b) + P)
                out = K.ps[:, 2 * slot + j, 256 * b:256 * b + 256].rearrange("p (j n) -> p j n", n=P)
                for k in range(KC):
                    hi, lo = K.xhi[:, k, tok], K.xlo[:, k, tok]
                    K.nc.tensor.matmul(out, hi, whi[:, k], start=k == 0, stop=False)
                    K.nc.tensor.matmul(out, hi, wlo[:, k], start=False, stop=False)
                    last = K.nc.tensor.matmul(out, lo, whi[:, k], start=False, stop=k == KC - 1)
            last.then_inc(done[j].sem, 1)
    tile_loop(pe, names, body)


NMAX, SUMS, RSUM = 704, 708, 712


def phase_attention(K, label, heads, p_unit, pt_unit, load=None):
    nc, s = K.nc, K.s
    A = K.A
    groups = [(h, b) for h in range(len(heads)) for b in range(len(heads[h]["branches"]))]
    items = [(y, i) for y in range(len(groups)) for i in range(NT)]
    n = len(items)

    def br(y):
        h, b = groups[y]
        return heads[h]["branches"][b]

    def prob(x):
        return p_unit[0][:, p_unit[1] + x % 4, :]

    def turned(y, mt):
        return pt_unit[0][:, pt_unit[1] + 4 * (y % 2) + mt, :]

    def blocks(y, i):
        w = br(y)["width"](i)
        return [(m, min(P, w - P * m)) for m in range((w + P - 1) // P)]

    def out_bank(h, o):
        return 5 + (len(heads[h]["out"]) * h + o) % 3

    def col(at, x):
        return K.small[:, at + x % 4:at + x % 4 + 1]

    with nc.Block() as block:
        @block.sync
        def _(sp):
            if load:
                load(sp)

        @block.tensor
        def _(pe):
            def scores(x):
                y, i = items[x]
                w = br(y)["width"](i)
                if x >= 3:
                    pe.wait_ge(s("att_exp").sem, s("att_exp").at(x - 2))
                parts = br(y)["scores"](i)
                for p, (q, k) in enumerate(parts):
                    last = nc.tensor.matmul(K.ps[:, x % 3, :w], q, k[:, :w], start=p == 0, stop=p == len(parts) - 1)
                last.then_inc(s("att_scores").sem, s("att_scores").n())

            def turn(x):
                y, i = items[x]
                pe.wait_ge(s("att_prob").sem, s("att_prob").at(x + 1))
                if x >= 2:
                    pe.wait_ge(s("att_copied").sem, s("att_copied").at(x - 1))
                for m, w in blocks(y, i):
                    last = nc.tensor.transpose(K.ps[:w, 3 + x % 2, P * m:P * m + P], prob(x)[:, P * m:P * m + w], K.mat("ident"))
                last.then_inc(s("att_turned").sem, s("att_turned").n())

            def product(y):
                h, b = groups[y]
                head = heads[h]
                pe.wait_ge(s("att_copied").sem, s("att_copied").at(4 * y + 4))
                before = h - 1 if len(head["out"]) == 2 else h - 3
                if b == 0 and before >= 0:
                    pe.wait_ge(s("att_out").sem, s("att_out").at(before + 1))
                bl = blocks(y, NT - 1)
                for o, (rows, _) in enumerate(head["out"]):
                    for m, w in bl:
                        first = P * m if br(y)["causal"] else 0
                        last = nc.tensor.matmul(K.ps[rows, out_bank(h, o), first:], br(y)["v"](m, o), turned(y, m)[:w, first:],
                                                start=b == 0 and m == 0,
                                                stop=b == len(head["branches"]) - 1 and m == bl[-1][0])
                last.then_inc(s("att_pv").sem, s("att_pv").n())

            for x in range(3):
                scores(x)
            for x, (y, i) in enumerate(items):
                turn(x)
                if x + 3 < n:
                    scores(x + 3)
                if i == 0 and y >= 1:
                    product(y - 1)
            product(len(groups) - 1)

        @block.vector
        def _(dve):
            def before(x):
                y, i = items[x]
                w = br(y)["width"](i)
                dve.wait_ge(s("att_scores").sem, s("att_scores").at(x + 1))
                if br(y)["bias"]:
                    cols, bias = br(y)["bias"](i)
                    out = K.ps[:, x % 3, cols]
                    if len(bias.shape) == 3:
                        out = out.rearrange("p (r c) -> p r c", c=bias.shape[2])
                    nc.vector.tensor_tensor(out, out, bias, ALU.add).then_inc(s("att_bias").sem, s("att_bias").n())
                    dve.wait_ge(s("att_bias").sem, s("att_bias").base + s("att_bias").pending)
                nc.vector.tensor_reduce(col(NMAX, x), K.ps[:, x % 3, :w], AX.X, ALU.max, negate=True).then_inc(
                    s("att_max").sem, s("att_max").n())

            def after(x):
                y, i = items[x]
                w = br(y)["width"](i)
                step = s("att_dve")
                dve.wait_ge(s("att_exp").sem, s("att_exp").at(x + 1))
                nc.vector.reciprocal(col(RSUM, x), col(SUMS, x)).then_inc(step.sem, step.n())
                dve.wait_ge(step.sem, step.base + step.pending)
                if br(y)["gate"]:
                    nc.vector.tensor_tensor(col(RSUM, x), col(RSUM, x), br(y)["gate"](i), ALU.mult).then_inc(step.sem, step.n())
                    dve.wait_ge(step.sem, step.base + step.pending)
                if br(y)["mask"]:
                    last = nc.vector.scalar_tensor_tensor(prob(x)[:, :w], prob(x)[:, :w], col(RSUM, x), br(y)["mask"](i),
                                                          ALU.mult, ALU.mult)
                else:
                    last = nc.vector.tensor_scalar(prob(x)[:, :w], prob(x)[:, :w], col(RSUM, x), None, ALU.mult)
                last.then_inc(s("att_prob").sem, s("att_prob").n())

            def evacuate(y):
                h, b = groups[y]
                if b < len(heads[h]["branches"]) - 1:
                    return
                dve.wait_ge(s("att_pv").sem, s("att_pv").at(y + 1))
                for o, (rows, unit) in enumerate(heads[h]["out"]):
                    if "times" in heads[h]:
                        last = nc.vector.tensor_tensor(A[rows, unit, :], K.ps[rows, out_bank(h, o), :],
                                                       heads[h]["times"], ALU.mult)
                        continue
                    last = nc.vector.tensor_copy(A[rows, unit, :], K.ps[rows, out_bank(h, o), :])
                last.then_inc(s("att_out").sem, s("att_out").n())

            if load:
                dve.wait_ge(s("reloaded").sem, s("reloaded").at(16))
            before(0)
            before(1)
            for x, (y, i) in enumerate(items):
                after(x)
                if x + 2 < n:
                    before(x + 2)
                if i == 1 and y >= 1:
                    evacuate(y - 1)
            evacuate(len(groups) - 1)

        @block.scalar
        def _(act):
            def exponential(x):
                y, i = items[x]
                w = br(y)["width"](i)
                act.wait_ge(s("att_max").sem, s("att_max").at(x + 1))
                if x >= 4:
                    act.wait_ge(s("att_turned").sem, s("att_turned").at(x - 3))
                nc.scalar.activation(prob(x)[:, :w], K.ps[:, x % 3, :w], ACT.Exp, bias=col(NMAX, x),
                                     accum_out=col(SUMS, x)).then_inc(s("att_exp").sem, s("att_exp").n())

            def copy(x):
                y, i = items[x]
                bl = blocks(y, i)
                act.wait_ge(s("att_turned").sem, s("att_turned").at(x + 1))
                if i == 0 and y >= 2:
                    act.wait_ge(s("att_pv").sem, s("att_pv").at(y - 1))
                w = bl[-1][1]
                at = pt_unit[1] + 4 * (y % 2)
                nc.scalar.activation(pt_unit[0][:w, at:at + len(bl), P * i:P * i + P],
                                     K.ps[:w, 3 + x % 2, :P * len(bl)].rearrange("p (m c) -> p m c", c=P),
                                     ACT.Copy).then_inc(s("att_copied").sem, s("att_copied").n())
            exponential(0)
            exponential(1)
            for x in range(n):
                if x + 2 < n:
                    exponential(x + 2)
                copy(x)
    K.end_block()


def copy_evac(K, unit_of, scale=1.0, func=ACT.Copy, bias=None):
    def act(act, t, g, slot):
        for j in range(2):
            c = 2 * t + j
            unit, f, sc, b = unit_of(c)
            wait_bank(K, act, g, j)
            kw = {"bias": b} if b is not None else {}
            K.nc.scalar.activation(unit, K.ps[:, 2 * slot + j, :unit.shape[-1]], f, scale=sc, **kw).then_inc(*free_bank(K, j))
    return act


def block1_memory(K):
    nc, s = K.nc, K.s
    A = K.A
    phase_stream(K, "xk", "xk", presplit=48, width=N_MEM, pe=lambda pe: stream_pe(K, pe, "xk", n=N_MEM, split=True),
                 act=copy_evac(K, lambda c: (A[:, 16 + c, :N_MEM], ACT.Copy, 1.0, None)))

    def take_v(act, t, g, slot):
        for j in range(2):
            wait_bank(K, act, g, j)
            nc.scalar.activation(A[:, 24 + 2 * j + t // 2, 256 * (t % 2):256 * (t % 2) + 256],
                                 K.ps[:, 2 * slot + j, :256], ACT.Copy).then_inc(*free_bank(K, j))
    phase_stream(K, "xv", "xv", pe=lambda pe: stream_pe_tokens(K, pe, "xv", 2), act=take_v)
    phase_stream(K, "xq", "xq", norm=Affine(K, 0, "ln2_g", "ln2_b"), act=copy_evac(K, lambda c: (A[:, 32 + c, :], ACT.Copy, 1 / 16, None)))
    heads = []
    for h in range(XATTN_HEADS):
        heads.append({
            "out": [(slice(0, P), 40 + 2 * h), (slice(0, P), 41 + 2 * h)],
            "branches": [{
                "scores": lambda i, h=h: [(A[:, 32 + 2 * h + d, P * i:P * i + P], A[:, 16 + 2 * h + d, :]) for d in range(2)],
                "width": lambda i: N_MEM, "bias": None, "gate": None, "mask": None, "causal": False,
                "v": lambda m, o, h=h: A[:, 24 + 2 * m + h // 2, 256 * (h % 2) + P * o:256 * (h % 2) + P * o + P],
            }]})
    phase_attention(K, "xattn", heads, (A, 28), (A, 48))
    phase_residual(K, "xo", 40, reload=False)


GATE = 0
W2K, W2V = 384, 512
HID, KCMP, VCMP = 768, 1024, 1056


def phase_mla_norms(K):
    nc, s = K.nc, K.s
    sq = K.pair
    with nc.Block() as block:
        @block.sync
        def _(sp):
            sp.dma_start(sq[:, 8:13, :], K.dram["mla_w"]).then_inc(s("reloaded").sem, s("reloaded").n(16))
            sp.wait_ge(s("reloaded").sem, s("reloaded").at(16))

        @block.scalar
        def _(act):
            for c in range(3):
                nc.scalar.activation(sq[:, c, :], K.A[:, 20 + c, :], ACT.Square).then_inc(s("squared").sem, s("squared").n())
            for i in range(2):
                act.wait_ge(s("var_ready").sem, s("var_ready").at(i + 1))
                nc.scalar.activation(sq[:, 3 + i, :], K.ps[:, 4 + i, :], ACT.Abs_reciprocal_sqrt,
                                     bias=K.eps(RMS_EPS)).then_inc(s("rstd_ready").sem, s("rstd_ready").n())

        @block.tensor
        def _(pe):
            for c in range(3):
                pe.wait_ge(s("squared").sem, s("squared").at(c + 1))
                last = nc.tensor.matmul(K.ps[:, 4 + c // 2, :], K.mat("mean256" if c < 2 else "mean128"), sq[:, c, :],
                                        start=c != 1, stop=c != 0)
                if c > 0:
                    last.then_inc(s("var_ready").sem, s("var_ready").n())

        @block.vector
        def _(dve):
            for c in range(3):
                dve.wait_ge(s("rstd_ready").sem, s("rstd_ready").at(1 + c // 2))
                gain = K.vec("mla_q", c) if c < 2 else K.vec("mla_kv")
                nc.vector.scalar_tensor_tensor(K.A[:, 20 + c, :], K.A[:, 20 + c, :], gain, sq[:, 3 + c // 2, :],
                                               ALU.mult, ALU.mult)
    K.end_block()


def phase_rope(K, label, chunks, matrix, cos, sin, load=None, rows=P, copies=None):
    nc, s = K.nc, K.s
    A, W = K.A, K.pair

    def wait_added(eng, x):
        eng.wait_ge(s("rope_added").sem, s("rope_added").at(x + 1))
    with nc.Block() as block:
        @block.sync
        def _(sp):
            if load:
                load(sp)

        @block.tensor
        def _(pe):
            for x, c in enumerate(chunks):
                if x >= 2:
                    pe.wait_ge(s("rope_sin").sem, s("rope_sin").at(x - 1))
                nc.tensor.matmul(K.ps[:rows, x % 2, :], K.mat(matrix)[:rows, :rows], A[:rows, c, :], start=True, stop=True).then_inc(
                    s("rope_turned").sem, s("rope_turned").n())

        @block.gpsimd
        def _(pool):
            pool.wait_ge(s("rope_tables").sem, s("rope_tables").at(1))
            for x, c in enumerate(chunks):
                if x >= 2:
                    wait_added(pool, x - 2)
                nc.gpsimd.tensor_tensor(W[:rows, 12 + x % 2, :], A[:rows, c, :], cos, ALU.mult).then_inc(
                    s("rope_cos").sem, s("rope_cos").n())

        @block.vector
        def _(dve):
            if load:
                dve.wait_ge(s("reloaded").sem, s("reloaded").at(16))
            nc.vector.nop().then_inc(s("rope_tables").sem, s("rope_tables").n())
            for x, c in enumerate(chunks):
                dve.wait_ge(s("rope_turned").sem, s("rope_turned").at(x + 1))
                nc.vector.tensor_tensor(W[:rows, 14 + x % 2, :], K.ps[:rows, x % 2, :], sin, ALU.mult).then_inc(
                    s("rope_sin").sem, s("rope_sin").n())
                dve.wait_ge(s("rope_sin").sem, s("rope_sin").at(x + 1))
                dve.wait_ge(s("rope_cos").sem, s("rope_cos").at(x + 1))
                nc.vector.tensor_tensor(A[:rows, c, :], W[:rows, 12 + x % 2, :], W[:rows, 14 + x % 2, :], ALU.add).then_inc(
                    s("rope_added").sem, s("rope_added").n())

        @block.scalar
        def _(act):
            if copies:
                wait_added(act, 0)
                copies(act)
    K.end_block()


def phase_norm_2(K):
    nc, s = K.nc, K.s
    with nc.Block() as block:
        @block.vector
        def _(dve):
            Affine(K, 0, "ln4_g", "ln4_b", split=False).dve(dve)

        @block.scalar
        def _(act):
            Affine(K, 0, "ln4_g", "ln4_b", split=False).act(act)
            for c in range(KC):
                act.wait_ge(s("normed").sem, s("normed").at(c + 1))
                nc.scalar.activation(K.pair[:, c, :], K.A[:, c, :], ACT.Square).then_inc(s("squared").sem, s("squared").n())
            act.wait_ge(s("var_ready").sem, s("var_ready").at(1))
            nc.scalar.activation(K.ps[:, LayerNorm.FACTOR, :], K.ps[:, 5, :], ACT.Abs_reciprocal_sqrt, bias=K.eps(RMS_EPS))

        @block.tensor
        def _(pe):
            for c in range(KC):
                pe.wait_ge(s("squared").sem, s("squared").at(c + 1))
                last = nc.tensor.matmul(K.ps[:, 5, :], K.mat("mean"), K.pair[:, c, :], start=c == 0, stop=c == KC - 1)
            last.then_inc(s("var_ready").sem, s("var_ready").n())
    K.end_block()


class Rms2:

    def __init__(self, K):
        self.K = K

    def act(self, act):
        pass

    def dve(self, dve):
        K, s = self.K, self.K.s
        for c in range(KC + 1):
            if c < KC:
                K.nc.vector.scalar_tensor_tensor(K.A[:, 8 + c, :], K.A[:, c, :], K.vec("norm_2", c),
                                                 K.ps[:, LayerNorm.FACTOR, :], ALU.mult, ALU.mult).then_inc(
                    s("scaled").sem, s("scaled").n())
            if c >= 1:
                split_one(K, dve, c - 1, 7 + c, s("scaled"), c)

    def pool(self, pool):
        split_lows(self.K, pool, 8)


def phase_in_2(K):
    nc, s = K.nc, K.s
    A = K.A
    names = ["rqk_2", "rv_2", "mid_2", "v_2"]

    def pe(pe):
        stream_pe(K, pe, "rqk_2", split=True)
        stream_pe_tokens(K, pe, "rv_2", t0=4)
        stream_pe(K, pe, "mid_2", t0=6)
        stream_pe_tokens(K, pe, "v_2", t0=14)
        for i in range(NT):
            for k in range(KC):
                last = nc.tensor.matmul(K.ps[:, 6, 24 * i:24 * i + 24], A[:, 8 + k, P * i:P * i + P],
                                        K.small[:, 128 + 24 * k:152 + 24 * k], start=k == 0, stop=k == KC - 1)
        last.then_inc(s("gl_ready").sem, s("gl_ready").n())

    def act(act, t, g, slot):
        for j in range(2):
            wait_bank(K, act, g, j)
            bank = K.ps[:, 2 * slot + j, :]
            func, scale = ACT.Copy, 1.0
            if t in (4, 5):
                out = A[:, 24 + 2 * j:26 + 2 * j, 256 * (t - 4):256 * (t - 4) + 256]
                bank = bank.rearrange("p (b n) -> p b n", n=256)
            elif t == 14:
                out = A[:, 44 + j, :]
            else:
                c = 2 * t + j
                out = A[:, 16 + c if t < 4 else 28 + c - 12, :]
                if t in (2, 3):
                    scale = HD ** -0.5
                if t in (6, 7, 10, 11):
                    func = ACT.Silu
            nc.scalar.activation(out, bank, func, scale=scale).then_inc(*free_bank(K, j))

    def dve(dve, t, g, slot):
        if t == 14:
            dve.wait_ge(s("gl_ready").sem, s("gl_ready").at(1))
            nc.vector.tensor_tensor(K.small[:, GATE:GATE + 96].rearrange("p (i c) -> p i c", c=24),
                                    K.ps[:, 6, 0:96].rearrange("p (i c) -> p i c", c=24),
                                    K.vec("b_gate_2", 0, 24).unsqueeze(1).broadcast_to([P, NT, 24]),
                                    ALU.add)

    def compression(sp):
        load_w1(K, sp, 0, 0, A[:, 48:56, :])
        sp.dma_start(K.small[:, W2K:W2K + 256], K.dram["w2"]).then_inc(s("w2_in").sem, 16)
    phase_stream(K, "in_2", names, pe=pe, act=act, dve=dve, load_next=compression, norm=Rms2(K))


def load_w1(K, eng, kind, part, to):
    eng.dma_start(to, K.dram[("w1_k", "w1_v")[kind]][:, 16 * part:16 * part + 16, :].rearrange(
        "p (u l) n -> p u (l n)", l=2)).then_inc(K.s(f"w1_in_{2 * kind + part}").sem, 16)


def phase_compress(K):
    nc, s = K.nc, K.s
    A, W = K.A, K.pair
    w1 = [A[:, 48:56, :], W[:, 0:8, :], W[:, 8:16, :], A[:, 8:16, :]]
    PART = 8
    both = [K.ps[:2 * 32, 1 + kind, 0:256] for kind in range(2)]
    silu = [W[:2 * 32, kind, 0:256] for kind in range(2)]

    def blocks(x):
        return A[:, 46 + x % 2, :].rearrange("p (l n) -> p l n", n=2 * 32)

    def w2(kind, m):
        at = (W2K, W2V)[kind] + HD * m
        return K.small[:, at:at + HD]

    def hid(kind, m, g):
        at = HID + 128 * kind + 64 * m + 32 * g
        return K.small[:, at:at + N_CMP]
    with nc.Block() as block:
        @block.sync
        def _(sp):
            for i in range(1, 4):
                load_w1(K, sp, i // 2, i % 2, w1[i])

        @block.vector
        def _(dve):
            nc.vector.memset(A[:, 46:48, :], 0.0).then_inc(s("cmp_zero").sem, s("cmp_zero").n())
            dve.wait_ge(s("cmp_zero").sem, s("cmp_zero").at(1))
            for x in range(8):
                kind, l0 = x // 4, PART * (x % 4)
                if x >= 2:
                    dve.wait_ge(s("cmp_part").sem, s("cmp_part").at(x - 1))
                for g in range(2):
                    rows = slice(HD * g, HD * g + HD)
                    src = A[rows, 40 + kind, l0:l0 + 1]
                    windows = bass.AP(tensor=src.tensor, offset=src.offset, ap=[src.ap[0], [1, PART], [CMP_STRIDE, N_CMP]])
                    pos = K.vec(("pos_k", "pos_v")[kind], l0, PART)[rows].unsqueeze(2).broadcast_to([HD, PART, N_CMP])
                    nc.vector.tensor_tensor(blocks(x)[rows, :, 32 * g:32 * g + N_CMP], windows, pos,
                                            ALU.add).then_inc(s("cmp_blocks").sem, s("cmp_blocks").n())
            for kind in range(2):
                dve.wait_ge(s("cmp_turned").sem, s("cmp_turned").at(kind + 1))
                nc.vector.tensor_copy(K.small[:, HID + 128 * kind:HID + 128 * kind + 128],
                                      K.ps[:, 3 + kind, 0:128]).then_inc(s("cmp_hid").sem, s("cmp_hid").n())
                if kind == 0:
                    dve.wait_ge(s("cmp_rstd").sem, s("cmp_rstd").at(1))
                    nc.vector.scalar_tensor_tensor(K.small[:, KCMP:KCMP + N_CMP], K.ps[:, 5, 0:N_CMP], K.vec("k_cmp"),
                                                   W[:, 3, 0:N_CMP], ALU.mult, ALU.mult)
            dve.wait_ge(s("cmp_out").sem, s("cmp_out").at(2))
            nc.vector.tensor_copy(K.small[:N_CMP, VCMP:VCMP + 128], K.ps[:N_CMP, 6, 0:128])

        @block.scalar
        def _(act):
            nc.scalar.activation(K.small[:, GATE:GATE + 96], K.small[:, GATE:GATE + 96], ACT.Sigmoid)
            act.wait_ge(s("cmp_part").sem, s("cmp_part").at(4))
            nc.scalar.activation(silu[0], both[0], ACT.Silu).then_inc(s("cmp_silu").sem, s("cmp_silu").n())
            act.wait_ge(s("cmp_out").sem, s("cmp_out").at(1))
            nc.scalar.activation(W[:, 2, 0:N_CMP], K.ps[:, 5, 0:N_CMP], ACT.Square).then_inc(s("cmp_sq").sem, s("cmp_sq").n())
            act.wait_ge(s("cmp_part").sem, s("cmp_part").at(8))
            nc.scalar.activation(silu[1], both[1], ACT.Silu).then_inc(s("cmp_silu").sem, s("cmp_silu").n())
            act.wait_ge(s("cmp_mean").sem, s("cmp_mean").at(1))
            nc.scalar.activation(W[:, 3, 0:N_CMP], K.ps[:, 7, 0:N_CMP], ACT.Abs_reciprocal_sqrt,
                                 bias=K.eps(RMS_EPS)).then_inc(s("cmp_rstd").sem, s("cmp_rstd").n())

        @block.tensor
        def _(pe):
            def part(x):
                kind = x // 4
                if x % 2 == 0:
                    pe.wait_ge(s(f"w1_in_{x // 2}").sem, 16)
                pe.wait_ge(s("cmp_blocks").sem, s("cmp_blocks").at(2 * x + 2))
                for i in range(PART):
                    l = PART * (x % 2) + i
                    last = nc.tensor.matmul(both[kind], blocks(x)[:, i, :],
                                            w1[x // 2][:, l // 2, 256 * (l % 2):256 * (l % 2) + 256],
                                            start=x % 4 == 0 and i == 0, stop=x % 4 == 3 and i == PART - 1)
                last.then_inc(s("cmp_part").sem, s("cmp_part").n())

            def turn(kind):
                pe.wait_ge(s("cmp_silu").sem, s("cmp_silu").at(kind + 1))
                for m in range(2):
                    last = nc.tensor.transpose(K.ps[:, 3 + kind, 64 * m:64 * m + 64], silu[kind][:, P * m:P * m + P],
                                               K.mat("ident")[:2 * 32, :2 * 32])
                last.then_inc(s("cmp_turned").sem, s("cmp_turned").n())

            def second(kind):
                pe.wait_ge(s("cmp_hid").sem, s("cmp_hid").at(kind + 1))
                for g in range(2):
                    for m in range(2):
                        if kind == 0:
                            last = nc.tensor.matmul(K.ps[HD * g:HD * g + HD, 5, 0:N_CMP], w2(0, m), hid(0, m, g),
                                                    start=m == 0, stop=m == 1)
                        else:
                            last = nc.tensor.matmul(K.ps[:N_CMP, 6, HD * g:HD * g + HD], hid(1, m, g), w2(1, m),
                                                    start=m == 0, stop=m == 1)
                last.then_inc(s("cmp_out").sem, s("cmp_out").n())
            pe.wait_ge(s("w2_in").sem, 16)
            for x in range(6):
                part(x)
            turn(0)
            part(6)
            second(0)
            part(7)
            pe.wait_ge(s("cmp_sq").sem, s("cmp_sq").at(1))
            nc.tensor.matmul(K.ps[:, 7, 0:N_CMP], K.mat("mean64"), W[:, 2, 0:N_CMP], start=True, stop=True).then_inc(
                s("cmp_mean").sem, s("cmp_mean").n())
            turn(1)
            second(1)
    K.end_block()


def phase_retention(K):
    nc, s = K.nc, K.s
    A, W = K.A, K.pair
    items = [(h, i) for h in range(HEADS) for i in range(NT)]
    n = len(items)

    def place(h):
        return slice(HD * (h % 2), HD * (h % 2) + HD), h // 2

    def scores_bank(x):
        return K.ps[:, (0, 1, 4, 5)[x % 4], :]
    with nc.Block() as block:
        @block.tensor
        def _(pe):
            def scores(x):
                h, i = items[x]
                rows, c = place(h)
                if x >= 4:
                    pe.wait_ge(s("ret_a").sem, s("ret_a").at(x - 3))
                nc.tensor.matmul(scores_bank(x)[:, :T - P * i], A[rows, 20 + c, P * i:P * i + P], A[rows, 16 + c, P * i:],
                                 start=True, stop=True).then_inc(s("ret_scores").sem, s("ret_scores").n())
            for x in range(3):
                scores(x)
            for x, (h, i) in enumerate(items):
                rows, c = place(h)
                if x + 3 < n:
                    scores(x + 3)
                pe.wait_ge(s("ret_a").sem, s("ret_a").at(x + 1))
                if i == 0 and h >= 2:
                    pe.wait_ge(s("ret_out").sem, s("ret_out").at(h - 1))
                nc.tensor.matmul(K.ps[rows, 2 + h % 2, P * i:], A[:, 24 + i, HD * h:HD * h + HD], W[:, x % 4, :T - P * i],
                                 start=i == 0, stop=i == NT - 1).then_inc(s("ret_o").sem, s("ret_o").n())

        @block.vector
        def _(dve):
            dve.wait_ge(s("decay_in").sem, 16)
            for x, (h, i) in enumerate(items):
                dve.wait_ge(s("ret_scores").sem, s("ret_scores").at(x + 1))
                if x >= 4:
                    dve.wait_ge(s("ret_o").sem, s("ret_o").at(x - 3))
                nc.vector.tensor_tensor(W[:, x % 4, :T - P * i], scores_bank(x)[:, :T - P * i], A[:, 48 + h, :T - P * i],
                                        ALU.mult).then_inc(s("ret_a").sem, s("ret_a").n())

        @block.scalar
        def _(act):
            for h in range(HEADS):
                rows, c = place(h)
                act.wait_ge(s("ret_o").sem, s("ret_o").at(4 * h + 4))
                nc.scalar.activation(A[rows, 8 + c, :], K.ps[rows, 2 + h % 2, :], ACT.Copy).then_inc(s("ret_out").sem, s("ret_out").n())
    K.end_block()


def block2(K):
    nc, s = K.nc, K.s
    A = K.A
    phase_norm_2(K)
    phase_in_2(K)
    phase_compress(K)

    def tables(sp):
        sp.dma_start(A[:, 46:48, :], K.dram["rope_2"]).then_inc(s("reloaded").sem, s("reloaded").n(16))
        sp.dma_start(A[:, 48:56, :], K.dram["decay"]).then_inc(s("decay_in").sem, 16)
    phase_rope(K, "rope_2", list(range(16, 24)), "rope64", A[:, 46, :], A[:, 47, :], tables)
    phase_retention(K)
    phase_head_norm(K, "norms_2", [(8 + c, "mean64", K.vec("ret_norm", c), 28 + c) for c in range(4)] +
                    [(32 + c, "chunk_ones", K.vec("q_norm_2")) for c in range(4)] +
                    [(42, "mean64", K.vec("k_slc")), (43, "mean64", K.vec("k_win"))], 48,
                    eps=lambda i: 64 * RMS_EPS if 4 <= i < 8 else RMS_EPS)
    masks = A[:, 46, :]

    def load(sp):
        sp.dma_start(masks[:, 0:384], K.dram["masks_2"]).then_inc(s("reloaded").sem, s("reloaded").n(16))

    def gate(b, h):
        return lambda i: K.small[:, GATE + 24 * i + 8 * b + h:GATE + 24 * i + 8 * b + h + 1]
    heads = []
    for c in range(4):
        for g in range(2):
            h, rows = c + 4 * g, slice(HD * g, HD * g + HD)

            def q(i, rows=rows, c=c):
                return A[rows, 32 + c, P * i:P * i + P]
            branches = [{
                "scores": lambda i, q=q, rows=rows: [(q(i), K.small[rows, KCMP:KCMP + N_CMP])],
                "width": lambda i: N_CMP, "causal": False, "gate": gate(0, h),
                "bias": lambda i: (slice(0, N_CMP), masks[:, 32 * i:32 * i + N_CMP]),
                "mask": lambda i: masks[:, 128 + 32 * i:128 + 32 * i + N_CMP],
                "v": lambda m, o, g=g: K.small[:N_CMP, VCMP + HD * g:VCMP + HD * g + HD],
            }]
            for b in (1, 2):
                branches.append({
                    "scores": lambda i, q=q, rows=rows, b=b: [(q(i), A[rows, 41 + b, :])],
                    "width": lambda i: P * (i + 1), "causal": True, "gate": gate(b, h), "mask": None,
                    "bias": lambda i: (slice(P * i, P * i + P), masks[:, 256:384]),
                    "v": lambda m, o, g=g, b=b: A[:, 44 + m // 2, 256 * (m % 2) + P * (b - 1) + HD * g:
                                                 256 * (m % 2) + P * (b - 1) + HD * g + HD],
                })
            heads.append({"out": [(rows, 12 + c)], "times": A[rows, 36 + c, :], "branches": branches})
    phase_attention(K, "nsa", heads, (A, 16), (A, 48), load)
    phase_residual(K, "out_2", 8, reload=False, alpha=1.0, stats=False)


def phase_mla_in(K):
    nc, s = K.nc, K.s
    A, W = K.A, K.pair
    uq = W[:, 8:11, :].rearrange("p a b -> p (a b)").rearrange("p (k n) -> p k n", k=2)
    ukv = W[:, 11:13, :].rearrange("p a b -> p (a b)")
    with nc.Block() as block:
        @block.sync
        def _(sp):
            sp.dma_start(A[:, 52:54, :], K.dram["rope_3"]).then_inc(s("reloaded").sem, s("reloaded").n(16))

        @block.tensor
        def _(pe):
            for x in range(20):
                if x >= 4:
                    pe.wait_ge(s("mla_taken").sem, s("mla_taken").at(x - 3))
                if x < 8:
                    for k in range(2):
                        last = nc.tensor.matmul(K.ps[:MLA_QK, x % 4, :], uq[:, k, MLA_QK * x:MLA_QK * x + MLA_QK],
                                                A[:, 20 + k, :], start=k == 0, stop=k == 1)
                elif x < 16:
                    last = nc.tensor.matmul(K.ps[:HD, x % 4, :], ukv[:, HD * (x - 8):HD * (x - 7)], A[:, 22, :],
                                            start=True, stop=True)
                else:
                    last = nc.tensor.matmul(K.ps[:, x % 4, :], A[:, 22, P * (x - 16):P * (x - 15)], ukv[:, 512:],
                                            start=True, stop=True)
                last.then_inc(s("mla_ready").sem, s("mla_ready").n())

        @block.scalar
        def _(act):
            for x in range(20):
                act.wait_ge(s("mla_ready").sem, s("mla_ready").at(x + 1))
                rows, unit = (MLA_QK, 8 + x) if x < 8 else (HD, 44 + x - 8) if x < 16 else (P, x)
                nc.scalar.activation(A[:rows, unit, :], K.ps[:rows, x % 4, :], ACT.Copy,
                                     scale=MLA_QK ** -0.5 if x < 8 else 1.0).then_inc(s("mla_taken").sem, s("mla_taken").n())
            act.wait_ge(s("reloaded").sem, s("reloaded").at(16))
    K.end_block()


def phase_branches_3(K):
    nc, s = K.nc, K.s
    A = K.A

    def pe(pe):
        for t in range(4):
            g = FIRST_TILE["branches_3"] + t
            slot = g % 2
            pe.wait_ge(K.s("lo_ready").sem, g + 1)
            if t >= 2:
                pe.wait_ge(s("branch_taken").sem, s("branch_taken").at(4 * (t - 1)))
            for m in range(4):
                for k in range(4):
                    c = 4 * (t // 2) + k
                    if m == 0 and t % 2 == 0:
                        pe.wait_ge(K.s("x_split").sem, K.s("x_split").at(c + 1))
                    last = three_products(K, K.ps[:, 4 * (t % 2) + m, :], K.whi[:, slot, 4 * m + k, :],
                                          K.wlo[:, slot, 4 * m + k, :], K.xhi[:, c, :], K.xlo[:, c, :], k == 0, k == 3)
                if m in (1, 3):
                    last.then_inc(K.s(("first_done", "tile_done")[m // 2]).sem, 1)

    def dve(dve, t, g, slot):
        for m in range(4):
            wait_bank(K, dve, g, m // 2)
            c = 24 + 8 * (t // 2) + 4 * (t % 2) + m
            nc.vector.tensor_tensor(A[:, c, :], A[:, c, :], K.ps[:, 4 * (t % 2) + m, :], ALU.mult).then_inc(
                s("branch_taken").sem, s("branch_taken").n())
            if t >= 2:
                dve.wait_ge(s("branch_taken").sem, s("branch_taken").at(4 * t + m + 1))
                nc.vector.tensor_tensor(A[:, c - 8, :], A[:, c - 8, :], A[:, c, :], ALU.add)
    phase_stream(K, "branches_3", "branches_3", pe=pe, dve=dve, presplit=[40, 41, 42, 43, 8, 9, 10, 11])


def block3(K):
    nc, s = K.nc, K.s
    A = K.A
    names = ["qk_3", "v_3", "rest_3"]

    def pe(pe):
        stream_pe(K, pe, "qk_3", split=True)
        stream_pe_tokens(K, pe, "v_3", t0=4)
        stream_pe(K, pe, "rest_3", t0=6)

    def act(act, t, g, slot):
        for j in range(2):
            wait_bank(K, act, g, j)
            bank = K.ps[:, 2 * slot + j, :]
            c = 2 * t + j
            if t in (4, 5):
                out = A[:, 16 + 2 * j:18 + 2 * j, 256 * (t - 4):256 * (t - 4) + 256]
                nc.scalar.activation(out, bank.rearrange("p (b n) -> p b n", n=256), ACT.Copy).then_inc(*free_bank(K, j))
            elif t < 8:
                nc.scalar.activation(A[:, 8 + c, :], bank, ACT.Copy, scale=HD ** -0.5 if t < 2 else 1.0).then_inc(*free_bank(K, j))
            else:
                nc.scalar.activation(A[:, 8 + c, :], bank, ACT.Sigmoid, bias=K.vec("b_gate_3", c - 16)).then_inc(*free_bank(K, j))

    def load_bias(sp):
        sp.dma_start(A[:, 40:54, :], K.dram["na_bias"]).then_inc(s("na_bias_in").sem, 16)
        sp.wait_ge(s("na_bias_in").sem, 16)
    phase_stream(K, "in_3", names, pe=pe, act=act, presplit=0, load_next=load_bias)
    table = A[:, 40:54, :].rearrange("p a b -> p (a b)").rearrange("p (h j c) -> p h j c", h=HEADS, c=GRID_W)
    heads = []
    for h in range(HEADS):
        rows, c = slice(HD * (h % 2), HD * (h % 2) + HD), h // 2
        heads.append({"out": [(rows, 40 + c)], "branches": [{
            "scores": lambda i, rows=rows, c=c: [(A[rows, 8 + c, P * i:P * i + P], A[rows, 12 + c, :])],
            "width": lambda i: T, "causal": False, "gate": None, "mask": None,
            "bias": lambda i, h=h: (slice(0, T), table[:, h, 6 - 2 * i:14 - 2 * i, :]),
            "v": lambda m, o, h=h: A[:, 16 + m, HD * h:HD * h + HD],
        }]})
    phase_attention(K, "na", heads, (K.pair, 8), (K.pair, 0))

    phase_mla_norms(K)
    phase_mla_in(K)

    def copies(act):
        for h in range(HEADS):
            nc.scalar.activation(A[HD:MLA_QK, 44 + h, :], A[HD:MLA_QK, 23, :], ACT.Copy)
    phase_rope(K, "rope_3", [23] + list(range(8, 16)), "rope32", A[:MLA_QK, 52, :], A[:MLA_QK, 53, :], rows=MLA_QK,
               copies=copies)
    heads = []
    for h in range(HEADS):
        rows, c = slice(HD * (h % 2), HD * (h % 2) + HD), h // 2
        heads.append({"out": [(rows, 8 + c)], "branches": [{
            "scores": lambda i, h=h: [(A[:MLA_QK, 8 + h, P * i:P * i + P], A[:MLA_QK, 44 + h, :])],
            "width": lambda i: T, "causal": False, "gate": None, "mask": None, "bias": None,
            "v": lambda m, o, h=h: A[:, 16 + m, HD * h:HD * h + HD],
        }]})
    phase_attention(K, "mla", heads, (K.pair, 8), (K.pair, 0))
    phase_branches_3(K)
    phase_residual(K, "out_3", 24, reload=False)
    phase_ffn_in(K, "ffn3_in", 1.0, norm=Affine(K, 0, "ln1_g_3", "ln1_b_3"))
    phase_ffn_out(K, "ffn3_out")


def program(nc, dram):
    K = Kernel(nc, dram)
    phase_start(K)
    phase_ffn_in(K, "ffn1_in", norm=FirstSplit(K))
    phase_ffn_out(K, "ffn1_out")
    block1_mixers(K)
    block1_memory(K)
    phase_ffn_in(K, "ffn2_in", norm=Affine(K, 0, "ln3_g", "ln3_b"))
    phase_ffn_out(K, "ffn2_out")
    block2(K)
    block3(K)
    last = Affine(K, 0, "ln2_g_3", "ln2_b_3", split=False)
    with nc.Block() as block:
        @block.vector
        def _(dve):
            last.dve(dve)

        @block.scalar
        def _(act):
            last.act(act)

        @block.sync
        def _(sp):
            for c in range(KC):
                sp.wait_ge(K.s("normed").sem, K.s("normed").at(c + 1))
                sp.dma_start(dram["out"][:, c, :], K.A[:, c, :]).then_inc(K.s("stored").sem, 16)
            sp.wait_ge(K.s("stored").sem, 16 * KC)



def columns(w):
    k, m = w.shape
    return w.reshape(k // P, P, m // (2 * P), 2, P).transpose(2, 1, 3, 0, 4).reshape(-1, P, 16, P)


def pairs(wa, wb):
    k, m = wa.shape
    both = np.stack([w.reshape(k // P, P, m // P, P) for w in (wa, wb)])
    return both.transpose(3, 2, 0, 1, 4).reshape(-1, P, 16, P)


def rows(w):
    k, m = w.shape
    return w.reshape(k // (2 * P), 2, P, KC, P).transpose(0, 2, 1, 3, 4).reshape(-1, P, 16, P)


def halves(w):
    return w.reshape(4, P, 2, 4, P).transpose(2, 1, 3, 0, 4).reshape(-1, P, 16, P)


NSA_ORDER = np.concatenate([np.arange(HD * h, HD * h + HD) for c in range(4) for h in (c, c + 4)])
ORDER_2 = np.concatenate([np.arange(0, 2048), 2048 + NSA_ORDER, 2560 + NSA_ORDER, np.arange(3072, 3328),
                          np.arange(3328, 3456), np.arange(3584, 3712), np.arange(3456, 3584), np.arange(3712, 3840)])
ROWS_OUT_2 = np.concatenate([np.arange(0, 512), 512 + NSA_ORDER])


def rope_table(position, half):
    f, t = np.arange(P), np.arange(T)
    inv = 10000.0 ** (-(f % half).astype(np.float64) / half)
    angle = position(f[:, None], t[None, :]) * inv[:, None]
    return np.stack([np.cos(angle), np.sin(angle)], axis=1).astype(np.float32)


def tables():
    t = np.arange(T)
    decay = np.zeros((P, HEADS, T))
    p, x = np.arange(P)[:, None], t[None, :]
    for h in range(HEADS):
        decay[:, h, :] = np.where(x >= p, (1.0 - 2.0 ** (-5.0 - h)) ** np.maximum(x - p, 0).astype(np.float64), 0.0)
    masks = np.zeros((P, 384), np.float32)
    end = np.arange(N_CMP) * CMP_STRIDE + CMP_BLOCK - 1
    for i in range(NT):
        ok = end[None, :] <= (P * i + np.arange(P))[:, None]
        masks[:, 32 * i:32 * i + N_CMP] = np.where(ok, 0.0, NEG)
        masks[:, 128 + 32 * i:128 + 32 * i + N_CMP] = ok
    masks[:, 256:384] = np.where(np.arange(P)[None, :] <= np.arange(P)[:, None], 0.0, NEG)
    return {
        "rope_2": rope_table(lambda f, t: t + 0 * f, HD // 2),
        "rope_3": rope_table(lambda f, t: np.where(f < HD, 0, np.where(f // 16 % 2 == 0, t // GRID_W, t % GRID_W)), 8),
        "decay": decay.astype(np.float32), "masks_2": masks,
    }


def na_table(rpb):
    q, j, c = np.arange(P)[:, None, None], np.arange(1, 15)[None, :, None], np.arange(GRID_W)[None, None, :]
    row, col = q // GRID_W, q % GRID_W
    start = np.clip(col - NA_WIN_COLS // 2, 0, GRID_W - NA_WIN_COLS)
    inside = (c >= start) & (c < start + NA_WIN_COLS)
    taken = rpb[:, np.broadcast_to(j - row, (P, 14, GRID_W)), np.clip(c - col + NA_WIN_COLS - 1, 0, 30) + 0 * j]
    return np.where(inside[None], taken, np.float32(NEG)).transpose(1, 0, 2, 3).reshape(P, 14, T)


def per_feature(v):
    return v.reshape(-1, P).T


def feature_major(x):
    return x.T.reshape(-1, P, x.shape[0]).transpose(1, 0, 2)


def matrices():
    m = np.zeros((len(MATRICES), P, P), np.float32)
    i, j = np.meshgrid(np.arange(P), np.arange(P), indexing="ij")
    same = i // CHUNK == j // CHUNK
    m[MAT["ident"]] = i == j
    m[MAT["mean"]] = 1.0 / D
    m[MAT["ones"]] = 1.0
    m[MAT["mean128"]] = 1.0 / P
    m[MAT["mean256"]] = 1.0 / 256
    m[MAT["mean64"]] = (i // HD == j // HD) / HD
    m[MAT["chunk_tri"]] = same & (i <= j)
    m[MAT["chunk_strict"]] = same & (i < j)
    m[MAT["chunk_ones"]] = same
    for s in (1, 2, 4, 8, 16, 32):
        m[MAT[f"level{s}"]] = (i // (2 * s) == j // (2 * s)) & (i // s % 2 == 0) & (j // s % 2 == 1)
    for name, half, off, group in (("rope64", 32, 0, 64), ("rope32", 8, 0, 16)):
        r = np.zeros((P, P), np.float32)
        for o in range(P):
            w = o % group
            if w < half:
                r[o + half, o] = -1.0
            else:
                r[o - half, o] = 1.0
        m[MAT[name]] = r
    return m.transpose(1, 0, 2)


def kernel(**inputs):
    import concourse.bacc as bacc
    from concourse.bass_utils import run_bass_kernel_spmd as run

    w = {k: np.asarray(v)[0] if k != "mem" else np.asarray(v) for k, v in inputs.items()}
    win = w["w_in"]
    in_3 = w["w_in_3"]
    in_3 = np.concatenate([in_3[:, :1920]] + 4 * [in_3[:, 1920:1952]] + [in_3[:, 1952:]], axis=1)
    tiles = [
        pairs(w["ffn1_wg"], w["ffn1_wu"]), rows(w["ffn1_wd"]),
        pairs(win[:, 4112:5136], win[:, 5136:6160]), columns(win[:, 0:3072]), columns(win[:, 3072:4096]),
        columns(win[:, 6160:8208]), columns(w["w_conv_out"]), columns(w["w_gdn_out"]), columns(w["w_mix_out"]),
        columns(w["w_xkv"]), columns(w["w_xq"]), columns(w["w_xo"]),
        pairs(w["ffn2_wg"], w["ffn2_wu"]), rows(w["ffn2_wd"]),
        columns(w["w_in_2"][:, :3840][:, ORDER_2]), columns(w["w_out_2"][ROWS_OUT_2]),
        columns(in_3), halves(w["w_branch_na_3"]), halves(w["w_branch_mla_3"]), columns(w["w_out_3"]),
        pairs(w["w_ffn_in_3"][:, :DFF], w["w_ffn_in_3"][:, DFF:]), rows(w["w_ffn_out_3"]),
    ]
    stream = np.concatenate(tiles)
    parts = {}
    for n in ("ln1", "ln2", "ln3", "ln4"):
        parts[n + "_g"], parts[n + "_b"] = per_feature(w[n + "_g"]), per_feature(w[n + "_b"])
    parts["gdn_conv"] = w["gdn_conv_qkv"].reshape(4, 24, P).transpose(2, 1, 0).reshape(P, 96)
    parts["gdn_norm"] = per_feature(w["gdn_norm_g"])
    parts["conv_w"] = w["conv_dw_w"].reshape(31, 8, P).transpose(2, 0, 1).reshape(P, 248)
    for n, source in (("conv_b", "conv_dw_b"), ("conv_ln_g", "conv_ln_g"), ("conv_ln_b", "conv_ln_b"),
                      ("b_conv_out", "b_conv_out")):
        parts[n] = per_feature(w[source])
    for n, source in (("a_log", "gdn_a_log"), ("dt_bias", "gdn_dt_bias"), ("b_gate_2", "b_gate_2")):
        parts[n] = np.broadcast_to(w[source], (P, w[source].size))
    parts["eps"] = np.broadcast_to(np.array([LN_EPS, RMS_EPS, 1.0, 64 * RMS_EPS], np.float32), (P, 4))
    small = np.concatenate([
        win[:, 4096:4112].reshape(KC, P, 16).transpose(1, 0, 2).reshape(P, 128),
        w["w_in_2"][:, 3840:3864].reshape(KC, P, 24).transpose(1, 0, 2).reshape(P, 192)], axis=1)
    parts["norm_2"] = per_feature(w["norm_w_2"])
    parts["ret_norm"] = per_feature(w["ret_norm_w_2"])
    for n, source in (("q_norm_2", "q_norm_w_2"), ("k_cmp", "k_norm_cmp_2"), ("k_slc", "k_norm_slc_2"), ("k_win", "k_norm_win_2")):
        parts[n] = per_feature(np.tile(w[source], 2))
    parts["pos_k"], parts["pos_v"] = np.tile(w["cmp_pos_k_2"].T, (2, 1)), np.tile(w["cmp_pos_v_2"].T, (2, 1))
    parts["b_gate_3"] = per_feature(w["b_gate_3"])
    parts["mla_q"], parts["mla_kv"] = per_feature(w["mla_q_norm_3"]), per_feature(w["mla_kv_norm_3"])
    for n in ("ln1_g_3", "ln1_b_3", "ln2_g_3", "ln2_b_3"):
        parts[n] = per_feature(w[n])
    vecs = np.concatenate([parts[n] for n, k in VECTORS], axis=1)
    uq = w["mla_w_uq_3"]
    ukv = w["mla_w_ukv_3"].reshape(P, HEADS, 2, HD).transpose(0, 2, 1, 3).reshape(P, 1024)
    mla_w = np.concatenate([uq.reshape(2, P, 768).transpose(1, 0, 2).reshape(P, 1536), ukv], axis=1).reshape(P, 5, T)
    more = tables()
    for n in ("k", "v"):
        more["w1_" + n] = np.tile(w[f"cmp_w1_{n}_2"].reshape(CMP_BLOCK, HD, CMP_HIDDEN).transpose(1, 0, 2), (2, 1, 1))
    more["w2"] = np.concatenate([w[f"cmp_w2_{n}_2"].reshape(2, P, HD).transpose(1, 0, 2).reshape(P, P) for n in ("k", "v")], axis=1)
    more["mla_w"], more["na_bias"] = mla_w, na_table(w["na_rpb_3"])
    arrays = {
        **more, "x_t": feature_major(w["x"]), "stream": stream, "vecs": vecs, "mats": matrices(), "small": small, "mem_t": feature_major(w["mem"][0]),
    }
    nc = bacc.Bacc("TRN2", target_bir_lowering=False, num_devices=1)
    arrays = {k: np.ascontiguousarray(v) for k, v in arrays.items()}
    dram = {k: nc.dram_tensor("in_" + k, v.shape, F32, kind="ExternalInput").ap() for k, v in arrays.items()}
    dram["out"] = nc.dram_tensor("out_t", (P, KC, T), F32, kind="ExternalOutput").ap()
    dram["keep_x"] = nc.dram_tensor("keep_x", (P, KC, T), F32, kind="Internal").ap()
    dram["keep_yc"] = nc.dram_tensor("keep_yc", (P, KC, T), F32, kind="Internal").ap()
    dram["keep_gates"] = nc.dram_tensor("keep_gates", (24, P, T), F32, kind="Internal").ap()
    program(nc, dram)
    r = run(nc, [{"in_" + k: v for k, v in arrays.items()}], core_ids=[0])
    y = np.asarray(r.results[0]["out_t"])
    return y.transpose(2, 1, 0).reshape(1, T, D)
```
